# Optimizing a Trainium2 kernel written in Bass

```python
import jax, jax.numpy as jnp
from jax import lax
import numpy as np
import math
import jax
import jax.numpy as jnp

D_MODEL = 1024
BATCH = 1
SEQ = 512
DEPTH = 1

D_MIX = D_MODEL
HEAD_DIM = 64
GDN_HEADS = (D_MIX // 2) // HEAD_DIM
GDN_WIDTH = GDN_HEADS * HEAD_DIM
CONV_K = 4
CHUNK = 64
SWA_Q_HEADS = (D_MIX // 2) // HEAD_DIM
SWA_KV_HEADS = 2
SWA_GROUP = SWA_Q_HEADS // SWA_KV_HEADS
SWA_Q_WIDTH = SWA_Q_HEADS * HEAD_DIM
SWA_KV_WIDTH = SWA_KV_HEADS * HEAD_DIM
WINDOW = 128
BLOCK = 128
ROPE_THETA = 10000.0
N_GROUPS = 4
EXPERTS_PER_GROUP = 8
N_EXPERTS = N_GROUPS * EXPERTS_PER_GROUP
TOP_K = 2
D_EXPERT = D_MODEL // 4
EPS = 1e-6
IN_WIDTHS = (GDN_WIDTH, GDN_WIDTH, GDN_WIDTH, GDN_WIDTH, GDN_HEADS, GDN_HEADS,
             SWA_Q_WIDTH, SWA_KV_WIDTH, SWA_KV_WIDTH)
IN_WIDTH = sum(IN_WIDTHS)
MIX_OUT_WIDTH = GDN_WIDTH + SWA_Q_WIDTH


def rms_norm(x, gain):
    xf = x.astype(jnp.float32)
    y = xf * lax.rsqrt(jnp.mean(xf * xf, axis=-1, keepdims=True) + EPS)
    return (y * gain.astype(jnp.float32)).astype(x.dtype)

def l2_norm(x):
    return x * lax.rsqrt(jnp.sum(x * x, axis=-1, keepdims=True) + EPS)

def modulate(x, shift, scale):
    return x * (1 + scale[:, None, :]) + shift[:, None, :]

def causal_conv_silu(x, w):
    seq = x.shape[1]
    xp = jnp.pad(x, ((0, 0), (CONV_K - 1, 0), (0, 0)))
    y = xp[:, 0:seq] * w[0]
    for j in range(1, CONV_K):
        y = y + xp[:, j:j + seq] * w[j]
    return jax.nn.silu(y)

def rope(x, positions):
    half = x.shape[-1] // 2
    inv_freq = jnp.power(jnp.float32(ROPE_THETA), -jnp.arange(half, dtype=jnp.float32) / half)
    ang = positions.astype(jnp.float32)[..., None] * inv_freq
    cos = jnp.cos(ang)[:, :, None, :]
    sin = jnp.sin(ang)[:, :, None, :]
    xf = x.astype(jnp.float32)
    x1, x2 = xf[..., :half], xf[..., half:]
    out = jnp.concatenate([x1 * cos - x2 * sin, x1 * sin + x2 * cos], axis=-1)
    return out.astype(x.dtype)

def chunked_gated_delta_rule(q, k, v, g, beta):
    bsz, seq, heads, dh = q.shape
    n_chunks = seq // CHUNK

    def to_chunks(t):
        return t.reshape(bsz, n_chunks, CHUNK, heads, -1).transpose(0, 3, 1, 2, 4)

    q, k, v = to_chunks(q), to_chunks(k), to_chunks(v)
    g = g.reshape(bsz, n_chunks, CHUNK, heads).transpose(0, 3, 1, 2)
    beta = beta.reshape(bsz, n_chunks, CHUNK, heads).transpose(0, 3, 1, 2)
    G = jnp.cumsum(g, axis=-1)

    idx = jnp.arange(CHUNK)
    lower_incl = idx[:, None] >= idx[None, :]
    strict = idx[:, None] > idx[None, :]
    diff = G[..., :, None] - G[..., None, :]
    decay = jnp.where(lower_incl, jnp.exp(jnp.where(lower_incl, diff, 0.0)), 0.0)

    kb = k * beta[..., None]
    vb = v * beta[..., None]
    m = jnp.where(strict, jnp.einsum('bhncd,bhnsd->bhncs', kb, k) * decay, 0.0)
    eye = jnp.eye(CHUNK, dtype=jnp.float32)
    a_mat = eye + m
    t_mat = lax.linalg.triangular_solve(a_mat, jnp.broadcast_to(eye, a_mat.shape),
                                        left_side=True, lower=True)
    u = jnp.einsum('bhncs,bhnse->bhnce', t_mat, vb)
    w = jnp.einsum('bhncs,bhnsd->bhncd', t_mat, kb * jnp.exp(G)[..., None])
    qg = q * jnp.exp(G)[..., None]
    attn = jnp.einsum('bhncd,bhnsd->bhncs', q, k) * decay
    g_last = G[..., -1]
    k_dec = k * jnp.exp(g_last[..., None] - G)[..., None]

    xs = tuple(jnp.moveaxis(t, 2, 0) for t in (u, w, qg, attn, k_dec, g_last))

    def step(state, inp):
        u_n, w_n, qg_n, attn_n, kdec_n, gl_n = inp
        v_new = u_n - jnp.einsum('bhcd,bhde->bhce', w_n, state)
        o_n = (jnp.einsum('bhcd,bhde->bhce', qg_n, state)
               + jnp.einsum('bhcs,bhse->bhce', attn_n, v_new))
        state = (state * jnp.exp(gl_n)[..., None, None]
                 + jnp.einsum('bhcd,bhce->bhde', kdec_n, v_new))
        return state, o_n

    s0 = jnp.zeros((bsz, heads, dh, v.shape[-1]), jnp.float32)
    _, o = lax.scan(step, s0, xs)
    return o.transpose(1, 0, 3, 2, 4).reshape(bsz, seq, heads, -1)

def gated_deltanet(q_in, k_in, v_in, z, a, b, conv_w, a_log, dt_bias, out_norm):
    bsz, seq, _ = q_in.shape
    qkv = causal_conv_silu(jnp.concatenate([q_in, k_in, v_in], axis=-1), conv_w)
    q, k, v = jnp.split(qkv.astype(jnp.float32), 3, axis=-1)
    q = l2_norm(q.reshape(bsz, seq, GDN_HEADS, HEAD_DIM)) * (HEAD_DIM ** -0.5)
    k = l2_norm(k.reshape(bsz, seq, GDN_HEADS, HEAD_DIM))
    v = v.reshape(bsz, seq, GDN_HEADS, HEAD_DIM)
    g = -jnp.exp(a_log.astype(jnp.float32)) * jax.nn.softplus(
        a.astype(jnp.float32) + dt_bias.astype(jnp.float32))
    beta = jax.nn.sigmoid(b.astype(jnp.float32))
    o = chunked_gated_delta_rule(q, k, v, g, beta)
    zf = z.astype(jnp.float32).reshape(bsz, seq, GDN_HEADS, HEAD_DIM)
    o = rms_norm(o, out_norm) * jax.nn.silu(zf)
    return o.reshape(bsz, seq, GDN_WIDTH).astype(q_in.dtype)

def sliding_window_attention(q, k, v, q_norm, k_norm, sinks, positions):
    bsz, seq, _ = q.shape
    n_blk = seq // BLOCK
    q = rope(rms_norm(q.reshape(bsz, seq, SWA_Q_HEADS, HEAD_DIM), q_norm), positions)
    k = rope(rms_norm(k.reshape(bsz, seq, SWA_KV_HEADS, HEAD_DIM), k_norm), positions)
    v = v.reshape(bsz, seq, SWA_KV_HEADS, HEAD_DIM)

    qb = q.reshape(bsz, n_blk, BLOCK, SWA_KV_HEADS, SWA_GROUP, HEAD_DIM)

    def band(t):
        tb = t.reshape(bsz, n_blk, BLOCK, SWA_KV_HEADS, HEAD_DIM)
        prev = jnp.pad(tb[:, :-1], ((0, 0), (1, 0), (0, 0), (0, 0), (0, 0)))
        return jnp.concatenate([prev, tb], axis=2)

    k_band, v_band = band(k), band(v)
    scores = jnp.einsum('bnqhgd,bnkhd->bnhgqk', qb, k_band).astype(jnp.float32) * (HEAD_DIM ** -0.5)

    qi = jnp.arange(BLOCK)[:, None]
    kj = jnp.arange(2 * BLOCK)[None, :]
    rel = qi + BLOCK - kj
    in_window = (rel >= 0) & (rel < WINDOW)
    has_prev = jnp.arange(n_blk)[:, None, None] > 0
    valid = in_window[None] & (has_prev | (kj >= BLOCK)[None])
    scores = jnp.where(valid[None, :, None, None], scores, -jnp.inf)

    sink = sinks.astype(jnp.float32).reshape(SWA_KV_HEADS, SWA_GROUP)[None, None, :, :, None]
    mx = jnp.maximum(scores.max(axis=-1), sink)
    p = jnp.exp(scores - mx[..., None])
    denom = p.sum(axis=-1) + jnp.exp(sink - mx)
    p = p / denom[..., None]
    out = jnp.einsum('bnhgqk,bnkhd->bnqhgd', p, v_band.astype(jnp.float32))
    return out.reshape(bsz, seq, SWA_Q_WIDTH).astype(q.dtype)

def hierarchical_moe(h, w_group, b_group, w_router, b_router, w_gate, w_up, w_down):
    bsz, seq, d = h.shape
    t = h.reshape(-1, d)
    group_prob = jax.nn.softmax((t @ w_group + b_group).astype(jnp.float32), axis=-1)
    p_group, g_idx = lax.top_k(group_prob, 1)
    expert_logits = (t @ w_router + b_router).astype(jnp.float32).reshape(
        -1, N_GROUPS, EXPERTS_PER_GROUP)
    g_onehot = jax.nn.one_hot(g_idx[:, 0], N_GROUPS, dtype=jnp.float32)
    in_group = jnp.einsum('tg,tge->te', g_onehot, expert_logits)
    p_exp = jax.nn.softmax(in_group, axis=-1)
    w_top, e_idx = lax.top_k(p_exp, TOP_K)
    w_top = w_top / jnp.sum(w_top, axis=-1, keepdims=True) * p_group
    expert_ids = g_idx * EXPERTS_PER_GROUP + e_idx
    combine = jnp.sum(jax.nn.one_hot(expert_ids, N_EXPERTS, dtype=jnp.float32)
                      * w_top[..., None], axis=1)
    out = jnp.zeros(t.shape, jnp.float32)
    for e in range(N_EXPERTS):
        hid = jax.nn.silu(t @ w_gate[e]) * (t @ w_up[e])
        out = out + combine[:, e:e + 1] * (hid @ w_down[e]).astype(jnp.float32)
    return out.astype(h.dtype).reshape(bsz, seq, d)

def first_inputs(seed: int = 0) -> dict:
    key = jax.random.key(seed)
    ks = jax.random.split(key, 24)
    f32 = jnp.float32
    nrm = lambda k, shape: jax.random.normal(k, shape, f32)
    dt = jnp.exp(jax.random.uniform(ks[6], (DEPTH, GDN_HEADS), f32,
                                    jnp.log(jnp.float32(1e-3)), jnp.log(jnp.float32(1e-1))))
    return {
        "x": nrm(ks[0], (BATCH, SEQ, D_MODEL)),
        "c": nrm(ks[1], (BATCH, D_MODEL)),
        "positions": jnp.broadcast_to(jnp.arange(SEQ, dtype=jnp.int32), (BATCH, SEQ)),
        "w_ada": nrm(ks[2], (DEPTH, D_MODEL, 6 * D_MODEL)) * (0.5 * D_MODEL ** -0.5),
        "b_ada": 0.01 * nrm(ks[3], (DEPTH, 6 * D_MODEL)),
        "norm_mix": 1.0 + 0.1 * nrm(ks[4], (DEPTH, D_MODEL)),
        "w_in": nrm(ks[5], (DEPTH, D_MODEL, IN_WIDTH)) * D_MODEL ** -0.5,
        "conv_w": nrm(ks[7], (DEPTH, CONV_K, 3 * GDN_WIDTH)) * CONV_K ** -0.5,
        "a_log": jnp.log(jax.random.uniform(ks[8], (DEPTH, GDN_HEADS), f32, 1.0, 16.0)),
        "dt_bias": jnp.log(jnp.expm1(dt)),
        "gdn_out_norm": 1.0 + 0.1 * nrm(ks[9], (DEPTH, HEAD_DIM)),
        "q_norm": 1.0 + 0.1 * nrm(ks[10], (DEPTH, HEAD_DIM)),
        "k_norm": 1.0 + 0.1 * nrm(ks[11], (DEPTH, HEAD_DIM)),
        "sinks": nrm(ks[12], (DEPTH, SWA_Q_HEADS)),
        "w_out": nrm(ks[13], (DEPTH, MIX_OUT_WIDTH, D_MODEL)) * MIX_OUT_WIDTH ** -0.5,
        "norm_ffn": 1.0 + 0.1 * nrm(ks[14], (DEPTH, D_MODEL)),
        "w_group": nrm(ks[15], (DEPTH, D_MODEL, N_GROUPS)) * D_MODEL ** -0.5,
        "b_group": 0.01 * nrm(ks[16], (DEPTH, N_GROUPS)),
        "w_router": nrm(ks[17], (DEPTH, D_MODEL, N_EXPERTS)) * D_MODEL ** -0.5,
        "b_router": 0.01 * nrm(ks[18], (DEPTH, N_EXPERTS)),
        "w_gate": nrm(ks[19], (DEPTH, N_EXPERTS, D_MODEL, D_EXPERT)) * D_MODEL ** -0.5,
        "w_up": nrm(ks[20], (DEPTH, N_EXPERTS, D_MODEL, D_EXPERT)) * D_MODEL ** -0.5,
        "w_down": nrm(ks[21], (DEPTH, N_EXPERTS, D_EXPERT, D_MODEL)) * D_EXPERT ** -0.5,
    }

def first_block(x, c, positions, w_ada, b_ada, norm_mix, w_in, conv_w, a_log, dt_bias,
              gdn_out_norm, q_norm, k_norm, sinks, w_out, norm_ffn, w_group, b_group,
              w_router, b_router, w_gate, w_up, w_down):
    split_points = tuple(int(s) for s in np.cumsum(IN_WIDTHS)[:-1])
    c_act = jax.nn.silu(c)
    for l in range(DEPTH):
        mod = c_act @ w_ada[l] + b_ada[l]
        shift1, scale1, gate1, shift2, scale2, gate2 = jnp.split(mod, 6, axis=-1)

        h = modulate(rms_norm(x, norm_mix[l]), shift1, scale1)
        proj = h @ w_in[l]
        (g_q, g_k, g_v, g_z, g_a, g_b, s_q, s_k, s_v) = jnp.split(proj, split_points, axis=-1)
        gdn_out = gated_deltanet(g_q, g_k, g_v, g_z, g_a, g_b, conv_w[l], a_log[l],
                                 dt_bias[l], gdn_out_norm[l])
        swa_out = sliding_window_attention(s_q, s_k, s_v, q_norm[l], k_norm[l],
                                           sinks[l], positions)
        mixed = jnp.concatenate([gdn_out, swa_out], axis=-1) @ w_out[l]
        x = x + gate1[:, None, :] * mixed

        h2 = modulate(rms_norm(x, norm_ffn[l]), shift2, scale2)
        ffn = hierarchical_moe(h2, w_group[l], b_group[l], w_router[l], b_router[l],
                               w_gate[l], w_up[l], w_down[l])
        x = x + gate2[:, None, :] * ffn
    return x


CTX_LEN = 256
GRID_W = 64

MIX_W = 2 * D_MODEL
SSD_HEADDIM = 64
SSD_W = 3 * MIX_W // 4
SSD_HEADS = SSD_W // SSD_HEADDIM
SSD_GROUPS = 4
SSD_HPG = SSD_HEADS // SSD_GROUPS
SSD_STATE = 128
SSD_CONV = 5
SSD_CHUNK = 128
CONV_CH = SSD_W + 2 * SSD_GROUPS * SSD_STATE
XBCDT_COLS = CONV_CH + 2 * SSD_HEADS
POOL_W = MIX_W - SSD_W
POOL_WINDOWS = (2, 4, 8, 16)
POOL_GROUPS = len(POOL_WINDOWS)
POOL_GW = POOL_W // POOL_GROUPS
IN_COLS = XBCDT_COLS + SSD_W + POOL_W
N_EXPERTS_2 = 32
TOP_K_2 = 4
D_FF = D_MODEL
SWIGLU_ALPHA = 1.702
SWIGLU_LIMIT = 7.0
MOE_BLOCK = 128
RMS_EPS = 1e-6


def rmsnorm(h, w):
    hf = h.astype(jnp.float32)
    hf = hf * lax.rsqrt(jnp.mean(hf * hf, axis=-1, keepdims=True) + RMS_EPS)
    return (hf * w.astype(jnp.float32)).astype(h.dtype)

def modulate_2(h, shift, scale):
    return h * (1 + scale) + shift

def dwconv_centred(u, w, b):
    ch = u.shape[-1]
    y = lax.conv_general_dilated(
        u, w[:, None, :].astype(u.dtype), window_strides=(1,),
        padding=[(SSD_CONV // 2, SSD_CONV // 2)],
        dimension_numbers=("NWC", "WIO", "NWC"), feature_group_count=ch)
    return y + b.astype(u.dtype)

def segsum(a):
    t = a.shape[-1]
    cs = jnp.cumsum(a, axis=-1)
    diff = cs[..., :, None] - cs[..., None, :]
    return jnp.where(np.tril(np.ones((t, t), dtype=bool)), diff, -jnp.inf)

def ssd_direction_inputs(xbc, dt_raw, dt_bias, a_log, d):
    dtr = dt_raw[..., d, :]
    if d == 1:
        xbc = xbc[:, ::-1]
        dtr = dtr[:, ::-1]
    b, L, _ = xbc.shape
    gn = SSD_GROUPS * SSD_STATE
    xh = xbc[..., :SSD_W].reshape(b, L, SSD_GROUPS, SSD_HPG, SSD_HEADDIM).astype(jnp.float32)
    bm = xbc[..., SSD_W:SSD_W + gn].reshape(b, L, SSD_GROUPS, SSD_STATE).astype(jnp.float32)
    cm = xbc[..., SSD_W + gn:].reshape(b, L, SSD_GROUPS, SSD_STATE).astype(jnp.float32)
    dt = jax.nn.softplus(dtr.astype(jnp.float32) + dt_bias[d].astype(jnp.float32))
    dt = dt.reshape(b, L, SSD_GROUPS, SSD_HPG)
    log_a = -jnp.exp(a_log[d].astype(jnp.float32)).reshape(SSD_GROUPS, SSD_HPG) * dt
    return xh * dt[..., None], log_a, bm, cm

def ssd_chunked(xs, log_a, bm, cm, init_state):
    b, L, G, E, P = xs.shape
    n = bm.shape[-1]
    nc = L // SSD_CHUNK
    xs = xs.reshape(b, nc, SSD_CHUNK, G, E, P)
    bm = bm.reshape(b, nc, SSD_CHUNK, G, n)
    cm = cm.reshape(b, nc, SSD_CHUNK, G, n)
    a = jnp.moveaxis(log_a.reshape(b, nc, SSD_CHUNK, G, E), 2, -1)
    a_cs = jnp.cumsum(a, axis=-1)
    lmat = jnp.exp(segsum(a))
    cb = jnp.einsum("bclgn,bcsgn->bcgls", cm, bm)
    y_diag = jnp.einsum("bcgls,bcgels,bcsgep->bclgep", cb, lmat, xs)
    decay_states = jnp.exp(a_cs[..., -1:] - a_cs)
    states = jnp.einsum("bclgn,bcgel,bclgep->bcgepn", bm, decay_states, xs)
    states = jnp.concatenate([init_state[:, None], states], axis=1)
    chunk_end = jnp.pad(a_cs[..., -1], ((0, 0), (1, 0), (0, 0), (0, 0)))
    decay_chunk = jnp.exp(segsum(jnp.moveaxis(chunk_end, 1, -1)))
    new_states = jnp.einsum("bgezy,bygepn->bzgepn", decay_chunk, states)
    prev_states, final_state = new_states[:, :-1], new_states[:, -1]
    y_off = jnp.einsum("bclgn,bcgepn,bcgel->bclgep", cm, prev_states, jnp.exp(a_cs))
    return (y_diag + y_off).reshape(b, L, G, E, P), final_state

def ssd_final_state(xbc, dt_raw, dt_bias, a_log, d):
    xs, log_a, bm, _ = ssd_direction_inputs(xbc, dt_raw, dt_bias, a_log, d)
    a_cs = jnp.cumsum(log_a, axis=1)
    w = jnp.exp(a_cs[:, -1:] - a_cs)
    return jnp.einsum("blgn,blge,blgep->bgepn", bm, w, xs)

def ssd_bidir(xbc, dt_raw, dt_bias, a_log, d_skip, init_states):
    b, L, _ = xbc.shape
    xs_f, la_f, bm_f, cm_f = ssd_direction_inputs(xbc, dt_raw, dt_bias, a_log, 0)
    y_f, fin_f = ssd_chunked(xs_f, la_f, bm_f, cm_f, init_states[0])
    xs_b, la_b, bm_b, cm_b = ssd_direction_inputs(xbc, dt_raw, dt_bias, a_log, 1)
    y_b, fin_b = ssd_chunked(xs_b, la_b, bm_b, cm_b, init_states[1])
    x_heads = xbc[..., :SSD_W].reshape(b, L, SSD_HEADS, SSD_HEADDIM).astype(jnp.float32)
    y = (y_f + y_b[:, ::-1]).reshape(b, L, SSD_W) \
        + (x_heads * d_skip.astype(jnp.float32)[:, None]).reshape(b, L, SSD_W)
    return y.astype(xbc.dtype), fin_f, fin_b

def centred_mean_minus_self(u, window):
    wl = u.shape[1]
    cs = jnp.pad(jnp.cumsum(u.astype(jnp.float32), axis=1), ((0, 0), (1, 0), (0, 0)))
    t = np.arange(wl)
    lo = np.clip(t - window // 2, 0, wl)
    hi = np.clip(t + window - window // 2, 0, wl)
    cnt = (hi - lo).astype(np.float32)
    mean = (cs[:, hi] - cs[:, lo]) / cnt[None, :, None]
    return mean.astype(u.dtype) - u

def pool_mixer(u, pool_w, pool_scale):
    n, wl, _ = u.shape
    ug = u.reshape(n, wl, POOL_GROUPS, POOL_GW)
    pooled = jnp.stack([centred_mean_minus_self(ug[:, :, g], w)
                        for g, w in enumerate(POOL_WINDOWS)], axis=2)
    y = jnp.einsum("nwgi,gio->nwgo", pooled, pool_w)
    return y.reshape(n, wl, POOL_W) * pool_scale

def mixer_out(y_ssd, z, y_pool, ssd_norm_w, w_out):
    y_ssd = rmsnorm(y_ssd * jax.nn.silu(z), ssd_norm_w)
    return jnp.concatenate([y_ssd, y_pool], axis=-1) @ w_out

def moe_ffn(h, router_w, router_b, w1, b1, w2, b2):
    shp = h.shape
    xt = h.reshape(-1, shp[-1])
    t = xt.shape[0]
    logits = (xt @ router_w + router_b).astype(jnp.float32)
    top_val, top_idx = lax.top_k(logits, TOP_K_2)
    gates = jax.nn.softmax(top_val, axis=-1)
    e_flat = top_idx.reshape(-1).astype(jnp.int32)
    tok_flat = jnp.repeat(jnp.arange(t, dtype=jnp.int32), TOP_K_2)
    g_flat = gates.reshape(-1)
    n_assign = t * TOP_K_2
    order = jnp.argsort(e_flat)
    e_sorted = e_flat[order]
    counts = jnp.bincount(e_flat, length=N_EXPERTS_2).astype(jnp.int32)
    padded = (counts + MOE_BLOCK - 1) // MOE_BLOCK * MOE_BLOCK
    pad_end = jnp.cumsum(padded)
    pad_start = pad_end - padded
    grp_start = jnp.cumsum(counts) - counts
    rank = jnp.arange(n_assign, dtype=jnp.int32) - grp_start[e_sorted]
    dest = pad_start[e_sorted] + rank
    n_blocks = -(-n_assign // MOE_BLOCK) + N_EXPERTS_2
    n_slots = n_blocks * MOE_BLOCK
    slot_tok = jnp.full((n_slots,), t, jnp.int32).at[dest].set(tok_flat[order])
    slot_gate = jnp.zeros((n_slots,), jnp.float32).at[dest].set(g_flat[order])
    block_start = jnp.arange(n_blocks, dtype=jnp.int32) * MOE_BLOCK
    block_exp = jnp.minimum(jnp.searchsorted(pad_end, block_start, side="right"),
                            N_EXPERTS_2 - 1).astype(jnp.int32)
    x_pad = jnp.concatenate([xt, jnp.zeros((1, shp[-1]), xt.dtype)], axis=0)

    def run_block(args):
        toks, e = args
        hb = x_pad[toks] @ w1[e] + b1[e]
        g_part = jnp.minimum(hb[..., ::2], SWIGLU_LIMIT)
        u_part = jnp.clip(hb[..., 1::2], -SWIGLU_LIMIT, SWIGLU_LIMIT)
        act = g_part * jax.nn.sigmoid(SWIGLU_ALPHA * g_part) * (u_part + 1)
        return act @ w2[e] + b2[e]

    y_slots = lax.map(run_block, (slot_tok.reshape(n_blocks, MOE_BLOCK), block_exp))
    y_slots = y_slots.reshape(n_slots, shp[-1]) * slot_gate[:, None].astype(xt.dtype)
    out = jnp.zeros((t + 1, shp[-1]), xt.dtype).at[slot_tok].add(y_slots)[:t]
    return out.reshape(shp)

def second_inputs(seed: int = 0) -> dict:
    key = jax.random.key(seed)
    ks = jax.random.split(key, 25)
    f32 = jnp.float32

    def nrm(k, shape, s):
        return jax.random.normal(k, shape, f32) * s

    dt0 = jnp.exp(jax.random.uniform(ks[10], (DEPTH, 2, SSD_HEADS), f32,
                                     math.log(1e-3), math.log(1e-1)))
    return {
        "x": nrm(ks[0], (BATCH, SEQ, D_MODEL), 1.0),
        "c": nrm(ks[1], (BATCH, D_MODEL), 1.0),
        "ctx": nrm(ks[2], (BATCH, CTX_LEN, D_MODEL), 1.0),
        "c_ctx": nrm(ks[3], (D_MODEL,), 1.0),
        "w_mod": nrm(ks[4], (DEPTH, D_MODEL, 6 * D_MODEL), 0.5 * D_MODEL ** -0.5),
        "b_mod": nrm(ks[5], (DEPTH, 6 * D_MODEL), 0.01),
        "norm1_w": 1.0 + nrm(ks[6], (DEPTH, D_MODEL), 0.02),
        "norm2_w": 1.0 + nrm(ks[7], (DEPTH, D_MODEL), 0.02),
        "w_in": nrm(ks[8], (DEPTH, D_MODEL, IN_COLS), D_MODEL ** -0.5),
        "conv_w": nrm(ks[9], (DEPTH, SSD_CONV, CONV_CH), SSD_CONV ** -0.5),
        "conv_b": nrm(ks[11], (DEPTH, CONV_CH), 0.01),
        "dt_bias": dt0 + jnp.log(-jnp.expm1(-dt0)),
        "a_log": jnp.log(jax.random.uniform(ks[12], (DEPTH, 2, SSD_HEADS), f32, 1.0, 16.0)),
        "d_skip": 1.0 + nrm(ks[13], (DEPTH, SSD_HEADS), 0.1),
        "ssd_norm_w": 1.0 + nrm(ks[14], (DEPTH, SSD_W), 0.02),
        "pool_w": nrm(ks[15], (DEPTH, POOL_GROUPS, POOL_GW, POOL_GW), POOL_GW ** -0.5),
        "pool_scale": 1.0 + nrm(ks[16], (DEPTH, POOL_W), 0.1),
        "w_out": nrm(ks[17], (DEPTH, MIX_W, D_MODEL), MIX_W ** -0.5),
        "router_w": nrm(ks[18], (DEPTH, D_MODEL, N_EXPERTS_2), D_MODEL ** -0.5),
        "router_b": nrm(ks[19], (DEPTH, N_EXPERTS_2), 0.01),
        "w1": nrm(ks[20], (DEPTH, N_EXPERTS_2, D_MODEL, 2 * D_FF), D_MODEL ** -0.5),
        "b1": nrm(ks[21], (DEPTH, N_EXPERTS_2, 2 * D_FF), 0.01),
        "w2": nrm(ks[22], (DEPTH, N_EXPERTS_2, D_FF, D_MODEL), D_FF ** -0.5),
        "b2": nrm(ks[23], (DEPTH, N_EXPERTS_2, D_MODEL), 0.01),
        "final_norm_w": 1.0 + nrm(ks[24], (D_MODEL,), 0.02),
    }

def second_block(x, c, ctx, c_ctx, w_mod, b_mod, norm1_w, norm2_w, w_in, conv_w, conv_b,
              dt_bias, a_log, d_skip, ssd_norm_w, pool_w, pool_scale, w_out,
              router_w, router_b, w1, b1, w2, b2, final_norm_w):
    b, L, _ = x.shape
    rows = L // GRID_W
    zero_state = jnp.zeros((b, SSD_GROUPS, SSD_HPG, SSD_HEADDIM, SSD_STATE), jnp.float32)
    for l in range(DEPTH):
        last = l == DEPTH - 1
        mod = (jax.nn.silu(c) @ w_mod[l] + b_mod[l])[:, None, :]
        mod_c = jax.nn.silu(c_ctx) @ w_mod[l] + b_mod[l]
        sh1, sc1, g1, sh2, sc2, g2 = jnp.split(mod, 6, axis=-1)
        csh1, csc1, cg1, csh2, csc2, cg2 = jnp.split(mod_c, 6, axis=-1)

        hc = modulate_2(rmsnorm(ctx, norm1_w[l]), csh1, csc1)
        pc = hc @ w_in[l][:, :(XBCDT_COLS if last else IN_COLS)]
        xbc_c = jax.nn.silu(dwconv_centred(pc[..., :CONV_CH], conv_w[l], conv_b[l]))
        dt_c = pc[..., CONV_CH:XBCDT_COLS].reshape(b, -1, 2, SSD_HEADS)
        if last:
            init_states = (ssd_final_state(xbc_c, dt_c, dt_bias[l], a_log[l], 0),
                           ssd_final_state(xbc_c, dt_c, dt_bias[l], a_log[l], 1))
            ctx_next = ctx
        else:
            y_c, fin_cf, fin_cb = ssd_bidir(xbc_c, dt_c, dt_bias[l], a_log[l], d_skip[l],
                                            (zero_state, zero_state))
            init_states = (fin_cf, fin_cb)
            yp_c = pool_mixer(pc[..., XBCDT_COLS + SSD_W:], pool_w[l], pool_scale[l])
            ctx_next = ctx + cg1 * mixer_out(y_c, pc[..., XBCDT_COLS:XBCDT_COLS + SSD_W],
                                             yp_c, ssd_norm_w[l], w_out[l])
            ctx_next = ctx_next + cg2 * moe_ffn(
                modulate_2(rmsnorm(ctx_next, norm2_w[l]), csh2, csc2),
                router_w[l], router_b[l], w1[l], b1[l], w2[l], b2[l])

        hx = modulate_2(rmsnorm(x, norm1_w[l]), sh1, sc1)
        p = hx @ w_in[l]
        xbc = jax.nn.silu(dwconv_centred(p[..., :CONV_CH], conv_w[l], conv_b[l]))
        dt_x = p[..., CONV_CH:XBCDT_COLS].reshape(b, L, 2, SSD_HEADS)
        y_x, _, _ = ssd_bidir(xbc, dt_x, dt_bias[l], a_log[l], d_skip[l], init_states)
        u_pool = p[..., XBCDT_COLS + SSD_W:].reshape(b * rows, GRID_W, POOL_W)
        y_pool = pool_mixer(u_pool, pool_w[l], pool_scale[l]).reshape(b, L, POOL_W)
        x = x + g1 * mixer_out(y_x, p[..., XBCDT_COLS:XBCDT_COLS + SSD_W], y_pool,
                               ssd_norm_w[l], w_out[l])
        x = x + g2 * moe_ffn(modulate_2(rmsnorm(x, norm2_w[l]), sh2, sc2),
                             router_w[l], router_b[l], w1[l], b1[l], w2[l], b2[l])
        ctx = ctx_next
    return rmsnorm(x, final_norm_w)


def setup_inputs(seed=0):
    out = dict(first_inputs(seed))
    for name, value in second_inputs(seed + 1).items():
        if name != "x":
            out[name + "_2"] = value
    return out


def reference(
    x, c, positions, w_ada, b_ada, norm_mix, w_in, conv_w, a_log, dt_bias, gdn_out_norm, q_norm,
    k_norm, sinks, w_out, norm_ffn, w_group, b_group, w_router, b_router, w_gate, w_up, w_down,
    c_2, ctx_2, c_ctx_2, w_mod_2, b_mod_2, norm1_w_2, norm2_w_2, w_in_2, conv_w_2, conv_b_2,
    dt_bias_2, a_log_2, d_skip_2, ssd_norm_w_2, pool_w_2, pool_scale_2, w_out_2, router_w_2,
    router_b_2, w1_2, b1_2, w2_2, b2_2, final_norm_w_2,
):
    x = first_block(
        x, c, positions, w_ada, b_ada, norm_mix, w_in, conv_w, a_log, dt_bias, gdn_out_norm,
        q_norm, k_norm, sinks, w_out, norm_ffn, w_group, b_group, w_router, b_router, w_gate,
        w_up, w_down,
    )
    return second_block(
        x, c_2, ctx_2, c_ctx_2, w_mod_2, b_mod_2, norm1_w_2, norm2_w_2, w_in_2, conv_w_2,
        conv_b_2, dt_bias_2, a_log_2, d_skip_2, ssd_norm_w_2, pool_w_2, pool_scale_2, w_out_2,
        router_w_2, router_b_2, w1_2, b1_2, w2_2, b2_2, final_norm_w_2,
    )


_drawn_inputs = setup_inputs


def setup_inputs(seed=0):
    import zlib

    import numpy as np

    out = dict(_drawn_inputs(seed))
    spreads = {}
    factors = {'b_ada': 3.31,
     'q_norm': 4.955,
     'k_norm': 5.755,
     'sinks': 64.0,
     'b_group': 8.0,
     'b_router': 7.848,
     'ctx_2': 6.586,
     'c_ctx_2': 5.926,
     'b_mod_2': 3.155,
     'norm1_w_2': 4.957,
     'norm2_w_2': 10.822,
     'conv_b_2': 25.744,
     'd_skip_2': 200.0,
     'ssd_norm_w_2': 17.064,
     'pool_scale_2': 3.242,
     'router_b_2': 16.623,
     'b1_2': 25.157,
     'b2_2': 64.0,
     'final_norm_w_2': 23.489}
    for name, (base, spread) in spreads.items():
        noise = np.random.default_rng([zlib.crc32(name.encode()), seed]).standard_normal(out[name].shape)
        drawn = base * np.exp(spread * noise) if base else spread * noise
        out[name] = jnp.asarray(drawn.astype(out[name].dtype))
    for name, factor in factors.items():
        out[name] = (out[name] * factor).astype(out[name].dtype)
    return out
```

```python
from contextlib import ExitStack

import numpy as np
import concourse.bass as bass
from concourse import mybir

F32 = mybir.dt.float32
I32 = mybir.dt.int32
ACT = mybir.ActivationFunctionType
ALU = mybir.AluOpType
AX = mybir.AxisListType

P = 128
D = 1024
T = 512
CTX = 256
KT = D // P
NT = T // P
NC_ = CTX // P
EPS = 1e-6
HD = 64
WIN = 128
GH = 8
GW = GH * HD
SH = 8
SKV = 2
SSD_W = 1536
SSD_H = 24
SSD_G = 4
HPG = SSD_H // SSD_G
ST = 128
XT = SSD_W // P
CONV_T = (SSD_W + 2 * SSD_G * ST) // P
DT_C = 2 * SSD_H
POOL_G = 4
WINDOWS = (2, 4, 8, 16)
GRID = 64
MIXT = 2 * D // P
E = 32
FF1 = 256
FF2 = 1024
TOP1 = 2
TOP2 = 4
LIMIT = 7.0
ALPHA = 1.702
BIG = 1e30
MAXB = TOP2 * T // P + E - 1 + 1
RING = 4
PIECE = KT * 512
LEVELS = 7
TWO_PI = 2.0 * np.pi


def columns(parts):
    at, out = 0, {}
    for name, width in parts:
        out[name] = (at, width)
        at += width
    return out, at


CONST, CONST_W = columns(
    [("ident", P), ("ones", P), ("le", P), ("lt", P), ("ge", P), ("gt", P), ("halves", P),
     ("rot", P), ("block", P), ("swa", 4 * P), ("level", LEVELS * P), ("pool", POOL_G * P),
     ("rev", E), ("rev4", 4), ("slot", 64), ("freq", 1), ("eps", 1), ("eps64", 1), ("thresh", 4), ("one", 1)])
VEC, VEC_W = columns(
    [("c", KT), ("c2", KT), ("cc2", KT), ("b_ada", 48), ("b_mod", 48), ("g_mix", KT),
     ("g_ffn", KT), ("g1_2", KT), ("g2_2", KT), ("g_fin", KT), ("conv", 12 * 4),
     ("conv2", CONV_T * 5), ("convb2", CONV_T), ("qn", 1), ("kn", 1), ("skip", XT),
     ("pscale", POOL_G), ("g_ssd", XT)])
ROW, ROW_W = columns(
    [("a_log", GH), ("dt_bias", GH), ("g_out", HD), ("sinks", SH), ("b_rt", 4 + E),
     ("a_log2", DT_C), ("dt_bias2", DT_C), ("b_rt2", E)])


def shape_constants():
    c = np.zeros((P, CONST_W), np.float32)

    def put(name, a):
        at, w = CONST[name]
        c[:, at:at + w] = a

    r, l = np.arange(P)[:, None], np.arange(P)[None, :]
    put("ident", r == l)
    put("ones", 1.0)
    put("le", r <= l)
    put("lt", r < l)
    put("ge", r >= l)
    put("gt", r > l)
    put("halves", r // HD == l // HD)
    put("block", r // HD == l // HD)
    rot = np.zeros((P, P), np.float32)
    for h in range(2):
        for d in range(32):
            rot[h * HD + d + 32, h * HD + d] = -1.0
            rot[h * HD + d, h * HD + d + 32] = 1.0
    put("rot", rot)
    kj = np.arange(2 * WIN)[None, :]
    rel = r + WIN - kj
    inside = (rel >= 0) & (rel < WIN)
    first = inside & (kj >= WIN)
    put("swa", np.concatenate([np.where(first, 0.0, -BIG), np.where(inside, 0.0, -BIG)], 1))
    lev = []
    for b in range(LEVELS):
        s = 1 << b
        lev.append((r // (2 * s) == l // (2 * s)) & (r // s < l // s))
    put("level", np.concatenate(lev, 1))
    pools = []
    for w in WINDOWS:
        m = np.zeros((P, P), np.float32)
        for row in range(P // GRID):
            for t in range(GRID):
                lo, hi = max(t - w // 2, 0), min(t + w - w // 2, GRID)
                m[row * GRID + lo:row * GRID + hi, row * GRID + t] = np.float32(1.0) / np.float32(hi - lo)
                m[row * GRID + t, row * GRID + t] -= 1.0
        pools.append(m)
    put("pool", np.concatenate(pools, 1))
    put("rev", np.float32(E) - np.arange(E)[None, :])
    put("rev4", np.float32(4) - np.arange(4)[None, :])
    put("slot", np.arange(64, dtype=np.float32)[None, :])
    half = HD // 2
    freq = np.power(np.float32(10000.0), -np.arange(half, dtype=np.float32) / np.float32(half)).astype(np.float32)
    put("freq", freq[(np.arange(P) % half)][:, None])
    put("eps", EPS)
    put("thresh", np.float32(P) * np.arange(4)[None, :])
    put("one", 1.0)
    return c


class Core:

    def __init__(self, nc, ctx, a):
        self.nc, self.ctx, self.a = nc, ctx, a
        self.cst = self.sb("cst", [P, CONST_W])
        self.vec = self.sb("vec", [P, VEC_W])
        self.row = self.sb("row", [P, ROW_W])
        self.xT = self.sb("xT", [P, KT, T])
        self.hT = self.sb("hT", [P, KT, T])
        self.ring = self.sb("ring", [P, RING, PIECE])
        self.mod1 = self.sb("mod1", [P, 48])
        self.mod2 = self.sb("mod2", [P, 48, 2])
        self.gain = self.sb("gain", [P, 5, KT])
        self.ps = [ctx.enter_context(nc.psum_tensor(f"bank{i}", [P, 512], F32)) for i in range(8)]
        self.loaded = [nc.alloc_semaphore(f"piece_loaded{i}") for i in range(RING)]
        self.used = nc.alloc_semaphore("piece_used")
        self.inputs = nc.alloc_semaphore("inputs_loaded")
        self.phase_sems = []
        self.pieces = []
        self.sent = 0

    def sb(self, name, shape, dt=F32):
        return self.ctx.enter_context(self.nc.sbuf_tensor(name, shape, dt))

    def sem(self, name):
        self.phase_sems.append(self.nc.alloc_semaphore(name))
        return self.phase_sems[-1]

    def end(self):
        self.nc.clear_and_free_semaphores(self.phase_sems)
        self.nc.all_engine_barrier()
        self.phase_sems = []

    def c(self, name, lo=0, hi=None):
        at, w = CONST[name]
        return self.cst[:, at + lo:at + (w if hi is None else hi)]

    def v(self, name, lo=0, hi=None):
        at, w = VEC[name]
        return self.vec[:, at + lo:at + (w if hi is None else hi)]

    def r(self, name, lo=0, hi=None):
        at, w = ROW[name]
        return self.row[:, at + lo:at + (w if hi is None else hi)]

    def send_pieces(self, sp, upto):
        while self.sent < min(upto, len(self.pieces)):
            i = self.sent
            if i >= RING:
                sp.wait_ge(self.used, i - RING + 1)
            src = self.pieces[i]
            w = src.shape[-1]
            dst = self.ring[:, i % RING, 0:KT * w].rearrange("p (k n) -> p k n", k=KT)
            sp.dma_start(dst, src).then_inc(self.loaded[i % RING], 16)
            self.sent += 1

    def piece(self, pe, i):
        pe.wait_ge(self.loaded[i % RING], 16 * (i // RING + 1))
        w = self.pieces[i].shape[-1]
        return self.ring[:, i % RING, 0:KT * w].rearrange("p (k n) -> p k n", k=KT)


    def piece_done(self):
        one = self.c("one")
        self.nc.tensor.matmul(self.ps[7][0:1, 0:1], one, one, start=True, stop=True).then_inc(self.used, 1)


def bc(ap, n):
    return ap.unsqueeze(2).to_broadcast([ap.shape[0], ap.shape[1], n])


def bm(ap, n):
    return ap.unsqueeze(1).to_broadcast([ap.shape[0], n, ap.shape[1]])


def g4(ap, n=4):
    return ap.rearrange("p (h n) -> p h n", h=n)


def modulation_phase(k):
    nc = k.nc
    NP = 12
    with ExitStack() as mem:
        sb = lambda n, s: mem.enter_context(nc.sbuf_tensor(n, s, F32))
        act1 = sb("m_act1", [P, KT])
        act2 = sb("m_act2", [P, KT, 2])
        row1 = sb("m_row1", [1, 6 * D])
        row2 = sb("m_row2", [2, 6 * D])
        c_ready, row_sb, col_mm = (k.sem(f"m_{n}") for n in ("c_ready", "row_sb", "col_mm"))
        with nc.Block() as block:
            @block.sync
            def _(sp):
                sp.dma_start(k.vec[:], k.a["vec"]).then_inc(k.inputs, 16)
                sp.dma_start(k.cst[:], k.a["cst"]).then_inc(k.inputs, 16)
                sp.dma_start(k.row[:], k.a["row"].to_broadcast([P, ROW_W])).then_inc(k.inputs, 16)
                k.send_pieces(sp, RING)
                sp.dma_start(k.xT[:], k.a["xT"]).then_inc(k.inputs, 16)
                k.send_pieces(sp, 2 * NP + RING)
                sp.wait_ge(k.inputs, 64)

            @block.tensor
            def _(pe):
                pe.wait_ge(k.inputs, 64)
                pe.wait_ge(c_ready, 3)
                for j in range(2 * NP):
                    w = k.piece(pe, j)
                    if j >= 2:
                        pe.wait_ge(row_sb, j - 1)
                    m = 1 if j < NP else 2
                    for kk in range(KT):
                        lhs = act1[:, kk:kk + 1] if m == 1 else act2[:, kk, :]
                        last = nc.tensor.matmul(k.ps[j % 2][0:m, :], lhs, w[:, kk, :], start=kk == 0, stop=kk == KT - 1)
                    last.then_inc(k.used, 1)
                for b, (rows, m) in enumerate(((row1, 1), (row2, 2))):
                    pe.wait_ge(row_sb, NP * (b + 1))
                    for i in range(48):
                        last = nc.tensor.matmul(k.ps[2 + b][:, m * i:m * i + m], rows[0:m, i * P:(i + 1) * P],
                                                k.c("ident", 0, m)[0:m, :], start=True, stop=True)
                    last.then_inc(col_mm, 1)

            @block.scalar
            def _(act):
                act.wait_ge(k.inputs, 64)
                act.activation(act1[:], k.v("c"), ACT.Silu).then_inc(c_ready, 1)
                act.activation(act2[:, :, 0], k.v("c2"), ACT.Silu).then_inc(c_ready, 1)
                act.activation(act2[:, :, 1], k.v("cc2"), ACT.Silu).then_inc(c_ready, 1)
                for j in range(2 * NP):
                    act.wait_ge(k.used, j + 1)
                    m, rows = (1, row1) if j < NP else (2, row2)
                    n = j % NP
                    act.activation(rows[0:m, n * 512:(n + 1) * 512], k.ps[j % 2][0:m, :], ACT.Copy).then_inc(row_sb, 1)

            @block.vector
            def _(dve):
                dve.wait_ge(k.inputs, 64)
                dve.wait_ge(col_mm, 1)
                dve.tensor_tensor(k.mod1[:], k.ps[2][:, 0:48], k.v("b_ada"), ALU.add)
                dve.wait_ge(col_mm, 2)
                dve.tensor_tensor(k.mod2[:], k.ps[3][:, 0:96].rearrange("p (i m) -> p i m", m=2),
                                  bc(k.v("b_mod"), 2), ALU.add)
                dve.drain()
                for n, (scale, g) in enumerate((
                        (k.mod1[:, 8:16], "g_mix"), (k.mod1[:, 32:40], "g_ffn"),
                        (k.mod2[:, 8:16, 0], "g1_2"), (k.mod2[:, 32:40, 0], "g2_2"),
                        (k.mod2[:, 8:16, 1], "g1_2"))):
                    dve.scalar_tensor_tensor(k.gain[:, n, :], scale, 1.0, k.v(g), ALU.add, ALU.mult)
    k.end()


def norm_phase(k, name, src, dst, n, gain, shift, load=None, store=None):
    nc = k.nc
    ss = k.ps[0][:, 0:n]
    with ExitStack() as mem:
        r = mem.enter_context(nc.sbuf_tensor(f"{name}_r", [P, n], F32))
        s_sq, s_ss, s_rt, s_sc, s_st, s_ld = (k.sem(f"{name}_{x}") for x in ("squares", "sum", "root", "scaled", "stored", "src"))
        with nc.Block() as block:
            @block.sync
            def _(sp):
                if load is not None:
                    sp.dma_start(src[:], load).then_inc(s_ld, 16)
                if store is not None:
                    for kk in range(KT):
                        sp.wait_ge(s_sc, kk + 1)
                        sp.dma_start(store[kk * P:(kk + 1) * P, :], dst[:, kk, 0:n]).then_inc(s_st, 16)
                    sp.wait_ge(s_st, 16 * KT)

            @block.scalar
            def _(act):
                if load is not None:
                    act.wait_ge(s_ld, 16)
                for kk in range(KT):
                    act.activation(dst[:, kk, 0:n], src[:, kk, 0:n], ACT.Square).then_inc(s_sq, 1)
                act.wait_ge(s_ss, 1)
                act.activation(r[:], ss, ACT.Sqrt, scale=1.0 / D, bias=k.c("eps")).then_inc(s_rt, 1)
                if shift is not None:
                    for kk in range(KT):
                        act.wait_ge(s_sc, kk + 1)
                        act.activation(dst[:, kk, 0:n], dst[:, kk, 0:n], ACT.Identity, bias=shift(kk))

            @block.tensor
            def _(pe):
                for kk in range(KT):
                    pe.wait_ge(s_sq, kk + 1)
                    last = nc.tensor.matmul(ss, k.c("ones"), dst[:, kk, 0:n], start=kk == 0, stop=kk == KT - 1)
                last.then_inc(s_ss, 1)

            @block.vector
            def _(dve):
                dve.wait_ge(s_rt, 1)
                dve.reciprocal(r[:], r[:])
                dve.drain()
                for kk in range(KT):
                    dve.scalar_tensor_tensor(dst[:, kk, 0:n], src[:, kk, 0:n], gain(kk), r[:], ALU.mult, ALU.mult).then_inc(s_sc, 1)
    k.end()


def project1_phase(k, t, first):
    nc = k.nc
    units = [("conv", m) for m in range(12)] + [("z", i) for i in range(NT)] + \
            [("sq", m) for m in range(4)] + [("sk", g) for g in range(SKV)] + [("vab", i) for i in range(NT)]
    piece_of = {"z": first + 3, "sq": first + 4, "sk": first + 5, "vab": first + 5}
    last_use = {11: True, 15: True, 19: True, 25: True, 3: True, 7: True}
    NB = 4
    with ExitStack() as mem:
        cv = mem.enter_context(nc.sbuf_tensor("p1_cv", [P, 2, T], F32))
        s_mm, s_act, s_cv, s_silu = (k.sem(f"p1_{n}") for n in ("mm", "act_free", "conv", "silu"))
        with nc.Block() as block:
            @block.sync
            def _(sp):
                k.send_pieces(sp, first + 8)

            @block.tensor
            def _(pe):
                for u, (kind, m) in enumerate(units):
                    if u >= NB:
                        old = u - NB
                        if units[old][0] == "conv":
                            pe.wait_ge(s_cv, old + 1)
                        else:
                            pe.wait_ge(s_act, old - 12 + 1)
                    w = k.piece(pe, first + m // 4 if kind == "conv" else piece_of[kind])
                    o = k.ps[u % NB]
                    for kk in range(KT):
                        f = dict(start=kk == 0, stop=kk == KT - 1)
                        if kind in ("conv", "sq"):
                            c0 = (m % 4) * P
                            last = nc.tensor.matmul(o[:, :], w[:, kk, c0:c0 + P], k.hT[:, kk, :], **f)
                        elif kind == "sk":
                            nc.tensor.matmul(o[0:HD, :], w[:, kk, m * HD:(m + 1) * HD], k.hT[:, kk, :], **f)
                            last = nc.tensor.matmul(o[HD:P, :], w[:, kk, m * HD:(m + 1) * HD], k.hT[:, kk, :], **f)
                        elif kind == "z":
                            last = nc.tensor.matmul(o[:, :], k.hT[:, kk, m * P:(m + 1) * P], w[:, kk, :], **f)
                        else:
                            last = nc.tensor.matmul(o[:, 0:144], k.hT[:, kk, m * P:(m + 1) * P], w[:, kk, P:P + 144], **f)
                    last.then_inc(s_mm, 1)
                    if u in last_use:
                        k.piece_done()

            @block.vector
            def _(dve):
                dve.memset(t["swk"][:, :, 0:WIN], 0.0)
                dve.memset(t["swv"][:, 0, :], 0.0)
                for m in range(12):
                    dve.wait_ge(s_mm, m + 1)
                    if m >= 2:
                        dve.wait_ge(s_silu, m - 1)
                    y, x = cv[:, m % 2, :], k.ps[m % NB]
                    w = lambda j: k.v("conv", 4 * m + j, 4 * m + j + 1)
                    dve.tensor_scalar(y, x[:, :], w(3), None, ALU.mult)
                    for j in (2, 1, 0):
                        dve.drain()
                        s = 3 - j
                        last = dve.scalar_tensor_tensor(y[:, s:T], x[:, 0:T - s], w(j), y[:, s:T], ALU.mult, ALU.add)
                    last.then_inc(s_cv, 1)

            @block.scalar
            def _(act):
                for m in range(12):
                    act.wait_ge(s_cv, m + 1)
                    act.activation(t["qkv"][:, m, :], cv[:, m % 2, :], ACT.Silu).then_inc(s_silu, 1)
                for u in range(12, len(units)):
                    kind, m = units[u]
                    act.wait_ge(s_mm, u + 1)
                    o = k.ps[u % NB]
                    if kind == "z":
                        last = act.activation(t["z"][:, m, :], o[:, :], ACT.Silu)
                    elif kind == "sq":
                        last = act.activation(t["swq"][:, m, :], o[:, :], ACT.Copy)
                    elif kind == "sk":
                        last = act.activation(t["swk"][:, m, WIN:WIN + T], o[:, :], ACT.Copy)
                    else:
                        act.activation(t["swv"][:, 1 + m, :], o[:, 0:P], ACT.Copy)
                        last = act.activation(t["ab"][:, m, :], o[:, P:P + 16], ACT.Copy)
                    last.then_inc(s_act, 1)
    k.end()


def head_norm_phase(k, t):
    nc = k.nc
    tiles = [(t["qkv"][:, m, :], "l2q" if m < 4 else "l2k") for m in range(8)] + \
            [(t["swq"][:, m, :], "q") for m in range(4)] + [(t["swk"][:, g, WIN:WIN + T], "k") for g in range(SKV)]
    with ExitStack() as mem:
        sb = lambda n, s, d=F32: mem.enter_context(nc.sbuf_tensor(n, s, d))
        sq, rt, cos, sin, ang = sb("h_sq", [P, 2, T]), sb("h_rt", [P, 2, T]), sb("h_cos", [P, T]), sb("h_sin", [P, T]), sb("h_ang", [P, T])
        pos, turn, t1 = sb("h_pos", [P, T], I32), sb("h_turn", [P, T]), sb("h_t1", [P, T])
        s_pos, s_sq, s_ss, s_rt, s_nm, s_rot, s_ang, s_trig, s_fin, s_rin = (
            k.sem(f"h_{n}") for n in ("pos", "sq", "ss", "root", "normed", "rotated", "angle", "trig", "free", "root_in"))
        with nc.Block() as block:
            @block.sync
            def _(sp):
                sp.dma_start(pos[:], k.a["pos"].to_broadcast([P, T])).then_inc(s_pos, 16)

            @block.scalar
            def _(act):
                act.wait_ge(s_ang, 1)
                act.activation(sin[:], sin[:], ACT.Sin).then_inc(s_trig, 1)
                act.wait_ge(s_ang, 2)
                act.activation(cos[:], cos[:], ACT.Sin).then_inc(s_trig, 1)
                act.activation(sq[:, 0, :], tiles[0][0], ACT.Square).then_inc(s_sq, 1)
                for m, (x, kind) in enumerate(tiles):
                    if m + 1 < len(tiles):
                        if m >= 1:
                            act.wait_ge(s_ss, m)
                        act.activation(sq[:, (m + 1) % 2, :], tiles[m + 1][0], ACT.Square).then_inc(s_sq, 1)
                    act.wait_ge(s_ss, m + 1)
                    if m >= 2:
                        act.wait_ge(s_nm, m - 1)
                    act.activation(rt[:, m % 2, :], k.ps[m % 2][:, :], ACT.Sqrt,
                                   scale=1.0 if kind[0] == "l" else 1.0 / HD, bias=k.c("eps")).then_inc(s_rt, 1)

            @block.tensor
            def _(pe):
                for m, (x, kind) in enumerate(tiles):
                    pe.wait_ge(s_sq, m + 1)
                    if m >= 2:
                        pe.wait_ge(s_rt, m - 1)
                    nc.tensor.matmul(k.ps[m % 2][:, :], k.c("halves"), sq[:, m % 2, :], start=True, stop=True).then_inc(s_ss, 1)
                for m in range(8, len(tiles)):
                    pe.wait_ge(s_nm, m + 1)
                    if m >= 10:
                        pe.wait_ge(s_fin, m - 9)
                    nc.tensor.matmul(k.ps[2 + m % 2][:, :], k.c("rot"), tiles[m][0], start=True, stop=True).then_inc(s_rot, 1)

            @block.vector
            def _(dve):
                magic = 1.5 * 2.0 ** 23
                c1 = 6.28125
                c2 = float(np.float32(np.float32((TWO_PI - c1) * 2 ** 20).astype(np.int64) / 2.0 ** 20))
                c3 = float(np.float32(TWO_PI - c1 - c2))
                dve.wait_ge(s_pos, 16)
                dve.tensor_copy(turn[:], pos[:])
                dve.drain()
                dve.tensor_scalar(ang[:], turn[:], k.c("freq"), None, ALU.mult)
                dve.drain()
                for out, quarter in ((sin, 0.0), (cos, 0.25)):
                    dve.tensor_scalar(turn[:], ang[:], 1.0 / TWO_PI, quarter, ALU.mult, ALU.add)
                    dve.drain()
                    dve.tensor_scalar(turn[:], turn[:], magic, None, ALU.add)
                    dve.drain()
                    dve.tensor_scalar(turn[:], turn[:], -magic, None, ALU.add)
                    dve.drain()
                    dve.scalar_tensor_tensor(t1[:], turn[:], -c1, ang[:], ALU.mult, ALU.add)
                    dve.drain()
                    dve.scalar_tensor_tensor(t1[:], turn[:], -c2, t1[:], ALU.mult, ALU.add)
                    dve.drain()
                    dve.scalar_tensor_tensor(t1[:], turn[:], -c3, t1[:], ALU.mult, ALU.add)
                    dve.drain()
                    dve.tensor_scalar(t1[:], t1[:], quarter * TWO_PI, 3.1415925, ALU.add, ALU.min)
                    dve.drain()
                    dve.tensor_scalar(out[:], t1[:], -3.1415925, None, ALU.max).then_inc(s_ang, 1)
                for m, (x, kind) in enumerate(tiles):
                    dve.wait_ge(s_rt, m + 1)
                    r = rt[:, m % 2, :]
                    dve.reciprocal(r, r)
                    dve.drain()
                    g = {"l2q": HD ** -0.5, "l2k": 1.0, "q": k.v("qn"), "k": k.v("kn")}[kind]
                    dve.scalar_tensor_tensor(x, x, g, r, ALU.mult, ALU.mult).then_inc(s_nm, 1)
                dve.wait_ge(s_trig, 2)
                for m in range(8, len(tiles)):
                    x = tiles[m][0]
                    dve.wait_ge(s_rot, m - 7)
                    dve.tensor_tensor(t1[:], k.ps[2 + m % 2][:, :], sin[:], ALU.mult)
                    dve.tensor_tensor(x, x, cos[:], ALU.mult)
                    dve.drain()
                    dve.tensor_tensor(x, x, t1[:], ALU.add).then_inc(s_fin, 1)
                    dve.drain()
    k.end()


def gdn_prepare_phase(k, t):
    nc = k.nc
    NG = 2 * NT
    with ExitStack() as mem:
        sb = lambda n, s: mem.enter_context(nc.sbuf_tensor(n, s, F32))
        tmp, tmp2 = sb("g_tmp", [P, NT, GH]), sb("g_tmp2", [P, NT, GH])
        gu, em, A, Ab, Tm, Z = (sb(f"g_{n}", [P, 2, 4, P]) for n in ("gu", "em", "A", "Ab", "T", "Z"))
        names = ("tok_mm", "tok_sb", "ga", "gb", "small", "cum", "gu", "raw", "exp", "A", "ab", "zmm", "zsb", "tmm", "tsb", "gate", "e1", "e2", "raw_free", "gfin")
        s = {n: k.sem(f"g_{n}") for n in names}
        with nc.Block() as block:
            @block.scalar
            def _(act):
                for n in range(2 * NT):
                    act.wait_ge(s["tok_mm"], n + 1)
                    kv, c = divmod(n, NT)
                    act.activation(t["kvt"][:, kv, c, :], k.ps[n % 2][:, :], ACT.Copy).then_inc(s["tok_sb"], 1)
                act.wait_ge(s["ga"], 1)
                act.activation(tmp[:], tmp[:], ACT.Exp).then_inc(s["e1"], 1)
                act.activation(t["aexp"][:], k.r("a_log"), ACT.Exp).then_inc(s["e1"], 1)
                act.wait_ge(s["e1"], 2)
                act.activation(tmp[:], tmp[:], ACT.Ln, bias=k.c("one")).then_inc(s["e2"], 1)
                act.activation(t["beta"][:], t["ab"][:, :, GH:2 * GH], ACT.Sigmoid).then_inc(s["e2"], 1)
                act.wait_ge(s["cum"], 1)
                act.activation(t["dec"][:].rearrange("p a c h -> p (a c h)"), k.ps[2][:, 0:3 * NT * GH], ACT.Exp).then_inc(s["small"], 1)
                for pair in range(NG // 2):
                    for w in range(2):
                        q = 2 * pair + w
                        act.wait_ge(s["raw"], q + 1)
                        act.activation(em[:, w].rearrange("p h n -> p (h n)"), k.ps[3 * w][:, :], ACT.Exp).then_inc(s["exp"], 1)
                    for l in range(LEVELS):
                        for w in range(2):
                            n = (pair * LEVELS + l) * 2 + w
                            act.wait_ge(s["zmm"], n + 1)
                            act.activation(Z[:, w].rearrange("p h n -> p (h n)"), k.ps[3 * w][:, :], ACT.Copy).then_inc(s["zsb"], 1)

            @block.vector
            def _(dve):
                g = t["g"]
                dve.tensor_tensor(g[:], t["ab"][:, :, 0:GH], bm(k.r("dt_bias"), NT), ALU.add)
                dve.drain()
                dve.tensor_scalar(tmp2[:], g[:], -1.0, None, ALU.mult)
                dve.drain()
                dve.tensor_tensor(tmp[:], g[:], tmp2[:], ALU.min).then_inc(s["ga"], 1)
                dve.wait_ge(s["e2"], 2)
                dve.scalar_tensor_tensor(g[:], g[:], 0.0, tmp[:], ALU.max, ALU.add)
                dve.drain()
                dve.tensor_tensor(g[:], g[:], bm(t["aexp"][:], NT), ALU.mult)
                dve.drain()
                dve.tensor_scalar(g[:], g[:], -1.0, None, ALU.mult).then_inc(s["gate"], 1)
                dve.drain()
                for pair in range(NG // 2):
                    for w in range(2):
                        q = 2 * pair + w
                        c, hg = divmod(q, 2)
                        for h in range(4):
                            last = dve.tensor_scalar(gu[:, w, h, :], k.c("le"), g[:, c, 4 * hg + h:4 * hg + h + 1], None, ALU.mult)
                        last.then_inc(s["gu"], 1)
                    for w in range(2):
                        q = 2 * pair + w
                        c, hg = divmod(q, 2)
                        dve.wait_ge(s["exp"], q + 1)
                        e = em[:, w]
                        dve.tensor_tensor(e, e, bm(k.c("le"), 4), ALU.mult)
                        dve.drain()
                        for par in range(2):
                            raw = g4(k.ps[3 * w + 1 + par][:, :])
                            dve.tensor_tensor(t["att"][:, 4 * q + par:4 * q + 4:2, :], e[:, par::2, :], raw[:, 2:4, :], ALU.mult)
                            dve.tensor_tensor(A[:, w, par::2, :], e[:, par::2, :], raw[:, 0:2, :], ALU.mult)
                        dve.drain()
                        dve.tensor_tensor(A[:, w], A[:, w], bm(k.c("lt"), 4), ALU.mult)
                        dve.drain()
                        dve.tensor_tensor(A[:, w], A[:, w], bc(t["beta"][:, c, 4 * hg:4 * hg + 4], P), ALU.mult)
                        dve.tensor_copy(Tm[:, w], bm(k.c("ident"), 4))
                        dve.tensor_copy(t["S"][:, 4 * q:4 * q + 4, :], bm(k.c("ident"), 4)).then_inc(s["A"], 1)
                        dve.drain()
                    for l in range(LEVELS):
                        for w in range(2):
                            q = 2 * pair + w
                            n = (pair * LEVELS + l) * 2 + w
                            S = t["S"][:, 4 * q:4 * q + 4, :]
                            dve.wait_ge(s["tmm"], n + 1)
                            if l < LEVELS - 1:
                                dve.tensor_tensor(Tm[:, w], Tm[:, w], g4(k.ps[3 * w + 1][:, :]), ALU.subtract)
                            dve.tensor_tensor(S, S, g4(k.ps[3 * w + 2][:, :]), ALU.subtract).then_inc(s["tsb"], 1)
                            dve.drain()

            @block.gpsimd
            def _(pool):
                for pair in range(NG // 2):
                    for w in range(2):
                        pool.wait_ge(s["A"], 2 * pair + w + 1)
                    for l in range(LEVELS):
                        for w in range(2):
                            n = (pair * LEVELS + l) * 2 + w
                            if n >= 2:
                                pool.wait_ge(s["zmm"], n - 1)
                            pool.tensor_tensor(Ab[:, w], A[:, w], bm(k.c("level", l * P, (l + 1) * P), 4), ALU.mult).then_inc(s["ab"], 1)

            @block.tensor
            def _(pe):
                for n in range(2 * NT):
                    kv, c = divmod(n, NT)
                    if n >= 2:
                        pe.wait_ge(s["tok_sb"], n - 1)
                    for m in range(4):
                        last = nc.tensor.transpose(k.ps[n % 2][:, m * P:(m + 1) * P], t["qkv"][:, 4 + 4 * kv + m, c * P:(c + 1) * P], k.c("ident"))
                    last.then_inc(s["tok_mm"], 1)
                pe.wait_ge(s["gate"], 1)
                flat = t["g"][:].rearrange("p c h -> p (c h)")
                n = NT * GH
                for i, mask in enumerate(("le", "gt", "ones")):
                    last = nc.tensor.matmul(k.ps[2][:, i * n:(i + 1) * n], k.c(mask), flat, start=True, stop=True)
                last.then_inc(s["cum"], 1)
                pe.wait_ge(s["small"], 1)
                pe.wait_ge(s["tok_sb"], 2 * NT)
                for pair in range(NG // 2):
                    for w in range(2):
                        q = 2 * pair + w
                        c, hg = divmod(q, 2)
                        pe.wait_ge(s["gu"], q + 1)
                        if q >= 2:
                            pe.wait_ge(s["tsb"], (pair * LEVELS) * 2)
                        nc.tensor.matmul(k.ps[3 * w][:, :], k.c("gt"), gu[:, w].rearrange("p h n -> p (h n)"), start=True, stop=True)
                        for h in range(4):
                            m, o = (4 * hg + h) // 2, HD * (h % 2)
                            kk = t["qkv"][o:o + HD, 4 + m, c * P:(c + 1) * P]
                            bank, at = k.ps[3 * w + 1 + h % 2], (h // 2) * P
                            nc.tensor.matmul(bank[:, at:at + P], kk, kk, start=True, stop=True)
                            last = nc.tensor.matmul(bank[:, 2 * P + at:3 * P + at], kk, t["qkv"][o:o + HD, m, c * P:(c + 1) * P], start=True, stop=True)
                        last.then_inc(s["raw"], 1)
                    for l in range(LEVELS):
                        for w in range(2):
                            n = (pair * LEVELS + l) * 2 + w
                            pe.wait_ge(s["ab"], n + 1)
                            if n >= 2 and l > 0:
                                pe.wait_ge(s["tsb"], n - 1)
                            for h in range(4):
                                last = nc.tensor.matmul(k.ps[3 * w][:, h * P:(h + 1) * P], Ab[:, w, h, :], Tm[:, w, h, :], start=True, stop=True)
                            last.then_inc(s["zmm"], 1)
                        for w in range(2):
                            q = 2 * pair + w
                            n = (pair * LEVELS + l) * 2 + w
                            pe.wait_ge(s["zsb"], n + 1)
                            for h in range(4):
                                S = t["S"][:, 4 * q + h, :]
                                if l < LEVELS - 1:
                                    nc.tensor.matmul(k.ps[3 * w + 1][:, h * P:(h + 1) * P], S, Z[:, w, h, :], start=True, stop=True)
                                last = nc.tensor.matmul(k.ps[3 * w + 2][:, h * P:(h + 1) * P], Z[:, w, h, :], S, start=True, stop=True)
                            last.then_inc(s["tmm"], 1)
    k.end()


def gdn_scan_phase(k, t):
    nc = k.nc
    H8 = lambda ap: ap.rearrange("p (h e) -> p h e", h=GH)
    with ExitStack() as mem:
        sb = lambda n, s: mem.enter_context(nc.sbuf_tensor(n, s, F32))
        S = sb("s_state", [P, GW])
        r, vn, qs, kd, o, sq = (sb(f"s_{n}", [P, GW]) for n in ("r", "vn", "qs", "kd", "o", "sq"))
        st = sb("s_stat", [P, GH])
        names = ("state", "ks", "r", "vmm", "vn", "qs", "qsb", "omm", "kd", "smm", "o", "osq", "ms", "rt", "fin", "tmm", "tsb", "oread")
        s = {n: k.sem(f"s_{n}") for n in names}
        with nc.Block() as block:
            @block.gpsimd
            def _(pool):
                for c in range(NT):
                    if c >= 1:
                        pool.wait_ge(s["smm"], c)
                    pool.tensor_tensor(H8(kd[:]), H8(t["kvt"][:, 0, c, :]), bc(t["dec"][:, 1, c, :], HD), ALU.mult).then_inc(s["kd"], 1)

            @block.scalar
            def _(act):
                for c in range(NT):
                    act.wait_ge(s["fin"], c + 1)
                    act.activation(st[:], st[:], ACT.Sqrt, scale=1.0 / HD, bias=k.c("eps")).then_inc(s["rt"], 1)
                    act.wait_ge(s["tmm"], c + 1)
                    act.activation(t["mix"][:, 0:4, c * P:(c + 1) * P], g4(k.ps[5][:, :]), ACT.Copy).then_inc(s["tsb"], 1)

            @block.vector
            def _(dve):
                dve.memset(S[:], 0.0).then_inc(s["state"], 1)
                dve.drain()
                for c in range(NT):
                    eG, eT = t["dec"][:, 0, c, :], t["dec"][:, 2, c, :]
                    dve.wait_ge(s["ks"], c + 1)
                    dve.tensor_tensor(H8(r[:]), H8(k.ps[0][:, :]), bc(eG, HD), ALU.mult)
                    dve.drain()
                    dve.tensor_tensor(r[:], t["kvt"][:, 1, c, :], r[:], ALU.subtract).then_inc(s["r"], 1)
                    dve.tensor_tensor(H8(qs[:]), H8(k.ps[1][:, :]), bc(eG, HD), ALU.mult)
                    dve.wait_ge(s["vmm"], c + 1)
                    dve.tensor_tensor(H8(vn[:]), H8(k.ps[2][:, :]), bc(t["beta"][:, c, :], HD), ALU.mult).then_inc(s["vn"], 1)
                    dve.tensor_tensor(H8(S[:]), H8(S[:]), bc(eT, HD), ALU.mult)
                    dve.wait_ge(s["omm"], c + 1)
                    dve.drain()
                    dve.tensor_tensor(o[:], k.ps[3][:, :], qs[:], ALU.add)
                    dve.wait_ge(s["smm"], c + 1)
                    dve.tensor_tensor(g4(r[:]), g4(k.ps[4][:, :]), bm(k.c("block"), 4), ALU.mult)
                    dve.drain()
                    dve.tensor_tensor(S[:], S[:], r[:], ALU.add).then_inc(s["state"], 1)
                    dve.tensor_tensor(sq[:], o[:], o[:], ALU.mult)
                    dve.drain()
                    dve.tensor_reduce(st[:], H8(sq[:]), AX.X, ALU.add).then_inc(s["fin"], 1)
                    dve.wait_ge(s["rt"], c + 1)
                    dve.reciprocal(st[:], st[:])
                    dve.drain()
                    dve.tensor_tensor(H8(o[:]), H8(o[:]), bc(st[:], HD), ALU.mult)
                    dve.drain()
                    dve.tensor_tensor(H8(o[:]), H8(o[:]), bm(k.r("g_out"), GH), ALU.mult)
                    dve.drain()
                    dve.tensor_tensor(o[:], o[:], t["z"][:, c, :], ALU.mult).then_inc(s["o"], 1)
                    dve.wait_ge(s["tmm"], c + 1)

            @block.tensor
            def _(pe):
                for c in range(NT):
                    tok = slice(c * P, (c + 1) * P)
                    pe.wait_ge(s["state"], c + 1)
                    for m in range(4):
                        last = nc.tensor.matmul(k.ps[0][:, m * P:(m + 1) * P], t["qkv"][:, 4 + m, tok], S[:, m * P:(m + 1) * P], start=True, stop=True)
                        last = nc.tensor.matmul(k.ps[1][:, m * P:(m + 1) * P], t["qkv"][:, m, tok], S[:, m * P:(m + 1) * P], start=True, stop=True)
                    last.then_inc(s["ks"], 1)
                    pe.wait_ge(s["r"], c + 1)
                    for h in range(GH):
                        last = nc.tensor.matmul(k.ps[2][:, h * HD:(h + 1) * HD], t["S"][:, c * GH + h, :], r[:, h * HD:(h + 1) * HD], start=True, stop=True)
                    last.then_inc(s["vmm"], 1)
                    pe.wait_ge(s["vn"], c + 1)
                    for h in range(GH):
                        last = nc.tensor.matmul(k.ps[3][:, h * HD:(h + 1) * HD], t["att"][:, c * GH + h, :], vn[:, h * HD:(h + 1) * HD], start=True, stop=True)
                    last.then_inc(s["omm"], 1)
                    pe.wait_ge(s["kd"], c + 1)
                    for m in range(4):
                        last = nc.tensor.matmul(k.ps[4][:, m * P:(m + 1) * P], kd[:, m * P:(m + 1) * P], vn[:, m * P:(m + 1) * P], start=True, stop=True)
                    last.then_inc(s["smm"], 1)
                    pe.wait_ge(s["o"], c + 1)
                    if c >= 1:
                        pe.wait_ge(s["tsb"], c)
                    for m in range(4):
                        last = nc.tensor.transpose(k.ps[5][:, m * P:(m + 1) * P], o[:, m * P:(m + 1) * P], k.c("ident"))
                    last.then_inc(s["tmm"], 1)
    k.end()


def attention_phase(k, t):
    nc = k.nc
    units = [(n, hp) for n in range(NT) for hp in range(4)]
    with ExitStack() as mem:
        sb = lambda n, s: mem.enter_context(nc.sbuf_tensor(n, s, F32))
        sc, pT = sb("a_sc", [P, 2, 2, 2 * WIN]), sb("a_pT", [P, 2, 4, P])
        mx, nmx, den, snk = (sb(f"a_{n}", [P, 2, 2]) for n in ("mx", "nmx", "den", "snk"))
        out = sb("a_out", [P, 2, GW])
        names = ("smm", "mx", "exp", "snk", "tmm", "tsb", "pv", "out", "omm", "osb")
        s = {n: k.sem(f"a_{n}") for n in names}
        with nc.Block() as block:
            @block.tensor
            def _(pe):
                def scores(u):
                    n, hp = units[u]
                    if u >= 2:
                        pe.wait_ge(s["mx"], u - 1)
                    for i in range(2):
                        g = (2 * hp + i) // 4
                        o = HD * i
                        last = nc.tensor.matmul(k.ps[2 * (u % 2) + i][:, 0:256], t["swq"][o:o + HD, hp, n * P:(n + 1) * P],
                                                t["swk"][o:o + HD, g, n * P:n * P + 256], start=True, stop=True)
                    last.then_inc(s["smm"], 1)

                scores(0)
                for u, (n, hp) in enumerate(units):
                    if u + 1 < len(units):
                        scores(u + 1)
                    pe.wait_ge(s["exp"], u + 1)
                    if u >= 2:
                        pe.wait_ge(s["tsb"], u - 1)
                    for i in range(2):
                        for b in range(2):
                            last = nc.tensor.transpose(k.ps[4 + u % 2][:, (2 * i + b) * P:(2 * i + b + 1) * P],
                                                       sc[:, u % 2, i, b * P:(b + 1) * P], k.c("ident"))
                    last.then_inc(s["tmm"], 1)
                    pe.wait_ge(s["tsb"], u + 1)
                    if u >= 1:
                        pe.wait_ge(s["out"], u)
                    for i in range(2):
                        g = (2 * hp + i) // 4
                        for b in range(2):
                            last = nc.tensor.matmul(k.ps[6][:, i * HD:(i + 1) * HD], pT[:, u % 2, 2 * i + b, :],
                                                    t["swv"][:, n + b, g * HD:(g + 1) * HD], start=b == 0, stop=b == 1)
                    last.then_inc(s["pv"], 1)
                    if hp == 3:
                        pe.wait_ge(s["out"], u + 1)
                        if n >= 1:
                            pe.wait_ge(s["osb"], n)
                        for m in range(4):
                            last = nc.tensor.transpose(k.ps[7][:, m * P:(m + 1) * P], out[:, n % 2, m * P:(m + 1) * P], k.c("ident"))
                        last.then_inc(s["omm"], 1)

            @block.vector
            def _(dve):
                def prepare(u):
                    n, hp = units[u]
                    m0 = 0 if n == 0 else 256
                    dve.wait_ge(s["smm"], u + 1)
                    if u >= 2:
                        dve.wait_ge(s["tmm"], u - 1)
                    for i in range(2):
                        dve.scalar_tensor_tensor(sc[:, u % 2, i, :], k.ps[2 * (u % 2) + i][:, 0:256], HD ** -0.5, k.c("swa", m0, m0 + 256), ALU.mult, ALU.add)
                    dve.drain()
                    dve.tensor_reduce(mx[:, u % 2, :], sc[:, u % 2], AX.X, ALU.max)
                    dve.drain()
                    dve.tensor_tensor(mx[:, u % 2, :], mx[:, u % 2, :], k.r("sinks", 2 * hp, 2 * hp + 2), ALU.max)
                    dve.drain()
                    dve.tensor_tensor(snk[:, u % 2, :], k.r("sinks", 2 * hp, 2 * hp + 2), mx[:, u % 2, :], ALU.subtract)
                    dve.tensor_scalar(nmx[:, u % 2, :], mx[:, u % 2, :], -1.0, None, ALU.mult).then_inc(s["mx"], 1)

                prepare(0)
                for u, (n, hp) in enumerate(units):
                    if u + 1 < len(units):
                        prepare(u + 1)
                    dve.wait_ge(s["tmm"], u + 1)
                    dve.tensor_copy(pT[:, u % 2], g4(k.ps[4 + u % 2][:, :])).then_inc(s["tsb"], 1)
                    dve.wait_ge(s["snk"], u + 1)
                    dve.tensor_tensor(den[:, u % 2, :], den[:, u % 2, :], snk[:, u % 2, :], ALU.add)
                    dve.drain()
                    dve.reciprocal(den[:, u % 2, :], den[:, u % 2, :])
                    dve.drain()
                    dve.wait_ge(s["pv"], u + 1)
                    if hp == 0 and n >= 2:
                        dve.wait_ge(s["omm"], n - 1)
                    dve.tensor_tensor(out[:, n % 2, hp * P:(hp + 1) * P].rearrange("p (i e) -> p i e", i=2),
                                      k.ps[6][:, 0:P].rearrange("p (i e) -> p i e", i=2), bc(den[:, u % 2, :], HD), ALU.mult).then_inc(s["out"], 1)

            @block.scalar
            def _(act):
                for u, (n, hp) in enumerate(units):
                    act.wait_ge(s["mx"], u + 1)
                    for i in range(2):
                        last = act.activation(sc[:, u % 2, i, :], sc[:, u % 2, i, :], ACT.Exp, bias=nmx[:, u % 2, i:i + 1],
                                              accum_out=den[:, u % 2, i:i + 1])
                    last.then_inc(s["exp"], 1)
                    act.activation(snk[:, u % 2, :], snk[:, u % 2, :], ACT.Exp).then_inc(s["snk"], 1)
                    if hp == 3:
                        act.wait_ge(s["omm"], n + 1)
                        act.activation(t["mix"][:, 4:8, n * P:(n + 1) * P], g4(k.ps[7][:, :]), ACT.Copy).then_inc(s["osb"], 1)
    k.end()


def output_phase(k, name, mix, first, halves, gate, keep):
    nc = k.nc
    s_mm, s_sb = k.sem(f"{name}_mm"), k.sem(f"{name}_sb")
    with nc.Block() as block:
        @block.sync
        def _(sp):
            k.send_pieces(sp, keep)

        @block.tensor
        def _(pe):
            for n in range(2):
                for h in range(halves):
                    w = k.piece(pe, first + n * halves + h)
                    for m in range(4):
                        u = 4 * n + m
                        if u >= 4 and h == 0:
                            pe.wait_ge(s_sb, u - 3)
                        for kk in range(KT):
                            last = nc.tensor.matmul(k.ps[m][:, :], w[:, kk, m * P:(m + 1) * P], mix[:, h * KT + kk, :],
                                                    start=h == 0 and kk == 0, stop=h == halves - 1 and kk == KT - 1)
                        if h == halves - 1:
                            last.then_inc(s_mm, 1)
                    k.piece_done()

        @block.vector
        def _(dve):
            for u in range(KT):
                dve.wait_ge(s_mm, u + 1)
                dve.scalar_tensor_tensor(k.xT[:, u, :], k.ps[u % 4][:, :], gate(u), k.xT[:, u, :], ALU.mult, ALU.add).then_inc(s_sb, 1)
    k.end()


def router_phase(k, name, t, w_src, n_logits, top, b_row, hier):
    nc = k.nc
    with ExitStack() as mem:
        sb = lambda n, s, d=F32: mem.enter_context(nc.sbuf_tensor(f"{name}_{n}", s, d))
        wr = sb("wr", [P, KT, n_logits])
        htok = sb("htok", [P, NT, D])
        lg, lm, eq, key = sb("lg", [P, NT, n_logits]), sb("lm", [P, NT, E]), sb("eq", [P, NT, E]), sb("key", [P, NT, E])
        oh = sb("oh", [P, top, NT, E])
        asg, pre = sb("asg", [P, NT, E]), sb("pre", [P, NT, E])
        m, mk = sb("m", [P, top, NT]), sb("mk", [P, NT])
        gl, gm, geq, gk, pg = sb("gl", [P, NT, 4]), sb("gm", [P, NT]), sb("geq", [P, NT, 4]), sb("gk", [P, NT]), sb("pg", [P, NT])
        cnt, blk, tot, beg = sb("cnt", [P, E]), sb("blk", [P, 4, E]), sb("tot", [P, E]), sb("beg", [P, E])
        pos, sl = sb("pos", [P, NT, E]), sb("sl", [P, top, NT])
        cmp_, tabf = sb("cmp", [P, 64, E]), sb("tabf", [P, 64])
        zero = sb("zero", [P, E])
        names = ("w", "lmm", "tmm", "tsb", "row", "gexp_in", "gexp", "exp_in", "exp", "asg", "rank", "slots", "sent")
        s = {n: k.sem(f"{name}_{n}") for n in names}
        with nc.Block() as block:
            @block.sync
            def _(sp):
                sp.dma_start(wr[:], w_src).then_inc(s["w"], 16)

            @block.tensor
            def _(pe):
                pe.wait_ge(s["w"], 16)
                for i in range(NT):
                    for kk in range(KT):
                        last = nc.tensor.matmul(k.ps[0][:, i * 64:i * 64 + n_logits], k.hT[:, kk, i * P:(i + 1) * P], wr[:, kk, :],
                                                start=kk == 0, stop=kk == KT - 1)
                last.then_inc(s["lmm"], 1)
                for n in range(2 * NT):
                    i, half = divmod(n, 2)
                    if n >= 2:
                        pe.wait_ge(s["tsb"], n - 1)
                    for j in range(4):
                        last = nc.tensor.transpose(k.ps[2 + n % 2][:, j * P:(j + 1) * P], k.hT[:, 4 * half + j, i * P:(i + 1) * P], k.c("ident"))
                    last.then_inc(s["tmm"], 1)
                pe.wait_ge(s["asg"], 1)
                fl = lambda a: a[:].rearrange("p i e -> p (i e)")
                nc.tensor.matmul(k.ps[1][:, 0:NT * E], k.c("lt"), fl(asg), start=True, stop=False)
                nc.tensor.matmul(k.ps[1][:, 0:NT * E], k.c("ones"), fl(pre), start=False, stop=True)
                nc.tensor.matmul(k.ps[4][:, 0:E], k.c("ones"), pre[:, NT - 1, :], start=True, stop=False)
                nc.tensor.matmul(k.ps[4][:, 0:E], k.c("ones"), asg[:, NT - 1, :], start=False, stop=True).then_inc(s["rank"], 1)

            @block.scalar
            def _(act):
                for n in range(2 * NT):
                    i, half = divmod(n, 2)
                    act.wait_ge(s["tmm"], n + 1)
                    act.activation(htok[:, i, half * 512:(half + 1) * 512], k.ps[2 + n % 2][:, :], ACT.Copy).then_inc(s["tsb"], 1)
                if hier:
                    act.wait_ge(s["gexp_in"], 1)
                    act.activation(gl[:], gl[:], ACT.Exp).then_inc(s["gexp"], 1)
                act.wait_ge(s["exp_in"], 1)
                act.activation(m[:], m[:], ACT.Exp).then_inc(s["exp"], 1)

            @block.vector
            def _(dve):
                def run(i):
                    dve.drain()
                    return i

                def first_max(x, rev, mx, eqt, kt, keyt, n):
                    dve.tensor_reduce(mx, x, AX.X, ALU.max)
                    dve.drain()
                    dve.tensor_tensor(eqt, x, bc(mx, n), ALU.is_equal)
                    dve.drain()
                    dve.tensor_tensor(keyt, eqt, bm(rev, NT), ALU.mult)
                    dve.drain()
                    dve.tensor_reduce(kt, keyt, AX.X, ALU.max)
                    dve.drain()

                dve.memset(zero[:], 0.0)
                dve.wait_ge(s["lmm"], 1)
                lgp = k.ps[0][:, 0:256].rearrange("p (i n) -> p i n", i=NT)[:, :, 0:n_logits]
                run(dve.tensor_tensor(lg[:], lgp, bm(b_row, NT), ALU.add))
                if hier:
                    first_max(lg[:, :, 0:4], k.c("rev4"), gm[:], geq[:], gk[:], gl[:], 4)
                    dve.tensor_tensor(geq[:], gl[:], bc(gk[:], 4), ALU.is_equal)
                    dve.drain()
                    run(dve.tensor_tensor(gl[:], lg[:, :, 0:4], bc(gm[:], 4), ALU.subtract).then_inc(s["gexp_in"], 1))
                    dve.wait_ge(s["gexp"], 1)
                    run(dve.tensor_reduce(pg[:], gl[:], AX.X, ALU.add))
                    run(dve.reciprocal(pg[:], pg[:]))
                    run(dve.tensor_scalar(geq[:], geq[:], BIG, -BIG, ALU.mult, ALU.add))
                    for gi in range(4):
                        dve.tensor_tensor(lm[:, :, 8 * gi:8 * gi + 8], lg[:, :, 4 + 8 * gi:12 + 8 * gi], bc(geq[:, :, gi], 8), ALU.add)
                else:
                    dve.tensor_copy(lm[:], lg[:])
                dve.drain()
                for n in range(top):
                    first_max(lm[:], k.c("rev"), m[:, n, :], eq[:], mk[:], key[:], E)
                    run(dve.tensor_tensor(oh[:, n], key[:], bc(mk[:], E), ALU.is_equal))
                    run(dve.scalar_tensor_tensor(lm[:], oh[:, n], -3.0 * BIG, lm[:], ALU.mult, ALU.add))
                run(dve.tensor_tensor(asg[:], oh[:, 0], oh[:, 1], ALU.add))
                for n in range(2, top):
                    run(dve.tensor_tensor(asg[:], asg[:], oh[:, n], ALU.add))
                dve.memset(pre[:, 0, :], 0.0)
                dve.drain()
                for i in range(1, NT):
                    last = dve.tensor_tensor(pre[:, i, :], pre[:, i - 1, :], asg[:, i - 1, :], ALU.add)
                    if i == NT - 1:
                        last.then_inc(s["asg"], 1)
                    dve.drain()
                for n in range(top - 1, -1, -1):
                    dve.tensor_tensor(m[:, n, :], m[:, n, :], m[:, 0, :], ALU.subtract) if n else dve.memset(m[:, 0, :], 0.0)
                    dve.drain()
                dve.tensor_copy(zero[:, 0:1], zero[:, 1:2]).then_inc(s["exp_in"], 1)
                dve.wait_ge(s["exp"], 1)
                run(dve.tensor_reduce(mk[:], m[:].rearrange("p n i -> p i n"), AX.X, ALU.add))
                run(dve.reciprocal(mk[:], mk[:]))
                if hier:
                    run(dve.tensor_tensor(mk[:], mk[:], pg[:], ALU.mult))
                dve.tensor_tensor(t["wts"][:, 0:top, :], m[:], bm(mk[:], top), ALU.mult)
                dve.wait_ge(s["rank"], 1)
                run(dve.tensor_copy(cnt[:], k.ps[4][:, 0:E]))
                run(dve.tensor_tensor(blk[:], bm(cnt[:], 4), bc(k.c("thresh"), E), ALU.is_gt))
                run(dve.tensor_reduce(cnt[:], blk[:].rearrange("p j e -> p e j"), AX.X, ALU.add))
                dve.tensor_tensor_scan(tot[:], cnt[:], zero[:], 0.0, ALU.add, ALU.add)
                dve.drain()
                run(dve.tensor_tensor(beg[:], tot[:], cnt[:], ALU.subtract))
                run(dve.scalar_tensor_tensor(pos[:], bm(beg[:], NT), float(P), k.ps[1][:, 0:NT * E].rearrange("p (i e) -> p i e", i=NT), ALU.mult, ALU.add))
                for n in range(top):
                    run(dve.tensor_tensor(key[:], oh[:, n], pos[:], ALU.mult))
                    run(dve.tensor_reduce(sl[:, n, :], key[:], AX.X, ALU.add))
                dve.tensor_copy(t["slots"][:, 0:top, :], sl[:]).then_inc(s["slots"], 1)
                run(dve.tensor_tensor(cmp_[:], bm(tot[:], 64), bc(k.c("slot"), E), ALU.is_le))
                run(dve.tensor_reduce(tabf[:], cmp_[:], AX.X, ALU.add))
                run(dve.tensor_scalar(tabf[:], tabf[:], float(E - 1), None, ALU.min))
                dve.tensor_copy(t["table"][:, 0:64], tabf[:])
                dve.tensor_copy(t["table"][:, 64:65], tot[:, E - 1:E])

            @block.gpsimd
            def _(pool):
                pool.wait_ge(s["slots"], 1)
                pool.wait_ge(s["tsb"], 2 * NT)
                for n in range(top):
                    for i in range(NT):
                        pool.indirect_dma_start(out=k.a["xs"], out_offset=bass.IndirectOffsetOnAxis(ap=t["slots"][:, n, i:i + 1], axis=0),
                                                in_=htok[:, i, :], in_offset=None).then_inc(s["sent"], 16)
                pool.wait_ge(s["sent"], 16 * top * NT)
    k.end()


def expert_phase(k, name, t, up, down, bias, ff, min_blocks):
    nc = k.nc
    NJ = up.shape[0] // E
    ND = down.shape[0] // E
    FK = ff // P
    PER = FK // NJ
    with ExitStack() as mem:
        sb = lambda n, s, d=F32: mem.enter_context(nc.sbuf_tensor(f"{name}_{n}", s, d))
        extra = sb("extra", [P, 2, PIECE]) if NJ + ND > RING else None
        slot = lambda j: k.ring[:, j, :] if j < RING else extra[:, j - RING, :]
        xg, xt = sb("xg", [P, D]), sb("xt", [P, KT, P])
        hb, u1, sg = sb("hb", [P, 2, 512]), sb("u1", [P, 2, 256]), sb("sg", [P, 2, 256])
        av, at, y = sb("av", [P, ff]), sb("at", [P, FK, P]), sb("y", [P, D])
        bb = sb("bb", [P, 2 * ff + D]) if bias is not None else None
        names = ("x_in", "h_mm", "h_free", "g_min", "sig", "a_out", "xt_mm", "xt_sb", "at_mm", "at_sb", "y_mm", "y_sb", "y_out", "y_free", "b1_in", "b2_in")
        s = {n: k.sem(f"{name}_{n}") for n in names}
        w_in = [k.sem(f"{name}_w{j}_in") for j in range(NJ + ND)]
        note, sign = sb("note", [P, 2]), sb("sign", [P, 8])
        count = lambda eng: eng.value_load(t["table"][0:1, 64:65], min_val=min_blocks, max_val=MAXB - 1)
        expert = lambda eng, b: eng.value_load(t["table"][0:1, bass.ds(b, 1)], min_val=0, max_val=E - 1)
        ncp = (FK + 3) // 4
        with nc.Block() as block:
            @block.sync
            def _(sp):
                nb = count(sp)

                def load(e, j):
                    if j < NJ:
                        src = up[bass.ds(e * NJ + j, 1), :, :]
                    else:
                        src = down[bass.ds(e * ND + (j - NJ), 1), :, :]
                    w = src.shape[-1]
                    sp.dma_start(slot(j)[:, 0:w], src.rearrange("a p n -> p (a n)")).then_inc(w_in[j], 16)

                def load_bias(e, lo, hi, sem):
                    sp.dma_start(bb[:, lo:hi], bias[bass.ds(e, 1), lo:hi].to_broadcast([P, hi - lo])).then_inc(sem, 16)

                e0 = expert(sp, 0)
                for j in range(NJ + ND):
                    load(e0, j)
                    if j == 0 and bb is not None:
                        load_bias(e0, 0, 2 * ff, s["b1_in"])
                if bb is not None:
                    load_bias(e0, 2 * ff, 2 * ff + D, s["b2_in"])
                with sp.Fori(1, nb) as b:
                    e = expert(sp, b)
                    for j in range(NJ):
                        sp.wait_ge(s["h_mm"], b * NJ + (j + 1 - NJ))
                        load(e, j)
                    if bb is not None:
                        sp.wait_ge(s["h_free"], b * NJ + NJ)
                        load_bias(e, 0, 2 * ff, s["b1_in"])
                    for j in range(ND):
                        sp.wait_ge(s["y_mm"], b * 2 + (j - 1 if ND == 2 else 0))
                        load(e, NJ + j)
                    if bb is not None:
                        sp.wait_ge(s["y_sb"], b)
                        load_bias(e, 2 * ff, 2 * ff + D, s["b2_in"])

            @block.gpsimd
            def _(pool):
                nb = count(pool)
                rows = lambda ap, b: ap[bass.ds(b * P, P), :]
                pool.memset(note[:], 0.0).then_inc(s["y_free"], 1)
                pool.dma_start(xg[:], k.a["xs"][0:P, :]).then_inc(s["x_in"], 16)
                pool.wait_ge(s["xt_mm"], 2)
                pool.dma_start(xg[:], k.a["xs"][P:2 * P, :]).then_inc(s["x_in"], 16)
                with pool.Fori(0, nb) as b:
                    pool.wait_ge(s["xt_mm"], b * 2 + 4)
                    pool.dma_start(xg[:], rows(k.a["xs"], b + 2)).then_inc(s["x_in"], 16)
                    pool.wait_ge(s["y_sb"], b + 1)
                    pool.dma_start(rows(k.a["xs"], b), y[:]).then_inc(s["y_out"], 16)
                    pool.wait_ge(s["y_out"], b * 16 + 16)
                    pool.tensor_tensor(note[:, 1:2], note[:, 0:1], note[:, 0:1], ALU.add).then_inc(s["y_free"], 1)
                pool.wait_ge(s["x_in"], nb * 16 + 32)

            @block.tensor
            def _(pe):
                nb = count(pe)

                def transpose_x():
                    for half in range(2):
                        for j in range(4):
                            kk = 4 * half + j
                            last = nc.tensor.transpose(k.ps[4 + half][:, j * P:(j + 1) * P], xg[:, kk * P:(kk + 1) * P], k.c("ident"))
                        last.then_inc(s["xt_mm"], 1)

                pe.wait_ge(s["x_in"], 16)
                transpose_x()
                with pe.Fori(0, nb) as b:
                    pe.wait_ge(s["xt_sb"], b * 2 + 2)
                    for j in range(NJ):
                        pe.wait_ge(w_in[j], b * 16 + 16)
                        pe.wait_ge(s["h_free"], b * NJ + (j + 1))
                        w = slot(j).rearrange("p (k n) -> p k n", k=KT)
                        for kk in range(KT):
                            last = nc.tensor.matmul(k.ps[j][:, :], xt[:, kk, :], w[:, kk, :], start=kk == 0, stop=kk == KT - 1)
                        last.then_inc(s["h_mm"], 1)
                    pe.wait_ge(s["x_in"], b * 16 + 32)
                    pe.wait_ge(s["at_sb"], b * ncp + ncp)
                    pe.wait_ge(s["y_free"], b + 1)
                    transpose_x()
                    for j in range(NJ):
                        pe.wait_ge(s["a_out"], b * NJ + (j + 1))
                        for i in range(PER):
                            f = j * PER + i
                            last = nc.tensor.transpose(k.ps[6 + f // 4][:, (f % 4) * P:(f % 4 + 1) * P], av[:, f * P:(f + 1) * P], k.c("ident"))
                            if f % 4 == 3 or f == FK - 1:
                                last.then_inc(s["at_mm"], 1)
                    pe.wait_ge(s["at_sb"], b * ncp + 2 * ncp)
                    pe.wait_ge(s["xt_sb"], b * 2 + 4)
                    for n in range(2):
                        if n < ND:
                            pe.wait_ge(w_in[NJ + n], b * 16 + 16)
                        w = slot(NJ + min(n, ND - 1))[:, 0:FK * (512 if ND == 2 else D)].rearrange("p (k n) -> p k n", k=FK)
                        for kk in range(FK):
                            rhs = w[:, kk, :] if ND == 2 else w[:, kk, n * 512:(n + 1) * 512]
                            last = nc.tensor.matmul(k.ps[4 + n][:, :], at[:, kk, :], rhs, start=kk == 0, stop=kk == FK - 1)
                        last.then_inc(s["y_mm"], 1)

            @block.scalar
            def _(act):
                nb = count(act)

                def copy_x():
                    for half in range(2):
                        act.activation(xt[:, 4 * half:4 * half + 4, :], g4(k.ps[4 + half][:, :]), ACT.Copy).then_inc(s["xt_sb"], 1)

                for n in range(ncp):
                    act.activation(at[:, 0, n:n + 1], k.c("one"), ACT.Copy).then_inc(s["at_sb"], 1)
                act.wait_ge(s["xt_mm"], 2)
                copy_x()
                with act.Fori(0, nb) as b:
                    for j in range(NJ):
                        act.wait_ge(s["g_min"], b * NJ + (j + 1))
                        if bb is None:
                            act.activation(sg[:, j % 2, :], k.ps[j][:, 0:256], ACT.Silu).then_inc(s["sig"], 1)
                        else:
                            act.activation(sg[:, j % 2, :], hb[:, j % 2, 0:256], ACT.Sigmoid, scale=ALPHA).then_inc(s["sig"], 1)
                    act.wait_ge(s["xt_mm"], b * 2 + 4)
                    copy_x()
                    for n in range(ncp):
                        act.wait_ge(s["at_mm"], b * ncp + (n + 1))
                        w = min(4, FK - 4 * n)
                        act.activation(at[:, 4 * n:4 * n + w, :], g4(k.ps[6 + n][:, 0:w * P], w), ACT.Copy).then_inc(s["at_sb"], 1)

            @block.vector
            def _(dve):
                nb = count(dve)
                for j in range(NJ):
                    dve.memset(sign[:, j:j + 1], 0.0).then_inc(s["h_free"], 1)
                with dve.Fori(0, nb) as b:
                    if bb is not None:
                        dve.wait_ge(s["b1_in"], b * 16 + 16)
                    for j in range(NJ):
                        h, u, g = hb[:, j % 2, :], u1[:, j % 2, :], sg[:, j % 2, :]
                        a = av[:, j * 256:(j + 1) * 256]
                        dve.wait_ge(s["h_mm"], b * NJ + (j + 1))
                        if bb is None:
                            dve.tensor_copy(u, k.ps[j][:, 256:512]).then_inc(s["g_min"], 1)
                            dve.wait_ge(s["sig"], b * NJ + (j + 1))
                            dve.tensor_tensor(a, g, u, ALU.mult).then_inc(s["a_out"], 1)
                            dve.memset(sign[:, NJ:NJ + 1], 0.0).then_inc(s["h_free"], 1)
                        else:
                            dve.tensor_tensor(h, k.ps[j][:, :], bb[:, j * 512:(j + 1) * 512], ALU.add).then_inc(s["h_free"], 1)
                            dve.drain()
                            dve.tensor_scalar(h[:, 0:256], h[:, 0:256], LIMIT, None, ALU.min).then_inc(s["g_min"], 1)
                            dve.tensor_scalar(u, h[:, 256:512], LIMIT, -LIMIT, ALU.min, ALU.max)
                            dve.drain()
                            dve.scalar_tensor_tensor(u, u, 1.0, h[:, 0:256], ALU.add, ALU.mult)
                            dve.drain()
                            dve.wait_ge(s["sig"], b * NJ + (j + 1))
                            dve.tensor_tensor(a, u, g, ALU.mult).then_inc(s["a_out"], 1)
                    if bb is not None:
                        dve.wait_ge(s["b2_in"], b * 16 + 16)
                    dve.wait_ge(s["y_free"], b + 1)
                    for n in range(2):
                        dve.wait_ge(s["y_mm"], b * 2 + (n + 1))
                        o = y[:, n * 512:(n + 1) * 512]
                        if bb is None:
                            last = dve.tensor_copy(o, k.ps[4 + n][:, :])
                        else:
                            last = dve.tensor_tensor(o, k.ps[4 + n][:, :], bb[:, 2 * ff + n * 512:2 * ff + (n + 1) * 512], ALU.add)
                    last.then_inc(s["y_sb"], 1)
    k.end()


def combine_phase(k, name, t, top, gate, keep):
    nc = k.nc
    units = [(i, n) for i in range(NT) for n in range(top)]
    with ExitStack() as mem:
        sb = lambda n, s, d=F32: mem.enter_context(nc.sbuf_tensor(f"{name}_{n}", s, d))
        yb, acc = sb("yb", [P, 4, D]), sb("acc", [P, 2, D])
        got = [k.sem(f"{name}_got{i}") for i in range(4)]
        s_used, s_acc, s_mm, s_sb = (k.sem(f"{name}_{n}") for n in ("used", "acc", "mm", "sb"))
        with nc.Block() as block:
            @block.sync
            def _(sp):
                k.send_pieces(sp, keep)

            @block.gpsimd
            def _(pool):
                for u, (i, n) in enumerate(units):
                    if u >= 4:
                        pool.wait_ge(s_used, u - 3)
                    pool.indirect_dma_start(out=yb[:, u % 4, :], out_offset=None, in_=k.a["xs"],
                                            in_offset=bass.IndirectOffsetOnAxis(ap=t["slots"][:, n, i:i + 1], axis=0)).then_inc(got[u % 4], 16)

            @block.vector
            def _(dve):
                def add_x(i):
                    for half in range(2):
                        dve.wait_ge(s_mm, 2 * i + half + 1)
                        for j in range(4):
                            kk = 4 * half + j
                            x = k.xT[:, kk, i * P:(i + 1) * P]
                            last = dve.scalar_tensor_tensor(x, k.ps[2 * (i % 2) + half][:, j * P:(j + 1) * P], gate(kk), x, ALU.mult, ALU.add)
                        last.then_inc(s_sb, 1)

                for u, (i, n) in enumerate(units):
                    dve.wait_ge(got[u % 4], 16 * (u // 4 + 1))
                    w = t["wts"][:, n, i:i + 1]
                    if n == 0:
                        if i >= 2:
                            dve.wait_ge(s_mm, 2 * (i - 1))
                        dve.tensor_scalar(acc[:, i % 2, :], yb[:, u % 4, :], w, None, ALU.mult).then_inc(s_used, 1)
                    else:
                        dve.drain()
                        dve.scalar_tensor_tensor(acc[:, i % 2, :], yb[:, u % 4, :], w, acc[:, i % 2, :], ALU.mult, ALU.add).then_inc(s_used, 1)
                    if n == top - 1 and i >= 1:
                        add_x(i - 1)
                add_x(NT - 1)

            @block.tensor
            def _(pe):
                for i in range(NT):
                    pe.wait_ge(s_used, (i + 1) * top)
                    for half in range(2):
                        if i >= 2:
                            pe.wait_ge(s_sb, 2 * (i - 2) + half + 1)
                        for j in range(4):
                            kk = 4 * half + j
                            last = nc.tensor.transpose(k.ps[2 * (i % 2) + half][:, j * P:(j + 1) * P], acc[:, i % 2, kk * P:(kk + 1) * P], k.c("ident"))
                        last.then_inc(s_mm, 1)
    k.end()


def project2_phase(k, t, hc, first):
    nc = k.nc
    NX = 16
    with ExitStack() as mem:
        cv = mem.enter_context(nc.sbuf_tensor("p2_cv", [P, 2, T + CTX], F32))
        s_mm, s_cv, s_silu, s_dt = (k.sem(f"p2_{n}") for n in ("mm", "conv", "silu", "dt"))
        with nc.Block() as block:
            @block.sync
            def _(sp):
                k.send_pieces(sp, first + 6)

            @block.tensor
            def _(pe):
                for m in range(CONV_T):
                    if m >= 2:
                        pe.wait_ge(s_cv, m - 1)
                    w = k.piece(pe, first + m // 4)
                    c0 = (m % 4) * P
                    main, ctx_ = k.ps[2 * (m % 2)], k.ps[2 * (m % 2) + 1]
                    for kk in range(KT):
                        last = nc.tensor.matmul(main[:, :], w[:, kk, c0:c0 + P], k.hT[:, kk, :], start=kk == 0, stop=kk == KT - 1)
                    if m < NX:
                        for kk in range(KT):
                            last = nc.tensor.matmul(ctx_[:, 0:CTX], w[:, kk, c0:c0 + P], hc[:, kk, :], start=kk == 0, stop=kk == KT - 1)
                    last.then_inc(s_mm, 1)
                    if m % 4 == 3:
                        k.piece_done()
                w = k.piece(pe, first + 5)
                for i in range(NT + NC_):
                    h = k.hT[:, :, i * P:(i + 1) * P] if i < NT else hc[:, :, (i - NT) * P:(i - NT + 1) * P]
                    for kk in range(KT):
                        last = nc.tensor.matmul(k.ps[4][:, i * DT_C:(i + 1) * DT_C], h[:, kk, :], w[:, kk, :], start=kk == 0, stop=kk == KT - 1)
                last.then_inc(s_dt, 1)
                k.piece_done()

            @block.vector
            def _(dve):
                for m in range(CONV_T):
                    dve.wait_ge(s_mm, m + 1)
                    if m >= 2:
                        dve.wait_ge(s_silu, m - 1)
                    w = lambda j: k.v("conv2", 5 * m + j, 5 * m + j + 1)
                    parts = [(k.ps[2 * (m % 2)], 0, T)] + ([(k.ps[2 * (m % 2) + 1], T, CTX)] if m < NX else [])
                    for x, at, n in parts:
                        dve.tensor_scalar(cv[:, m % 2, at:at + n], x[:, 0:n], w(2), None, ALU.mult)
                    for j in (0, 1, 3, 4):
                        dve.drain()
                        d = j - 2
                        lo, hi = max(0, -d), max(0, d)
                        for x, at, n in parts:
                            y = cv[:, m % 2, at + lo:at + n - hi]
                            last = dve.scalar_tensor_tensor(y, x[:, lo + d:n - hi + d], w(j), y, ALU.mult, ALU.add)
                    last.then_inc(s_cv, 1)
                dve.wait_ge(s_dt, 1)
                dve.tensor_copy(t["dt"][:].rearrange("p i c -> p (i c)"), k.ps[4][:, 0:(NT + NC_) * DT_C])

            @block.scalar
            def _(act):
                for m in range(CONV_T):
                    act.wait_ge(s_cv, m + 1)
                    dst = t["mix"][:, m, :] if m < XT else t["bc"][:, m - XT, :]
                    b = k.v("convb2", m, m + 1)
                    last = act.activation(dst, cv[:, m % 2, 0:T], ACT.Silu, bias=b)
                    if m < NX:
                        last = act.activation(t["xc"][:, m, :], cv[:, m % 2, T:T + CTX], ACT.Silu, bias=b)
                    last.then_inc(s_silu, 1)
    k.end()


def ssd_prepare_phase(k, t):
    nc = k.nc
    NTT = NT + NC_
    W = NTT * DT_C
    with ExitStack() as mem:
        sb = lambda n, s, d=F32: mem.enter_context(nc.sbuf_tensor(f"q_{n}", s, d))
        tmp, tmp2, aexp = sb("tmp", [P, NTT, DT_C]), sb("tmp2", [P, NTT, DT_C]), sb("aexp", [P, DT_C])
        names = ("e_in", "e1", "e2", "a", "cum", "ecum", "coef", "tmm", "tsb", "xw", "smm", "ssb", "spill", "skip")
        s = {n: k.sem(f"q_{n}") for n in names}
        main = [("m", i, j) for i in range(NT) for j in range(4)]
        ctx_ = [("c", i, j) for i in range(NC_) for j in range(4)]
        jobs = ctx_ + main
        ring = k.ring[:].rearrange("p r n -> p (r n)")
        ctok = ring[:, 4096:8192].rearrange("p (i n) -> p i n", i=NC_)
        xw = ring[:, 8192:8192 + 4 * SSD_W].rearrange("p (n c) -> p n c", n=4)
        with nc.Block() as block:
            @block.sync
            def _(sp):
                sp.dma_start(k.a["spill_h"], k.hT[:]).then_inc(s["spill"], 16)
                sp.wait_ge(s["spill"], 16)

            @block.scalar
            def _(act):
                act.wait_ge(s["e_in"], 1)
                act.activation(tmp[:], tmp[:], ACT.Exp)
                act.activation(aexp[:], k.r("a_log2"), ACT.Exp).then_inc(s["e1"], 1)
                act.drain()
                act.activation(tmp[:], tmp[:], ACT.Ln, bias=k.c("one")).then_inc(s["e2"], 1)
                act.wait_ge(s["cum"], 1)
                for d, b in ((0, 0), (1, 1)):
                    src = k.ps[b][:, 0:W].rearrange("p (i d h) -> p i d h", i=NTT, d=2)[:, :, d, :]
                    act.activation(t["coef"][:, :, d, :], src, ACT.Exp)
                act.activation(t["etot"][:].rearrange("p i d h -> p (i d h)"), k.ps[2][:, 0:W], ACT.Exp).then_inc(s["ecum"], 1)
                for n, (kind, i, j) in enumerate(jobs):
                    act.wait_ge(s["tmm"], n + 1)
                    if kind == "c":
                        dst = ctok[:, i, j * 512:(j + 1) * 512]
                    elif j < 3:
                        dst = t["xtok"][:, i, j * 512:(j + 1) * 512]
                    else:
                        dst = t["btok"][:, i, :]
                    act.activation(dst, k.ps[3 + n % 2][:, :], ACT.Copy).then_inc(s["tsb"], 1)
                for n in range(2 * SSD_G):
                    d, g = divmod(n, SSD_G)
                    act.wait_ge(s["smm"], n + 1)
                    act.activation(t["state"][:, d, g * 384:(g + 1) * 384], k.ps[5 + n % 2][:, 0:384], ACT.Copy).then_inc(s["ssb"], 1)

            @block.vector
            def _(dve):
                dt, a = t["dt"], t["a"]
                dve.tensor_tensor(dt[:], dt[:], bm(k.r("dt_bias2"), NTT), ALU.add)
                dve.drain()
                dve.tensor_scalar(tmp2[:], dt[:], -1.0, None, ALU.mult)
                dve.drain()
                dve.tensor_tensor(tmp[:], dt[:], tmp2[:], ALU.min).then_inc(s["e_in"], 1)
                dve.wait_ge(s["e2"], 1)
                dve.scalar_tensor_tensor(dt[:], dt[:], 0.0, tmp[:], ALU.max, ALU.add)
                dve.tensor_scalar(aexp[:], aexp[:], -1.0, None, ALU.mult)
                dve.drain()
                dve.tensor_tensor(a[:], dt[:], bm(aexp[:], NTT), ALU.mult).then_inc(s["a"], 1)
                dve.wait_ge(s["ecum"], 1)
                dve.tensor_tensor(t["coef"][:].rearrange("p i d h -> p i (d h)"), t["coef"][:].rearrange("p i d h -> p i (d h)"), dt[:], ALU.mult).then_inc(s["coef"], 1)
                dve.drain()
                for n in range(2 * NC_):
                    d, i = divmod(n, NC_)
                    dve.wait_ge(s["tsb"], 4 * NC_)
                    dve.tensor_tensor(xw[:, n, :].rearrange("p (h e) -> p h e", h=SSD_H), ctok[:, i, 0:SSD_W].rearrange("p (h e) -> p h e", h=SSD_H),
                                      bc(t["coef"][:, NT + i, d, :], HD), ALU.mult).then_inc(s["xw"], 1)
                dve.wait_ge(s["tmm"], len(jobs))
                for m in range(XT):
                    dve.tensor_scalar(t["mix"][:, m, :], t["mix"][:, m, :], k.v("skip", m, m + 1), None, ALU.mult)

            @block.tensor
            def _(pe):
                pe.wait_ge(s["a"], 1)
                fl = t["a"][:].rearrange("p i c -> p (i c)")
                c0, c1 = NT * DT_C, (NT + 1) * DT_C
                nc.tensor.matmul(k.ps[0][:, 0:W], k.c("gt"), fl, start=True, stop=False)
                nc.tensor.matmul(k.ps[0][:, c0:c1], k.c("ones"), t["a"][:, NT + 1, :], start=False, stop=True)
                nc.tensor.matmul(k.ps[1][:, 0:W], k.c("lt"), fl, start=True, stop=False)
                nc.tensor.matmul(k.ps[1][:, c1:W], k.c("ones"), t["a"][:, NT, :], start=False, stop=True)
                nc.tensor.matmul(k.ps[2][:, 0:W], k.c("ones"), fl, start=True, stop=True).then_inc(s["cum"], 1)
                for n, (kind, i, j) in enumerate(jobs):
                    if n >= 2:
                        pe.wait_ge(s["tsb"], n - 1)
                    for q in range(4):
                        m = 4 * j + q
                        if kind == "c":
                            src = t["xc"][:, m, i * P:(i + 1) * P]
                        else:
                            src = (t["mix"][:, m, :] if m < XT else t["bc"][:, m - XT, :])[:, i * P:(i + 1) * P]
                        last = nc.tensor.transpose(k.ps[3 + n % 2][:, q * P:(q + 1) * P], src, k.c("ident"))
                    last.then_inc(s["tmm"], 1)
                for n in range(2 * SSD_G):
                    d, g = divmod(n, SSD_G)
                    if n >= 2:
                        pe.wait_ge(s["ssb"], n - 1)
                    pe.wait_ge(s["xw"], NC_ * (d + 1))
                    for i in range(NC_):
                        last = nc.tensor.matmul(k.ps[5 + n % 2][:, 0:384], ctok[:, i, (XT + g) * P:(XT + g + 1) * P], xw[:, d * NC_ + i, g * 384:(g + 1) * 384],
                                                start=i == 0, stop=i == NC_ - 1)
                    last.then_inc(s["smm"], 1)
    k.end()


def ssd_scan_phase(k, t):
    nc = k.nc
    TF = k.hT[:].rearrange("p k n -> p (k n)")
    TX = k.xT[:].rearrange("p k n -> p (k n)")
    R6 = lambda ap: ap.rearrange("p (h n) -> p h n", h=HPG)
    gf, gb = R6(TF[:, 0:768]), R6(TF[:, 768:1536])
    ew, dl = R6(TF[:, 1536:2304]), R6(TF[:, 2304:3072])
    eg = TF[:, 3072:3456].rearrange("p (m n) -> p m n", m=3)
    xw = TX[:, 0:SSD_W]
    cb = TX[:, 1536:1664]
    tmp = TX[:, 1664:2048].rearrange("p (m n) -> p m n", m=3)
    fwd = [("f", c, g) for c in range(NT) for g in range(SSD_G)]
    bwd = [("b", c, g) for c in reversed(range(NT)) for g in range(SSD_G)]
    units = fwd + bwd
    names = ("gm", "pmm", "e", "cb", "w", "ymm", "omm", "eg", "y", "off", "xw", "smm", "ssb", "dl")
    s = {n: k.sem(f"r_{n}") for n in names}
    with nc.Block() as block:
        @block.gpsimd
        def _(pool):
            for u, (kind, c, g) in enumerate(units):
                d = 0 if kind == "f" else 1
                if kind == "f":
                    if u >= 1:
                        pool.wait_ge(s["pmm"], u)
                    for h in range(HPG):
                        hh = g * HPG + h
                        pool.tensor_scalar(gb[:, h, :], k.c("ge"), t["a"][:, c, SSD_H + hh:SSD_H + hh + 1], None, ALU.mult)
                        last = pool.tensor_scalar(gf[:, h, :], k.c("le"), t["a"][:, c, hh:hh + 1], None, ALU.mult)
                    last.then_inc(s["gm"], 1)
                if g == 0:
                    if u >= SSD_G:
                        pool.wait_ge(s["smm"], u)
                    pool.tensor_tensor(xw.rearrange("p (h e) -> p h e", h=SSD_H), t["xtok"][:, c, :].rearrange("p (h e) -> p h e", h=SSD_H),
                                       bc(t["coef"][:, c, d, :], HD), ALU.mult).then_inc(s["xw"], 1)

        @block.tensor
        def _(pe):
            for u, (kind, c, g) in enumerate(units):
                d = 0 if kind == "f" else 1
                tok = slice(c * P, (c + 1) * P)
                B, C = t["bc"][:, g, tok], t["bc"][:, SSD_G + g, tok]
                if kind == "f":
                    pe.wait_ge(s["gm"], u + 1)
                    for half in range(2):
                        hs = slice(3 * half, 3 * half + 3)
                        if u >= 1 and half == 0:
                            pe.wait_ge(s["e"], u)
                        nc.tensor.matmul(k.ps[half][:, 0:384], k.c("gt"), gf[:, hs, :].rearrange("p h n -> p (h n)"), start=True, stop=False)
                        last = nc.tensor.matmul(k.ps[half][:, 0:384], k.c("lt"), gb[:, hs, :].rearrange("p h n -> p (h n)"), start=False, stop=True)
                    if u >= 1:
                        pe.wait_ge(s["cb"], u)
                    last = nc.tensor.matmul(k.ps[2][:, 0:P], B, C, start=True, stop=True)
                    last.then_inc(s["pmm"], 1)
                if u >= 1:
                    pe.wait_ge(s["eg"], u)
                    pe.wait_ge(s["off"], u)
                if u >= SSD_G:
                    pe.wait_ge(s["ssb"], u - SSD_G + 1)
                for m in range(3):
                    h0 = g * HPG + 2 * m
                    for half in range(2):
                        lhs = t["a"][:, c, d * SSD_H + h0 + half:d * SSD_H + h0 + half + 1].to_broadcast([P, HD])
                        nc.tensor.matmul(k.ps[4][half * HD:(half + 1) * HD, m * P:(m + 1) * P], lhs, k.c("le" if d == 0 else "ge"), start=True, stop=True)
                    last = nc.tensor.matmul(k.ps[5][:, m * P:(m + 1) * P], t["state"][:, d, g * 384 + m * P:g * 384 + (m + 1) * P], C, start=True, stop=True)
                last.then_inc(s["omm"], 1)
                if kind == "f":
                    pe.wait_ge(s["w"], u + 1)
                    if u >= 1:
                        pe.wait_ge(s["y"], u)
                    for m in range(3):
                        for half in range(2):
                            h = 2 * m + half
                            last = nc.tensor.matmul(k.ps[3][half * HD:(half + 1) * HD, m * P:(m + 1) * P], t["xtok"][:, c, (g * HPG + h) * HD:(g * HPG + h + 1) * HD],
                                                    ew[:, h, :], start=True, stop=True)
                    last.then_inc(s["ymm"], 1)
                pe.wait_ge(s["xw"], u // SSD_G + 1)
                if u >= 1:
                    pe.wait_ge(s["ssb"], u)
                nc.tensor.matmul(k.ps[6][:, 0:384], t["btok"][:, c, g * P:(g + 1) * P], xw[:, g * 384:(g + 1) * 384], start=True, stop=True).then_inc(s["smm"], 1)

        @block.scalar
        def _(act):
            for u, (kind, c, g) in enumerate(units):
                if kind == "f":
                    act.wait_ge(s["gm"], u + 1)
                    if u >= 1:
                        act.wait_ge(s["w"], u)
                    for h in range(HPG):
                        hh = g * HPG + h
                        last = act.activation(dl[:, h, :], k.c("ge"), ACT.Copy, scale=t["dt"][:, c, SSD_H + hh:SSD_H + hh + 1])
                    last.then_inc(s["dl"], 1)
                    act.wait_ge(s["pmm"], u + 1)
                    if u >= 1:
                        act.wait_ge(s["ymm"], u)
                    for half in range(2):
                        last = act.activation(ew[:, 3 * half:3 * half + 3, :], k.ps[half][:, 0:384].rearrange("p (h n) -> p h n", h=3), ACT.Exp)
                    last.then_inc(s["e"], 1)
                    act.activation(cb, k.ps[2][:, 0:P], ACT.Copy).then_inc(s["cb"], 1)
                act.wait_ge(s["omm"], u + 1)
                if u >= 1:
                    act.wait_ge(s["off"], u)
                act.activation(eg, k.ps[4][:, 0:384].rearrange("p (m n) -> p m n", m=3), ACT.Exp).then_inc(s["eg"], 1)

        @block.vector
        def _(dve):
            for u, (kind, c, g) in enumerate(units):
                d = 0 if kind == "f" else 1
                tok = slice(c * P, (c + 1) * P)
                y = t["mix"][:, 3 * g:3 * g + 3, tok]
                S = t["state"][:, d, g * 384:(g + 1) * 384]
                if kind == "f":
                    dve.wait_ge(s["dl"], u + 1)
                    for h in range(HPG):
                        hh = g * HPG + h
                        dve.scalar_tensor_tensor(dl[:, h, :], k.c("le"), t["dt"][:, c, hh:hh + 1], dl[:, h, :], ALU.mult, ALU.add)
                    dve.wait_ge(s["cb"], u + 1)
                    dve.drain()
                    dve.tensor_tensor(dl, dl, bm(cb, HPG), ALU.mult)
                    dve.drain()
                    dve.tensor_tensor(ew, ew, dl, ALU.mult).then_inc(s["w"], 1)
                dve.wait_ge(s["eg"], u + 1)
                dve.tensor_tensor(tmp, k.ps[5][:, 0:384].rearrange("p (m n) -> p m n", m=3), eg, ALU.mult).then_inc(s["off"], 1)
                dve.drain()
                dve.tensor_tensor(y, y, tmp, ALU.add)
                if kind == "f":
                    dve.wait_ge(s["ymm"], u + 1)
                    dve.drain()
                    dve.tensor_tensor(y, y, k.ps[3][:, 0:384].rearrange("p (m n) -> p m n", m=3), ALU.add).then_inc(s["y"], 1)
                S6 = S.rearrange("p (h e) -> p h e", h=HPG)
                dve.tensor_tensor(S6, S6, bc(t["etot"][:, c, d, g * HPG:(g + 1) * HPG], HD), ALU.mult)
                dve.wait_ge(s["smm"], u + 1)
                dve.drain()
                dve.tensor_tensor(S, S, k.ps[6][:, 0:384], ALU.add).then_inc(s["ssb"], 1)
    k.end()


def gate2_phase(k, t, first):
    nc = k.nc
    with ExitStack() as mem:
        sb = lambda n, s, d=F32: mem.enter_context(nc.sbuf_tensor(f"z_{n}", s, d))
        zs, sq, r = sb("zs", [P, 2, T]), sb("sq", [P, 2, T]), sb("r", [P, T])
        ut, pw = sb("ut", [P, NT, T]), sb("pw", [P, POOL_G, P])
        pl = sb("pl", [P, 2, T])
        names = ("h", "pw", "mm", "silu", "y", "sq", "ss", "rt", "umm", "usb", "pmm", "psb", "omm", "osb")
        s = {n: k.sem(f"z_{n}") for n in names}
        with nc.Block() as block:
            @block.sync
            def _(sp):
                sp.dma_start(k.hT[:], k.a["spill_h"]).then_inc(s["h"], 16)
                k.send_pieces(sp, first + 1)
                sp.dma_start(k.xT[:], k.a["spill_x"]).then_inc(s["h"], 16)
                sp.dma_start(pw[:], k.a["pool_w"]).then_inc(s["pw"], 16)
                k.send_pieces(sp, first + 4 + RING)

            @block.tensor
            def _(pe):
                pe.wait_ge(s["h"], 32)
                for m in range(XT):
                    w = k.piece(pe, first + m // 4)
                    if m >= 2:
                        pe.wait_ge(s["silu"], m - 1)
                    for kk in range(KT):
                        last = nc.tensor.matmul(k.ps[m % 2][:, :], w[:, kk, (m % 4) * P:(m % 4 + 1) * P], k.hT[:, kk, :], start=kk == 0, stop=kk == KT - 1)
                    last.then_inc(s["mm"], 1)
                    if m % 4 == 3:
                        k.piece_done()
                    if m >= 1:
                        pe.wait_ge(s["sq"], m)
                        nc.tensor.matmul(k.ps[2][:, :], k.c("ones"), sq[:, (m - 1) % 2, :], start=m == 1, stop=False).then_inc(s["ss"], 1)
                w = k.piece(pe, first + 3)
                for i in range(NT):
                    if i >= 2:
                        pe.wait_ge(s["usb"], i - 1)
                    for kk in range(KT):
                        last = nc.tensor.matmul(k.ps[3 + i % 2][:, :], k.hT[:, kk, i * P:(i + 1) * P], w[:, kk, :], start=kk == 0, stop=kk == KT - 1)
                    last.then_inc(s["umm"], 1)
                    if i == 0:
                        pe.wait_ge(s["sq"], XT)
                        nc.tensor.matmul(k.ps[2][:, :], k.c("ones"), sq[:, (XT - 1) % 2, :], start=False, stop=True).then_inc(s["ss"], 1)
                k.piece_done()
                pe.wait_ge(s["pw"], 16)
                for g in range(POOL_G):
                    pe.wait_ge(s["usb"], NT)
                    if g >= 2:
                        pe.wait_ge(s["psb"], g - 1)
                    for i in range(NT):
                        last = nc.tensor.matmul(k.ps[5 + g % 2][:, i * P:(i + 1) * P], ut[:, i, g * P:(g + 1) * P], k.c("pool", g * P, (g + 1) * P), start=True, stop=True)
                    last.then_inc(s["pmm"], 1)
                    pe.wait_ge(s["psb"], g + 1)
                    if g >= 2:
                        pe.wait_ge(s["osb"], g - 1)
                    nc.tensor.matmul(k.ps[g % 2][:, :], pw[:, g, :], pl[:, g % 2, :], start=True, stop=True).then_inc(s["omm"], 1)

            @block.scalar
            def _(act):
                for m in range(XT):
                    act.wait_ge(s["mm"], m + 1)
                    if m >= 2:
                        act.wait_ge(s["y"], m - 1)
                    act.activation(zs[:, m % 2, :], k.ps[m % 2][:, :], ACT.Silu).then_inc(s["silu"], 1)
                    if m >= 1:
                        act.wait_ge(s["y"], m)
                        if m >= 3:
                            act.wait_ge(s["ss"], m - 2)
                        act.activation(sq[:, (m - 1) % 2, :], t["mix"][:, m - 1, :], ACT.Square).then_inc(s["sq"], 1)
                act.wait_ge(s["y"], XT)
                act.wait_ge(s["ss"], XT - 2)
                act.activation(sq[:, (XT - 1) % 2, :], t["mix"][:, XT - 1, :], ACT.Square).then_inc(s["sq"], 1)
                act.wait_ge(s["ss"], XT)
                act.activation(r[:], k.ps[2][:, :], ACT.Sqrt, scale=1.0 / SSD_W, bias=k.c("eps")).then_inc(s["rt"], 1)
                for g in range(POOL_G):
                    act.wait_ge(s["pmm"], g + 1)
                    if g >= 2:
                        act.wait_ge(s["omm"], g - 1)
                    act.activation(pl[:, g % 2, :], k.ps[5 + g % 2][:, :], ACT.Copy).then_inc(s["psb"], 1)

            @block.vector
            def _(dve):
                for m in range(XT):
                    dve.wait_ge(s["silu"], m + 1)
                    dve.tensor_tensor(t["mix"][:, m, :], t["mix"][:, m, :], zs[:, m % 2, :], ALU.mult).then_inc(s["y"], 1)
                for i in range(NT):
                    dve.wait_ge(s["umm"], i + 1)
                    dve.tensor_copy(ut[:, i, :], k.ps[3 + i % 2][:, :]).then_inc(s["usb"], 1)
                dve.wait_ge(s["rt"], 1)
                dve.reciprocal(r[:], r[:])
                dve.drain()
                for m in range(XT):
                    dve.scalar_tensor_tensor(t["mix"][:, m, :], t["mix"][:, m, :], k.v("g_ssd", m, m + 1), r[:], ALU.mult, ALU.mult)
                for g in range(POOL_G):
                    dve.wait_ge(s["omm"], g + 1)
                    dve.tensor_scalar(t["mix"][:, XT + g, :], k.ps[g % 2][:, :], k.v("pscale", g, g + 1), None, ALU.mult).then_inc(s["osb"], 1)
    k.end()


def spill_phase(k):
    s_out = k.sem("spilled")
    with k.nc.Block() as block:
        @block.sync
        def _(sp):
            sp.dma_start(k.a["spill_x"], k.xT[:]).then_inc(s_out, 16)
            sp.wait_ge(s_out, 16)
    k.end()


def clear_slots_phase(k):
    nc = k.nc
    with ExitStack() as mem:
        z = mem.enter_context(nc.sbuf_tensor("zero_row", [P, D], F32))
        s_z, s_out = k.sem("zero_ready"), k.sem("slots_cleared")
        with nc.Block() as block:
            @block.vector
            def _(dve):
                dve.memset(z[:], 0.0).then_inc(s_z, 1)

            @block.sync
            def _(sp):
                sp.wait_ge(s_z, 1)
                sp.dma_start(k.a["xs"].rearrange("(b p) d -> p b d", p=P), z[:].unsqueeze(1).to_broadcast([P, MAXB + 2, D])).then_inc(s_out, 16)
                sp.wait_ge(s_out, 16)
    k.end()


def two_blocks(nc, a, stop=None):
    ctx = ExitStack()
    with ctx:
        k = Core(nc, ctx, a)
        win, win2 = a["w_in"], a["w_in_2"]
        ada = [a["w_ada"][i] for i in range(12)] + [a["w_mod"][i] for i in range(12)]
        cols = lambda w, c0, c1, r0=0: w[r0 * P:(r0 + KT) * P, c0:c1].rearrange("(k p) n -> p k n", p=P)
        in1 = [cols(win, 512 * i, 512 * (i + 1)) for i in range(4)] + [cols(win, 2064, 2576)] + [a["w_tail"]]
        out1 = [cols(a["w_out"], 512 * i, 512 * (i + 1)) for i in range(2)]
        z0 = CONV_T * P + DT_C
        in2 = [cols(win2, 512 * i, 512 * (i + 1)) for i in range(5)] + [cols(win2, CONV_T * P, z0)] + \
              [cols(win2, z0 + 512 * i, z0 + 512 * (i + 1)) for i in range(4)]
        out2 = [cols(a["w_out_2"], 512 * n, 512 * (n + 1), KT * h) for n in range(2) for h in range(2)]
        k.pieces = ada + in1 + out1 + in2 + out2
        p_in1, p_out1 = 24, 30
        p_in2, p_z, p_out2 = 32, 38, 42
        table = k.sb("table", [P, 68], I32)
        slots = k.sb("slots", [P, TOP2, NT], I32)
        wts = k.sb("wts", [P, TOP2, NT])
        t = {"table": table, "slots": slots, "wts": wts}
        clear_slots_phase(k)
        modulation_phase(k)
        if stop == "mod":
            return k
        g = lambda n: (lambda kk: k.gain[:, n, kk:kk + 1])
        norm_phase(k, "n1", k.xT, k.hT, T, g(0), lambda kk: k.mod1[:, kk:kk + 1])
        with ExitStack() as mem:
            def sb(n, s, d=F32):
                t[n] = mem.enter_context(nc.sbuf_tensor(f"t_{n}", s, d))
            sb("qkv", [P, 12, T])
            sb("z", [P, NT, T])
            sb("swq", [P, 4, T])
            sb("swk", [P, SKV, WIN + T])
            sb("swv", [P, NT + 1, P])
            sb("ab", [P, NT, 16])
            for n in ("g", "beta"):
                sb(n, [P, NT, GH])
            sb("aexp", [P, GH])
            sb("dec", [P, 3, NT, GH])
            project1_phase(k, t, p_in1)
            if stop == "proj1":
                return k
            head_norm_phase(k, t)
            if stop == "head":
                return k
            t["att"] = k.hT[:].rearrange("p k (a b) -> p (k a) b", b=P)
            sb("mix", [P, KT, T])
            attention_phase(k, t)
            if stop == "attn":
                return k
            with ExitStack() as mem2:
                t["kvt"] = k.ring[:, 0, :].rearrange("p (a c n) -> p a c n", a=2, c=NT)
                t["S"] = k.ring[:, 1, :].rearrange("p (g n) -> p g n", n=P)
                gdn_prepare_phase(k, t)
                if stop == "gprep":
                    return k
                gdn_scan_phase(k, t)
            if stop == "gdn":
                return k
            output_phase(k, "o1", t["mix"], p_out1, 1, lambda m: k.mod1[:, 16 + m:17 + m], p_in2)
        if stop == "out1":
            return k
        norm_phase(k, "n2", k.xT, k.hT, T, g(1), lambda kk: k.mod1[:, 24 + kk:25 + kk])
        router_phase(k, "rt1", t, a["w_rt"], 4 + E, TOP1, k.r("b_rt"), True)
        if stop == "router1":
            return k
        expert_phase(k, "ex1", t, a["up1"], a["down1"], None, FF1, TOP1 * T // P)
        combine_phase(k, "cb1", t, TOP1, lambda kk: k.mod1[:, 40 + kk:41 + kk], p_in2 + RING)
        if stop == "block1":
            return k
        norm_phase(k, "n3", k.xT, k.hT, T, g(2), lambda kk: k.mod2[:, kk, 0:1])
        with ExitStack() as mem:
            def sb(n, s, d=F32):
                t[n] = mem.enter_context(nc.sbuf_tensor(f"u_{n}", s, d))
            sb("mix", [P, MIXT, T])
            with ExitStack() as mem1:
                for n, shape in (("bc", [P, 8, T]), ("dt", [P, NT + NC_, DT_C]), ("a", [P, NT + NC_, DT_C]),
                                 ("coef", [P, NT + NC_, 2, SSD_H]), ("etot", [P, NT + NC_, 2, SSD_H])):
                    t[n] = mem1.enter_context(nc.sbuf_tensor(f"u_{n}", shape, F32))
                xt_b = mem1.enter_context(nc.sbuf_tensor("u_xb", [P, 8192], F32))
                t["xtok"] = xt_b[:, 0:NT * SSD_W].rearrange("p (i c) -> p i c", i=NT)
                t["btok"] = xt_b[:, NT * SSD_W:8192].rearrange("p (i c) -> p i c", i=NT)
                hc = xt_b[:, 0:KT * CTX].rearrange("p (k n) -> p k n", k=KT)
                xflat = k.xT[:].rearrange("p k n -> p (k n)")
                cx = xflat[:, 0:KT * CTX].rearrange("p (k n) -> p k n", k=KT)
                spill_phase(k)
                norm_phase(k, "n4", cx, hc, CTX, g(4), lambda kk: k.mod2[:, kk, 1:2], load=a["ctxT"])
                t["xc"] = xflat.rearrange("p (m n) -> p m n", n=CTX)
                project2_phase(k, t, hc, p_in2)
                if stop == "proj2":
                    return k
                t["state"] = k.ring[:, 0, 0:2 * SSD_W].rearrange("p (d c) -> p d c", d=2)
                ssd_prepare_phase(k, t)
                if stop == "sprep":
                    return k
                ssd_scan_phase(k, t)
                if stop == "sscan":
                    return k
            gate2_phase(k, t, p_z)
            if stop == "gate2":
                return k
            output_phase(k, "o2", t["mix"], p_out2, 2, lambda m: k.mod2[:, 16 + m, 0:1], p_out2 + 4)
        if stop == "out2":
            return k
        norm_phase(k, "n5", k.xT, k.hT, T, g(3), lambda kk: k.mod2[:, 24 + kk, 0:1])
        router_phase(k, "rt2", t, a["w_rt2"], E, TOP2, k.r("b_rt2"), False)
        if stop == "router2":
            return k
        expert_phase(k, "ex2", t, a["up2"], a["down2"], a["bias2"], FF2, TOP2 * T // P)
        combine_phase(k, "cb2", t, TOP2, lambda kk: k.mod2[:, 40 + kk, 0:1], 0)
        norm_phase(k, "n6", k.xT, k.hT, T, lambda kk: k.v("g_fin", kk, kk + 1), None, store=a["out"])
    return k


def lay_out(x):
    f = np.ascontiguousarray
    col = lambda v: f(np.asarray(v).reshape(-1, P).T)
    i = x
    halves = lambda v: np.concatenate([np.asarray(v).reshape(-1, 1)] * 2, 0)
    conv = np.asarray(i["conv_w"])[0].reshape(4, 12, P).transpose(2, 1, 0).reshape(P, -1)
    conv2 = np.asarray(i["conv_w_2"])[0].reshape(5, CONV_T, P).transpose(2, 1, 0).reshape(P, -1)
    skip = np.repeat(np.asarray(i["d_skip_2"])[0], HD)
    vec = dict(c=col(i["c"]), c2=col(i["c_2"]), cc2=col(i["c_ctx_2"]), b_ada=col(i["b_ada"]), b_mod=col(i["b_mod_2"]),
               g_mix=col(i["norm_mix"]), g_ffn=col(i["norm_ffn"]), g1_2=col(i["norm1_w_2"]), g2_2=col(i["norm2_w_2"]),
               g_fin=col(i["final_norm_w_2"]), conv=conv, conv2=conv2, convb2=col(i["conv_b_2"]), qn=halves(i["q_norm"]),
               kn=halves(i["k_norm"]), skip=col(skip), pscale=col(i["pool_scale_2"]), g_ssd=col(i["ssd_norm_w_2"]))
    row = dict(a_log=i["a_log"], dt_bias=i["dt_bias"], g_out=i["gdn_out_norm"], sinks=i["sinks"],
               b_rt=np.concatenate([np.asarray(i["b_group"]).ravel(), np.asarray(i["b_router"]).ravel()]),
               a_log2=i["a_log_2"], dt_bias2=i["dt_bias_2"], b_rt2=i["router_b_2"])
    ktile = lambda w: f(np.asarray(w).reshape(KT, P, -1).transpose(1, 0, 2))
    pieces = lambda w: f(np.asarray(w)[0].reshape(KT, P, 12, 512).transpose(2, 1, 0, 3))
    w_in = np.asarray(i["w_in"])[0]
    tail = np.concatenate([w_in[:, 2576:2832], w_in[:, 2048:2064]], 1)
    gate, up = np.asarray(i["w_gate"])[0], np.asarray(i["w_up"])[0]
    up1 = np.concatenate([gate, up], 2).reshape(E, KT, P, 512).transpose(0, 2, 1, 3)
    down1 = np.asarray(i["w_down"])[0].reshape(E, 2, P, D).transpose(0, 2, 1, 3)
    w1 = np.asarray(i["w1_2"])[0].reshape(E, KT, P, 4, 256, 2).transpose(0, 3, 2, 1, 5, 4)
    w2 = np.asarray(i["w2_2"])[0].reshape(E, KT, P, 2, 512).transpose(0, 3, 2, 1, 4)
    b1 = np.asarray(i["b1_2"])[0].reshape(E, 4, 256, 2).transpose(0, 1, 3, 2).reshape(E, -1)
    return {
        "xT": f(np.asarray(i["x"])[0].T.reshape(KT, P, T).transpose(1, 0, 2)),
        "ctxT": f(np.asarray(i["ctx_2"])[0].T.reshape(KT, P, CTX).transpose(1, 0, 2)),
        "pos": f(np.asarray(i["positions"]).reshape(1, T)),
        "cst": shape_constants(),
        "vec": f(np.concatenate([vec[n] for n in VEC], 1)),
        "row": f(np.concatenate([np.asarray(row[n]).ravel() for n in ROW]).reshape(1, -1)),
        "w_ada": pieces(i["w_ada"]), "w_mod": pieces(i["w_mod_2"]),
        "w_in": f(w_in), "w_tail": ktile(tail), "w_out": f(np.asarray(i["w_out"])[0]),
        "w_rt": ktile(np.concatenate([np.asarray(i["w_group"])[0], np.asarray(i["w_router"])[0]], 1)),
        "up1": f(up1).reshape(E, P, -1), "down1": f(down1).reshape(E, P, -1),
        "w_in_2": f(np.asarray(i["w_in_2"])[0]), "w_out_2": f(np.asarray(i["w_out_2"])[0]),
        "pool_w": f(np.asarray(i["pool_w_2"])[0].transpose(1, 0, 2)),
        "w_rt2": ktile(np.asarray(i["router_w_2"])[0]),
        "up2": f(w1).reshape(4 * E, P, -1), "down2": f(w2).reshape(2 * E, P, -1),
        "bias2": f(np.concatenate([b1, np.asarray(i["b2_2"])[0]], 1)),
    }


def declare(nc, arrays):
    a = {}
    for name, x in arrays.items():
        a[name] = nc.dram_tensor(f"in_{name}", x.shape, mybir.dt.from_np(x.dtype), kind="ExternalInput").ap()
    for name, shape in (("xs", ((MAXB + 2) * P, D)), ("spill_h", (P, KT, T)), ("spill_x", (P, KT, T))):
        a[name] = nc.dram_tensor(name, shape, F32).ap()
    a["out"] = nc.dram_tensor("out_T", (D, T), F32, kind="ExternalOutput").ap()
    return a


def kernel(**inputs):
    import concourse.bacc as bacc
    from concourse.bass_utils import run_bass_kernel_spmd

    arrays = lay_out(inputs)
    nc = bacc.Bacc("TRN2", target_bir_lowering=False, num_devices=1)
    two_blocks(nc, declare(nc, arrays))
    r = run_bass_kernel_spmd(nc, [{f"in_{n}": x for n, x in arrays.items()}], core_ids=[0])
    return np.ascontiguousarray(np.asarray(r.results[0]["out_T"]).T).reshape(1, T, D)
```

```python
from contextlib import ExitStack

import numpy as np
import concourse.bass as bass
from concourse import mybir

F32 = mybir.dt.float32
I32 = mybir.dt.int32
ACT = mybir.ActivationFunctionType
ALU = mybir.AluOpType
AX = mybir.AxisListType

P = 128
D = 1024
T = 512
CTX = 256
KT = D // P
NT = T // P
NC_ = CTX // P
EPS = 1e-6
HD = 64
WIN = 128
GH = 8
GW = GH * HD
SH = 8
SKV = 2
SSD_W = 1536
SSD_H = 24
SSD_G = 4
HPG = SSD_H // SSD_G
ST = 128
XT = SSD_W // P
CONV_T = (SSD_W + 2 * SSD_G * ST) // P
DT_C = 2 * SSD_H
POOL_G = 4
WINDOWS = (2, 4, 8, 16)
GRID = 64
MIXT = 2 * D // P
E = 32
FF1 = 256
FF2 = 1024
TOP1 = 2
TOP2 = 4
LIMIT = 7.0
ALPHA = 1.702
BIG = 1e30
MAXB = TOP2 * T // P + E - 1 + 1
RING = 4
PIECE = KT * 512
LEVELS = 7
TWO_PI = 2.0 * np.pi
ZERO_W = 256
MAGIC = 1.5 * 2.0 ** 23


def columns(parts):
    at, out = 0, {}
    for name, width in parts:
        out[name] = (at, width)
        at += width
    return out, at


CONST, CONST_W = columns(
    [("ident", P), ("ones", P), ("le", P), ("lt", P), ("ge", P), ("gt", P), ("halves", P),
     ("rot", P), ("block", P), ("swa", 4 * P), ("level", LEVELS * P), ("pool", POOL_G * P),
     ("rev", E), ("rev4", 4), ("slot", 64), ("freq", 1), ("eps", 1), ("eps64", 1), ("thresh", 4), ("one", 1)])
VEC, VEC_W = columns(
    [("c", KT), ("c2", KT), ("cc2", KT), ("b_ada", 48), ("b_mod", 48), ("g_mix", KT),
     ("g_ffn", KT), ("g1_2", KT), ("g2_2", KT), ("g_fin", KT), ("conv", 12 * 4),
     ("conv2", CONV_T * 5), ("convb2", CONV_T), ("qn", 1), ("kn", 1), ("skip", XT),
     ("pscale", POOL_G), ("g_ssd", XT)])
ROW, ROW_W = columns(
    [("a_log", GH), ("dt_bias", GH), ("g_out", HD), ("sinks", SH), ("b_rt", 4 + E),
     ("a_log2", DT_C), ("dt_bias2", DT_C), ("b_rt2", E)])


def shape_constants():
    c = np.zeros((P, CONST_W), np.float32)

    def put(name, a):
        at, w = CONST[name]
        c[:, at:at + w] = a

    r, l = np.arange(P)[:, None], np.arange(P)[None, :]
    put("ident", r == l)
    put("ones", 1.0)
    put("le", r <= l)
    put("lt", r < l)
    put("ge", r >= l)
    put("gt", r > l)
    put("halves", r // HD == l // HD)
    put("block", r // HD == l // HD)
    rot = np.zeros((P, P), np.float32)
    for h in range(2):
        for d in range(32):
            rot[h * HD + d + 32, h * HD + d] = -1.0
            rot[h * HD + d, h * HD + d + 32] = 1.0
    put("rot", rot)
    kj = np.arange(2 * WIN)[None, :]
    rel = r + WIN - kj
    inside = (rel >= 0) & (rel < WIN)
    first = inside & (kj >= WIN)
    put("swa", np.concatenate([np.where(first, 0.0, -BIG), np.where(inside, 0.0, -BIG)], 1))
    lev = []
    for b in range(LEVELS):
        s = 1 << b
        lev.append((r // (2 * s) == l // (2 * s)) & (r // s < l // s))
    put("level", np.concatenate(lev, 1))
    pools = []
    for w in WINDOWS:
        m = np.zeros((P, P), np.float32)
        for row in range(P // GRID):
            for t in range(GRID):
                lo, hi = max(t - w // 2, 0), min(t + w - w // 2, GRID)
                m[row * GRID + lo:row * GRID + hi, row * GRID + t] = np.float32(1.0) / np.float32(hi - lo)
                m[row * GRID + t, row * GRID + t] -= 1.0
        pools.append(m)
    put("pool", np.concatenate(pools, 1))
    put("rev", np.float32(E) - np.arange(E)[None, :])
    put("rev4", np.float32(4) - np.arange(4)[None, :])
    put("slot", np.arange(64, dtype=np.float32)[None, :])
    half = HD // 2
    freq = np.power(np.float32(10000.0), -np.arange(half, dtype=np.float32) / np.float32(half)).astype(np.float32)
    put("freq", freq[(np.arange(P) % half)][:, None])
    put("eps", EPS)
    put("thresh", np.float32(P) * np.arange(4)[None, :])
    put("one", 1.0)
    return c


class Core:

    def __init__(self, nc, ctx, a):
        self.nc, self.ctx, self.a = nc, ctx, a
        self.cst = self.sb("cst", [P, CONST_W])
        self.vec = self.sb("vec", [P, VEC_W])
        self.row = self.sb("row", [P, ROW_W])
        self.xT = self.sb("xT", [P, KT, T])
        self.hT = self.sb("hT", [P, KT, T])
        self.ring = self.sb("ring", [P, RING, PIECE])
        self.mod1 = self.sb("mod1", [P, 48])
        self.mod2 = self.sb("mod2", [P, 48, 2])
        self.act2 = self.sb("act2", [P, 2, KT])
        self.gain = self.sb("gain", [P, 5, KT])
        self.ps = [ctx.enter_context(nc.psum_tensor(f"bank{i}", [P, 512], F32)) for i in range(8)]
        self.loaded = [nc.alloc_semaphore(f"piece_loaded{i}") for i in range(RING)]
        self.used = nc.alloc_semaphore("piece_used")
        self.inputs = nc.alloc_semaphore("inputs_loaded")
        self.zero = self.sb("zero", [P, ZERO_W])
        self.cleared = nc.alloc_semaphore("slots_cleared")
        self.phase_sems = []
        self.pieces = []
        self.sent = 0

    def sb(self, name, shape, dt=F32):
        return self.ctx.enter_context(self.nc.sbuf_tensor(name, shape, dt))

    def sem(self, name):
        self.phase_sems.append(self.nc.alloc_semaphore(name))
        return self.phase_sems[-1]

    def end(self):
        self.nc.clear_and_free_semaphores(self.phase_sems)
        self.nc.all_engine_barrier()
        self.phase_sems = []

    def c(self, name, lo=0, hi=None):
        at, w = CONST[name]
        return self.cst[:, at + lo:at + (w if hi is None else hi)]

    def v(self, name, lo=0, hi=None):
        at, w = VEC[name]
        return self.vec[:, at + lo:at + (w if hi is None else hi)]

    def r(self, name, lo=0, hi=None):
        at, w = ROW[name]
        return self.row[:, at + lo:at + (w if hi is None else hi)]

    def send_pieces(self, sp, upto):
        while self.sent < min(upto, len(self.pieces)):
            i = self.sent
            if i >= RING:
                sp.wait_ge(self.used, i - RING + 1)
            src = self.pieces[i]
            w = src.shape[-1]
            dst = self.ring[:, i % RING, 0:KT * w].rearrange("p (k n) -> p k n", k=KT)
            sp.dma_start(dst, src).then_inc(self.loaded[i % RING], 16)
            self.sent += 1

    def piece(self, pe, i):
        pe.wait_ge(self.loaded[i % RING], 16 * (i // RING + 1))
        w = self.pieces[i].shape[-1]
        return self.ring[:, i % RING, 0:KT * w].rearrange("p (k n) -> p k n", k=KT)


    def piece_done(self):
        one = self.c("one")
        self.nc.tensor.matmul(self.ps[7][0:1, 0:1], one, one, start=True, stop=True).then_inc(self.used, 1)


def bc(ap, n):
    return ap.unsqueeze(2).to_broadcast([ap.shape[0], ap.shape[1], n])


def bm(ap, n):
    return ap.unsqueeze(1).to_broadcast([ap.shape[0], n, ap.shape[1]])


def g4(ap, n=4):
    return ap.rearrange("p (h n) -> p h n", h=n)


MOD_P = 12
CTX_P = 4
MOD_ORDER = [4, 5, 6, 7, 8, 9, 0, 1, 2, 3, 10, 11]


def weighted_rows(dve, w, acc, columns, k0, k1):
    for kk in range(k0, k1):
        for a, cc in zip(acc, columns):
            if kk == 0:
                last = dve.tensor_scalar(a, w[:, kk, :], cc[:, kk:kk + 1], None, ALU.mult)
            else:
                last = dve.scalar_tensor_tensor(a, w[:, kk, :], cc[:, kk:kk + 1], a, ALU.mult, ALU.add)
        if kk < k1 - 1:
            dve.drain()
    return last


def modulation_phase(k):
    nc = k.nc
    own = [j for j in range(MOD_P) if j % 3 != 2]
    with ExitStack() as mem:
        sb = lambda n, s: mem.enter_context(nc.sbuf_tensor(n, s, F32))
        act1 = sb("m_act1", [P, KT])
        row1 = sb("m_row1", [1, 6 * D])
        acc = sb("m_acc", [P, 2, 512])
        consts, c_ready, row_mm, row_sb, s_acc, s_sum = (
            k.sem(f"m_{n}") for n in ("consts_loaded", "c_ready", "row_mm", "row_sb", "acc", "sum"))
        with nc.Block() as block:
            @block.sync
            def _(sp):
                sp.dma_start(k.vec[:], k.a["vec"]).then_inc(consts, 16)
                sp.dma_start(k.cst[:], k.a["cst"]).then_inc(consts, 16)
                k.send_pieces(sp, RING)
                sp.dma_start(k.row[:], k.a["row"].to_broadcast([P, ROW_W])).then_inc(k.inputs, 16)
                k.send_pieces(sp, MOD_P)
                sp.dma_start(k.xT[:], k.a["xT"]).then_inc(k.inputs, 16)
                k.send_pieces(sp, MOD_P + RING)
                sp.wait_ge(k.inputs, 32)

            @block.tensor
            def _(pe):
                def columns_of_row(j):
                    pe.wait_ge(row_sb, own.index(j) + 1)
                    for i in range(4 * j, 4 * j + 4):
                        nc.tensor.matmul(k.ps[2][:, i:i + 1], row1[0:1, i * P:(i + 1) * P], k.c("one")[0:1, :], start=True, stop=True)

                pe.wait_ge(c_ready, 3)
                for j in range(MOD_P):
                    if j in own:
                        w = k.piece(pe, j)
                        n = own.index(j)
                        if n >= 2:
                            pe.wait_ge(row_sb, n - 1)
                        for kk in range(KT):
                            last = nc.tensor.matmul(k.ps[n % 2][0:1, :], act1[:, kk:kk + 1], w[:, kk, :], start=kk == 0, stop=kk == KT - 1)
                        last.then_inc(row_mm, 1)
                    else:
                        columns_of_row(j - 2)
                        columns_of_row(j - 1)
                        pe.wait_ge(s_acc, j // 3 + 1)
                        for i in range(4):
                            last = nc.tensor.matmul(k.ps[2][:, 4 * j + i:4 * j + i + 1], acc[:, j // 3 % 2, i * P:(i + 1) * P], k.c("one"), start=True, stop=True)
                        last.then_inc(s_sum, 1)
                    k.piece_done()

            @block.scalar
            def _(act):
                act.wait_ge(consts, 32)
                act.activation(act1[:], k.v("c"), ACT.Silu).then_inc(c_ready, 1)
                act.activation(k.act2[:, 0, :], k.v("c2"), ACT.Silu).then_inc(c_ready, 1)
                act.activation(k.act2[:, 1, :], k.v("cc2"), ACT.Silu).then_inc(c_ready, 1)
                for n, j in enumerate(own):
                    act.wait_ge(row_mm, n + 1)
                    act.activation(row1[0:1, j * 512:(j + 1) * 512], k.ps[n % 2][0:1, :], ACT.Copy).then_inc(row_sb, 1)

            @block.vector
            def _(dve):
                dve.wait_ge(c_ready, 3)
                for n, j in enumerate(range(2, MOD_P, 3)):
                    w = k.piece(dve, j)
                    if n >= 2:
                        dve.wait_ge(s_sum, n - 1)
                    weighted_rows(dve, w, [acc[:, n % 2, :]], [act1], 0, KT).then_inc(s_acc, 1)
                dve.wait_ge(s_sum, MOD_P // 3)
                dve.tensor_tensor(k.mod1[:], k.ps[2][:, 0:48], k.v("b_ada"), ALU.add)
                dve.drain()
                for n, (scale, g) in enumerate(((k.mod1[:, 8:16], "g_mix"), (k.mod1[:, 32:40], "g_ffn"))):
                    dve.scalar_tensor_tensor(k.gain[:, n, :], scale, 1.0, k.v(g), ALU.add, ALU.mult)
    k.end()


def norm_phase(k, name, src, dst, n, gain, shift, load=None, store=None, spill=None, pieces=0):
    nc = k.nc
    ss = k.ps[0][:, 0:n]
    with ExitStack() as mem:
        r = mem.enter_context(nc.sbuf_tensor(f"{name}_r", [P, n], F32))
        s_sq, s_ss, s_rt, s_sc, s_st, s_ld = (k.sem(f"{name}_{x}") for x in ("squares", "sum", "root", "scaled", "stored", "src"))
        with nc.Block() as block:
            @block.sync
            def _(sp):
                if load is not None:
                    sp.dma_start(src[:], load).then_inc(s_ld, 16)
                if spill is not None:
                    sp.dma_start(spill, src[:]).then_inc(s_ld, 16)
                k.send_pieces(sp, pieces)
                if spill is not None:
                    sp.wait_ge(s_ld, 16)
                if store is not None:
                    for kk in range(KT):
                        sp.wait_ge(s_sc, kk + 1)
                        sp.dma_start(store[kk * P:(kk + 1) * P, :], dst[:, kk, 0:n]).then_inc(s_st, 16)
                    sp.wait_ge(s_st, 16 * KT)

            @block.scalar
            def _(act):
                if load is not None:
                    act.wait_ge(s_ld, 16)
                for kk in range(KT):
                    act.activation(dst[:, kk, 0:n], src[:, kk, 0:n], ACT.Square).then_inc(s_sq, 1)
                act.wait_ge(s_ss, 1)
                act.activation(r[:], ss, ACT.Sqrt, scale=1.0 / D, bias=k.c("eps")).then_inc(s_rt, 1)
                if shift is not None:
                    for kk in range(KT):
                        act.wait_ge(s_sc, kk + 1)
                        act.activation(dst[:, kk, 0:n], dst[:, kk, 0:n], ACT.Identity, bias=shift(kk))

            @block.tensor
            def _(pe):
                for kk in range(KT):
                    pe.wait_ge(s_sq, kk + 1)
                    last = nc.tensor.matmul(ss, k.c("ones"), dst[:, kk, 0:n], start=kk == 0, stop=kk == KT - 1)
                last.then_inc(s_ss, 1)

            @block.vector
            def _(dve):
                dve.wait_ge(s_rt, 1)
                dve.reciprocal(r[:], r[:])
                dve.drain()
                for kk in range(KT):
                    dve.scalar_tensor_tensor(dst[:, kk, 0:n], src[:, kk, 0:n], gain(kk), r[:], ALU.mult, ALU.mult).then_inc(s_sc, 1)
    k.end()


def project1_phase(k, t, first):
    nc = k.nc
    units = [("conv", m) for m in range(12)] + [("z", i) for i in range(NT)] + \
            [("sq", m) for m in range(4)] + [("sk", g) for g in range(SKV)] + [("vab", i) for i in range(NT)]
    piece_of = {"z": first + 9, "sq": first + 12, "sk": first + 15, "vab": first + 15}
    last_use = {3: 0, 7: 1, 11: 2, 15: 3, 19: 4, 25: 5}
    mod_piece = lambda j: first + 3 * (j // 2) + 1 + j % 2
    streams = lambda j: 2 if MOD_ORDER[j] < CTX_P else 1
    NB = 4
    with ExitStack() as mem:
        cv = mem.enter_context(nc.sbuf_tensor("p1_cv", [P, 2, T], F32))
        acc = mem.enter_context(nc.sbuf_tensor("p1_acc", [P, 2, 2, 512], F32))
        s_mm, s_act, s_cv, s_silu, s_acc, s_sum = (k.sem(f"p1_{n}") for n in ("mm", "act_free", "conv", "silu", "acc", "sum"))
        with nc.Block() as block:
            @block.sync
            def _(sp):
                k.send_pieces(sp, first + 20)

            @block.tensor
            def _(pe):
                for u, (kind, m) in enumerate(units):
                    if u >= NB:
                        old = u - NB
                        if units[old][0] == "conv":
                            pe.wait_ge(s_cv, old + 1)
                        else:
                            pe.wait_ge(s_act, old - 12 + 1)
                    w = k.piece(pe, first + 3 * (m // 4) if kind == "conv" else piece_of[kind])
                    o = k.ps[u % NB]
                    for kk in range(KT):
                        f = dict(start=kk == 0, stop=kk == KT - 1)
                        if kind in ("conv", "sq"):
                            c0 = (m % 4) * P
                            last = nc.tensor.matmul(o[:, :], w[:, kk, c0:c0 + P], k.hT[:, kk, :], **f)
                        elif kind == "sk":
                            last = nc.tensor.matmul(o[:, :], w[:, kk, m * P:(m + 1) * P], k.hT[:, kk, :], **f)
                        elif kind == "z":
                            last = nc.tensor.matmul(o[:, :], k.hT[:, kk, m * P:(m + 1) * P], w[:, kk, :], **f)
                        else:
                            last = nc.tensor.matmul(o[:, 0:144], k.hT[:, kk, m * P:(m + 1) * P], w[:, kk, 2 * P:3 * P + 16], **f)
                    last.then_inc(s_mm, 1)
                    if u in last_use:
                        k.piece_done()
                        for j in range(2 * last_use[u], 2 * last_use[u] + 2):
                            pe.wait_ge(s_acc, j + 1)
                            for i in range(4):
                                for x in range(streams(j)):
                                    at = 2 * (4 * MOD_ORDER[j] + i) + x
                                    last = nc.tensor.matmul(k.ps[4][:, at:at + 1], acc[:, j % 2, x, i * P:(i + 1) * P], k.c("one"), start=True, stop=True)
                            last.then_inc(s_sum, 1)
                            k.piece_done()

            @block.vector
            def _(dve):
                dve.memset(t["swk"][:, :, 0:WIN], 0.0)
                dve.memset(t["swv"][:, 0, :], 0.0)

                def modulate(j, k0, k1):
                    w = k.piece(dve, mod_piece(j))
                    if j >= 2:
                        dve.wait_ge(s_sum, j - 1)
                    n = streams(j)
                    last = weighted_rows(dve, w, [acc[:, j % 2, x, :] for x in range(n)], [k.act2[:, x, :] for x in range(n)], k0, k1)
                    if k1 == KT:
                        last.then_inc(s_acc, 1)

                for m in range(12):
                    half = KT // 2 * (m % 2)
                    modulate(m // 2, half, half + KT // 2)
                    dve.wait_ge(s_mm, m + 1)
                    if m >= 2:
                        dve.wait_ge(s_silu, m - 1)
                    y, x = cv[:, m % 2, :], k.ps[m % NB]
                    w = lambda j: k.v("conv", 4 * m + j, 4 * m + j + 1)
                    dve.tensor_scalar(y, x[:, :], w(3), None, ALU.mult)
                    for j in (2, 1, 0):
                        dve.drain()
                        s = 3 - j
                        last = dve.scalar_tensor_tensor(y[:, s:T], x[:, 0:T - s], w(j), y[:, s:T], ALU.mult, ALU.add)
                    last.then_inc(s_cv, 1)
                for j in range(6, MOD_P):
                    modulate(j, 0, KT)
                dve.wait_ge(s_sum, MOD_P)
                col2 = k.ps[4][:, 0:96].rearrange("p (i m) -> p i m", m=2)
                dve.tensor_tensor(k.mod2[:, :, 0], col2[:, :, 0], k.v("b_mod"), ALU.add)
                dve.tensor_tensor(k.mod2[:, 0:4 * CTX_P, 1], col2[:, 0:4 * CTX_P, 1], k.v("b_mod", 0, 4 * CTX_P), ALU.add)
                dve.drain()
                for n, (scale, g) in enumerate(((k.mod2[:, 8:16, 0], "g1_2"), (k.mod2[:, 32:40, 0], "g2_2"), (k.mod2[:, 8:16, 1], "g1_2"))):
                    dve.scalar_tensor_tensor(k.gain[:, 2 + n, :], scale, 1.0, k.v(g), ALU.add, ALU.mult)

            @block.scalar
            def _(act):
                for m in range(12):
                    act.wait_ge(s_cv, m + 1)
                    act.activation(t["qkv"][:, m, :], cv[:, m % 2, :], ACT.Silu).then_inc(s_silu, 1)
                for u in range(12, len(units)):
                    kind, m = units[u]
                    act.wait_ge(s_mm, u + 1)
                    o = k.ps[u % NB]
                    if kind == "z":
                        last = act.activation(t["z"][:, m, :], o[:, :], ACT.Silu)
                    elif kind == "sq":
                        last = act.activation(t["swq"][:, m, :], o[:, :], ACT.Copy)
                    elif kind == "sk":
                        last = act.activation(t["swk"][:, m, WIN:WIN + T], o[:, :], ACT.Copy)
                    else:
                        act.activation(t["swv"][:, 1 + m, :], o[:, 0:P], ACT.Copy)
                        last = act.activation(t["ab"][:, m, :], o[:, P:P + 16], ACT.Copy)
                    last.then_inc(s_act, 1)
    k.end()


def head_norm_phase(k, t):
    nc = k.nc
    tiles = [(t["qkv"][:, m, :], "l2q" if m < 4 else "l2k") for m in range(8)] + \
            [(t["swq"][:, m, :], "q") for m in range(4)] + [(t["swk"][:, g, WIN:WIN + T], "k") for g in range(SKV)]
    NH = 2 * len(tiles)
    order = list(range(8, len(tiles))) + list(range(8))
    NR = len(tiles) - 8
    with ExitStack() as mem:
        sb = lambda n, s, d=F32: mem.enter_context(nc.sbuf_tensor(n, s, d))
        sq, rt, cos, sin, ang = sb("h_sq", [P, 4, T]), sb("h_rt", [NH, T]), sb("h_cos", [P, T]), sb("h_sin", [P, T]), sb("h_ang", [P, T])
        pos, turn, t1 = sb("h_pos", [P, T], I32), sb("h_turn", [P, T]), sb("h_t1", [P, 2, T])
        pick, spread = sb("h_pick", [P, 2 * NH]), sb("h_spread", [NH, len(tiles) * P + 1])
        s_pos, s_sel, s_sq, s_ss, s_rt, s_inv, s_bc, s_nm, s_rot, s_ang, s_trig, s_fin, s_zero = (
            k.sem(f"h_{n}") for n in ("pos", "sel", "sq", "ss", "root", "inverse", "spread", "normed", "rotated", "angle", "trig", "free", "zero"))
        with nc.Block() as block:
            @block.sync
            def _(sp):
                sp.dma_start(pick[:], k.a["head_pick"]).then_inc(s_sel, 16)
                sp.dma_start(spread[:], k.a["head_spread"]).then_inc(s_sel, 16)
                sp.dma_start(pos[:], k.a["pos"].to_broadcast([P, T])).then_inc(s_pos, 16)
                sp.wait_ge(s_zero, 1)
                cut = k.a["xs"].rearrange("r (q d) -> (r q) d", d=ZERO_W).rearrange("(b p) d -> p b d", p=P)
                sp.dma_start(cut, bm(k.zero[:], cut.shape[1])).then_inc(k.cleared, 16)

            @block.scalar
            def _(act):
                for m, (x, kind) in enumerate(tiles):
                    if m >= 4:
                        act.wait_ge(s_ss, m - 3)
                    act.activation(sq[:, m % 4, :], x, ACT.Square).then_inc(s_sq, 1)
                act.wait_ge(s_ss, len(tiles))
                act.activation(rt[:], k.ps[0][0:NH, :], ACT.Sqrt, scale=spread[:, len(tiles) * P:len(tiles) * P + 1], bias=k.c("eps")[0:NH, :]).then_inc(s_rt, 1)
                act.wait_ge(s_ang, 2)
                act.activation(sin[:], sin[:], ACT.Sin).then_inc(s_trig, 1)
                act.activation(cos[:], cos[:], ACT.Sin).then_inc(s_trig, 1)

            @block.tensor
            def _(pe):
                pe.wait_ge(s_sel, 32)
                for m in range(len(tiles)):
                    pe.wait_ge(s_sq, m + 1)
                    nc.tensor.matmul(k.ps[0][0:NH, :], pick[:, NH - 2 * m:2 * NH - 2 * m], sq[:, m % 4, :], start=m == 0, stop=m == len(tiles) - 1).then_inc(s_ss, 1)
                pe.wait_ge(s_inv, 1)
                for n, m in enumerate(order):
                    if n >= 4:
                        pe.wait_ge(s_nm, n - 3)
                    nc.tensor.matmul(k.ps[1 + n % 4][:, :], spread[:, m * P:(m + 1) * P], rt[:], start=True, stop=True).then_inc(s_bc, 1)
                    if 1 <= n <= NR:
                        r = n - 1
                        pe.wait_ge(s_nm, r + 1)
                        if r >= 2:
                            pe.wait_ge(s_fin, r - 1)
                        nc.tensor.matmul(k.ps[5 + r % 2][:, :], k.c("rot"), tiles[order[r]][0], start=True, stop=True).then_inc(s_rot, 1)

            @block.vector
            def _(dve):
                c1 = 6.28125
                c2 = float(np.float32(np.float32((TWO_PI - c1) * 2 ** 20).astype(np.int64) / 2.0 ** 20))
                c3 = float(np.float32(TWO_PI - c1 - c2))
                dve.memset(k.zero[:], 0.0).then_inc(s_zero, 1)
                dve.wait_ge(s_pos, 16)
                dve.tensor_copy(turn[:], pos[:])
                dve.drain()
                dve.tensor_scalar(ang[:], turn[:], k.c("freq"), None, ALU.mult)
                dve.drain()
                for out, quarter in ((sin, 0.0), (cos, 0.25)):
                    dve.tensor_scalar(turn[:], ang[:], 1.0 / TWO_PI, quarter, ALU.mult, ALU.add)
                    dve.drain()
                    dve.tensor_scalar(turn[:], turn[:], MAGIC, None, ALU.add)
                    dve.drain()
                    dve.tensor_scalar(turn[:], turn[:], -MAGIC, None, ALU.add)
                    dve.drain()
                    dve.scalar_tensor_tensor(t1[:, 0, :], turn[:], -c1, ang[:], ALU.mult, ALU.add)
                    dve.drain()
                    dve.scalar_tensor_tensor(t1[:, 0, :], turn[:], -c2, t1[:, 0, :], ALU.mult, ALU.add)
                    dve.drain()
                    dve.scalar_tensor_tensor(t1[:, 0, :], turn[:], -c3, t1[:, 0, :], ALU.mult, ALU.add)
                    dve.drain()
                    dve.tensor_scalar(t1[:, 0, :], t1[:, 0, :], quarter * TWO_PI, 3.1415925, ALU.add, ALU.min)
                    dve.drain()
                    dve.tensor_scalar(out[:], t1[:, 0, :], -3.1415925, None, ALU.max).then_inc(s_ang, 1)
                dve.wait_ge(s_rt, 1)
                dve.reciprocal(rt[:], rt[:]).then_inc(s_inv, 1)

                def rotate(r):
                    x, tt = tiles[order[r]][0], t1[:, r % 2, :]
                    dve.wait_ge(s_rot, r + 1)
                    dve.tensor_tensor(tt, k.ps[5 + r % 2][:, :], sin[:], ALU.mult)
                    dve.tensor_tensor(x, x, cos[:], ALU.mult)
                    dve.drain()
                    dve.tensor_tensor(x, x, tt, ALU.add).then_inc(s_fin, 1)

                for n, m in enumerate(order):
                    x, kind = tiles[m]
                    dve.wait_ge(s_bc, n + 1)
                    g = {"l2q": HD ** -0.5, "l2k": 1.0, "q": k.v("qn"), "k": k.v("kn")}[kind]
                    dve.scalar_tensor_tensor(x, x, g, k.ps[1 + n % 4][:, :], ALU.mult, ALU.mult).then_inc(s_nm, 1)
                    if n == 2:
                        dve.wait_ge(s_trig, 2)
                    if 2 <= n < NR + 2:
                        rotate(n - 2)
    k.end()


def gdn_prepare_phase(k, t):
    nc = k.nc
    NG = 2 * NT
    PREPARE = (1, 3)
    with ExitStack() as mem:
        sb = lambda n, s: mem.enter_context(nc.sbuf_tensor(n, s, F32))
        tmp, tmp2 = sb("g_tmp", [P, NT, GH]), sb("g_tmp2", [P, NT, GH])
        gu, em, Ab, Tm, Z = (sb(f"g_{n}", [P, 2, 4, P]) for n in ("gu", "em", "Ab", "T", "Z"))
        A = sb("g_A", [P, 4, 4, P])
        names = ("tok_mm", "tok_sb", "ga", "gb", "small", "cum", "gu", "arg", "raw", "done", "exp", "A", "ab", "zmm", "zsb", "tmm", "tsb", "gate", "e1", "e2")
        s = {n: k.sem(f"g_{n}") for n in names}
        with nc.Block() as block:
            @block.scalar
            def _(act):
                for n in range(2 * NT):
                    act.wait_ge(s["tok_mm"], n + 1)
                    kv, c = divmod(n, NT)
                    act.activation(t["kvt"][:, kv, c, :], k.ps[n % 2][:, :], ACT.Copy).then_inc(s["tok_sb"], 1)
                act.wait_ge(s["ga"], 1)
                act.activation(tmp[:], tmp[:], ACT.Exp).then_inc(s["e1"], 1)
                act.activation(t["aexp"][:], k.r("a_log"), ACT.Exp).then_inc(s["e1"], 1)
                act.wait_ge(s["e1"], 2)
                act.activation(tmp[:], tmp[:], ACT.Ln, bias=k.c("one")).then_inc(s["e2"], 1)
                act.activation(t["beta"][:], t["ab"][:, :, GH:2 * GH], ACT.Sigmoid).then_inc(s["e2"], 1)
                act.wait_ge(s["cum"], 1)
                act.activation(t["dec"][:].rearrange("p a c h -> p (a c h)"), k.ps[2][:, 0:3 * NT * GH], ACT.Exp).then_inc(s["small"], 1)
                def exps(q):
                    act.wait_ge(s["arg"], q + 1)
                    act.activation(em[:, q % 2].rearrange("p h n -> p (h n)"), k.ps[6][:, :], ACT.Exp).then_inc(s["exp"], 1)

                exps(0)
                exps(1)
                for pair in range(NG // 2):
                    for l in range(LEVELS):
                        for w in range(2 if l else 0):
                            n = (pair * (LEVELS - 1) + l - 1) * 2 + w
                            act.wait_ge(s["zmm"], n + 1)
                            act.activation(Z[:, w].rearrange("p h n -> p (h n)"), k.ps[3 * w][:, :], ACT.Copy).then_inc(s["zsb"], 1)
                        if l in PREPARE and pair + 1 < NG // 2:
                            exps(2 * pair + 2 + PREPARE.index(l))

            @block.vector
            def _(dve):
                g = t["g"]
                dve.tensor_tensor(g[:], t["ab"][:, :, 0:GH], bm(k.r("dt_bias"), NT), ALU.add)
                dve.drain()
                dve.tensor_scalar(tmp2[:], g[:], -1.0, None, ALU.mult)
                dve.drain()
                dve.tensor_tensor(tmp[:], g[:], tmp2[:], ALU.min).then_inc(s["ga"], 1)
                dve.wait_ge(s["e2"], 2)
                dve.scalar_tensor_tensor(g[:], g[:], 0.0, tmp[:], ALU.max, ALU.add)
                dve.drain()
                dve.tensor_tensor(g[:], g[:], bm(t["aexp"][:], NT), ALU.mult)
                dve.drain()
                dve.tensor_scalar(g[:], g[:], -1.0, None, ALU.mult).then_inc(s["gate"], 1)
                dve.drain()
                def decays(q):
                    c, hg = divmod(q, 2)
                    for h in range(4):
                        last = dve.tensor_scalar(gu[:, q % 2, h, :], k.c("le"), g[:, c, 4 * hg + h:4 * hg + h + 1], None, ALU.mult)
                    last.then_inc(s["gu"], 1)

                def products(q):
                    c, hg = divmod(q, 2)
                    dve.wait_ge(s["exp"], q + 1)
                    e, M = em[:, q % 2], A[:, q % 4]
                    dve.tensor_tensor(e, e, bm(k.c("le"), 4), ALU.mult)
                    dve.drain()
                    for par in range(2):
                        dve.wait_ge(s["raw"], 2 * q + par + 1)
                        raw = g4(k.ps[7 - par][:, :])
                        dve.tensor_tensor(t["att"][:, 4 * q + par:4 * q + 4:2, :], e[:, par::2, :], raw[:, 2:4, :], ALU.mult)
                        dve.tensor_tensor(M[:, par::2, :], e[:, par::2, :], raw[:, 0:2, :], ALU.mult).then_inc(s["done"], 1)
                    dve.drain()
                    dve.tensor_tensor(M, M, bm(k.c("lt"), 4), ALU.mult)
                    dve.drain()
                    dve.tensor_tensor(M, M, bc(t["beta"][:, c, 4 * hg:4 * hg + 4], P), ALU.mult).then_inc(s["A"], 1)

                for q in range(2):
                    decays(q)
                for q in range(2):
                    products(q)
                for pair in range(NG // 2):
                    if pair + 1 < NG // 2:
                        for w in range(2):
                            decays(2 * pair + 2 + w)
                    for l in range(LEVELS):
                        for w in range(2):
                            q = 2 * pair + w
                            n = (pair * LEVELS + l) * 2 + w
                            S = t["S"][:, 4 * q:4 * q + 4, :]
                            dve.wait_ge(s["tmm"], n + 1)
                            if l == 0:
                                dve.tensor_tensor(Tm[:, w], bm(k.c("ident"), 4), g4(k.ps[3 * w + 1][:, :]), ALU.subtract)
                                dve.tensor_tensor(S, bm(k.c("ident"), 4), Ab[:, w], ALU.subtract).then_inc(s["tsb"], 1)
                                dve.drain()
                                continue
                            if l < LEVELS - 1:
                                dve.tensor_tensor(Tm[:, w], Tm[:, w], g4(k.ps[3 * w + 1][:, :]), ALU.subtract)
                            dve.tensor_tensor(S, S, g4(k.ps[3 * w + 2][:, :]), ALU.subtract).then_inc(s["tsb"], 1)
                            dve.drain()
                        if l in PREPARE and pair + 1 < NG // 2:
                            products(2 * pair + 2 + PREPARE.index(l))

            @block.gpsimd
            def _(pool):
                for pair in range(NG // 2):
                    for w in range(2):
                        pool.wait_ge(s["A"], 2 * pair + w + 1)
                    for l in range(LEVELS):
                        for w in range(2):
                            n = (pair * LEVELS + l) * 2 + w
                            z = (pair * (LEVELS - 1) + l - 1) * 2 + w
                            if l == 1:
                                pool.wait_ge(s["tsb"], n - 1)
                            elif n >= 2:
                                pool.wait_ge(s["zmm"], z - 1 if l else z + 1)
                            pool.tensor_tensor(Ab[:, w], A[:, (2 * pair + w) % 4], bm(k.c("level", l * P, (l + 1) * P), 4), ALU.mult).then_inc(s["ab"], 1)

            @block.tensor
            def _(pe):
                for n in range(2 * NT):
                    kv, c = divmod(n, NT)
                    if n >= 2:
                        pe.wait_ge(s["tok_sb"], n - 1)
                    for m in range(4):
                        last = nc.tensor.transpose(k.ps[n % 2][:, m * P:(m + 1) * P], t["qkv"][:, 4 + 4 * kv + m, c * P:(c + 1) * P], k.c("ident"))
                    last.then_inc(s["tok_mm"], 1)
                pe.wait_ge(s["gate"], 1)
                flat = t["g"][:].rearrange("p c h -> p (c h)")
                n = NT * GH
                for i, mask in enumerate(("le", "gt", "ones")):
                    last = nc.tensor.matmul(k.ps[2][:, i * n:(i + 1) * n], k.c(mask), flat, start=True, stop=True)
                last.then_inc(s["cum"], 1)
                pe.wait_ge(s["small"], 1)
                pe.wait_ge(s["tok_sb"], 2 * NT)
                def decay_sums(q):
                    pe.wait_ge(s["gu"], q + 1)
                    if q >= 1:
                        pe.wait_ge(s["done"], 2 * q)
                    nc.tensor.matmul(k.ps[6][:, :], k.c("gt"), gu[:, q % 2].rearrange("p h n -> p (h n)"), start=True, stop=True).then_inc(s["arg"], 1)

                def raw_products(q):
                    c, hg = divmod(q, 2)
                    pe.wait_ge(s["exp"], q + 1)
                    for par in range(2):
                        for at in range(2):
                            m, o = 2 * hg + at, HD * par
                            kk = t["qkv"][o:o + HD, 4 + m, c * P:(c + 1) * P]
                            bank = k.ps[7 - par]
                            nc.tensor.matmul(bank[:, at * P:(at + 1) * P], kk, kk, start=True, stop=True)
                            last = nc.tensor.matmul(bank[:, (2 + at) * P:(3 + at) * P], kk, t["qkv"][o:o + HD, m, c * P:(c + 1) * P], start=True, stop=True)
                        last.then_inc(s["raw"], 1)

                for q in range(2):
                    decay_sums(q)
                    raw_products(q)
                for pair in range(NG // 2):
                    for l in range(LEVELS):
                        new = 2 * pair + 2 + PREPARE.index(l) if l in PREPARE and pair + 1 < NG // 2 else None
                        if new is not None:
                            decay_sums(new)
                        for w in range(2):
                            n = (pair * LEVELS + l) * 2 + w
                            pe.wait_ge(s["ab"], n + 1)
                            if n >= 2:
                                pe.wait_ge(s["tsb"], n - 1)
                            if l == 0:
                                for h in range(4):
                                    last = nc.tensor.transpose(k.ps[3 * w + 1][:, h * P:(h + 1) * P], Ab[:, w, h, :], k.c("ident"))
                                last.then_inc(s["tmm"], 1)
                                continue
                            for h in range(4):
                                last = nc.tensor.matmul(k.ps[3 * w][:, h * P:(h + 1) * P], Ab[:, w, h, :], Tm[:, w, h, :], start=True, stop=True)
                            last.then_inc(s["zmm"], 1)
                        for w in range(2 if l else 0):
                            q = 2 * pair + w
                            pe.wait_ge(s["zsb"], (pair * (LEVELS - 1) + l - 1) * 2 + w + 1)
                            for h in range(4):
                                S = t["S"][:, 4 * q + h, :]
                                if l < LEVELS - 1:
                                    nc.tensor.matmul(k.ps[3 * w + 1][:, h * P:(h + 1) * P], S, Z[:, w, h, :], start=True, stop=True)
                                last = nc.tensor.matmul(k.ps[3 * w + 2][:, h * P:(h + 1) * P], Z[:, w, h, :], S, start=True, stop=True)
                            last.then_inc(s["tmm"], 1)
                        if new is not None:
                            raw_products(new)
    k.end()


def gdn_scan_phase(k, t):
    nc = k.nc
    H8 = lambda ap: ap.rearrange("p (h e) -> p h e", h=GH)
    with ExitStack() as mem:
        sb = lambda n, s: mem.enter_context(nc.sbuf_tensor(n, s, F32))
        S = sb("s_state", [P, GW])
        r, vn, qs, kd, sq = (sb(f"s_{n}", [P, GW]) for n in ("r", "vn", "qs", "kd", "sq"))
        out = sb("s_o", [P, 2, GW])
        st = sb("s_stat", [P, GH])
        names = ("state", "ks", "r", "vmm", "vn", "qs", "qsb", "omm", "kd", "smm", "o", "osq", "ms", "rt", "fin", "tmm", "tsb", "oread")
        s = {n: k.sem(f"s_{n}") for n in names}
        with nc.Block() as block:
            @block.gpsimd
            def _(pool):
                for c in range(NT):
                    if c >= 1:
                        pool.wait_ge(s["smm"], c)
                    pool.tensor_tensor(H8(kd[:]), H8(t["kvt"][:, 0, c, :]), bc(t["dec"][:, 1, c, :], HD), ALU.mult).then_inc(s["kd"], 1)

            @block.scalar
            def _(act):
                for c in range(NT):
                    act.wait_ge(s["fin"], c + 1)
                    act.activation(st[:], st[:], ACT.Sqrt, scale=1.0 / HD, bias=k.c("eps")).then_inc(s["rt"], 1)
                    act.wait_ge(s["tmm"], c + 1)
                    act.activation(t["mix"][:, 0:4, c * P:(c + 1) * P], g4(k.ps[5][:, :]), ACT.Copy).then_inc(s["tsb"], 1)

            @block.vector
            def _(dve):
                def finish(c):
                    o = out[:, c % 2, :]
                    dve.tensor_tensor(sq[:], o, o, ALU.mult)
                    dve.drain()
                    dve.tensor_reduce(st[:], H8(sq[:]), AX.X, ALU.add).then_inc(s["fin"], 1)
                    dve.tensor_tensor(o, o, t["z"][:, c, :], ALU.mult)
                    dve.drain()
                    dve.tensor_tensor(H8(o), H8(o), bm(k.r("g_out"), GH), ALU.mult)
                    dve.wait_ge(s["rt"], c + 1)
                    dve.reciprocal(st[:], st[:])
                    dve.drain()
                    dve.tensor_tensor(H8(o), H8(o), bc(st[:], HD), ALU.mult).then_inc(s["o"], 1)

                dve.memset(S[:], 0.0).then_inc(s["state"], 1)
                dve.drain()
                for c in range(NT):
                    eG, eT = t["dec"][:, 0, c, :], t["dec"][:, 2, c, :]
                    dve.wait_ge(s["ks"], c + 1)
                    dve.tensor_tensor(H8(r[:]), H8(k.ps[0][:, :]), bc(eG, HD), ALU.mult)
                    dve.drain()
                    dve.tensor_tensor(r[:], t["kvt"][:, 1, c, :], r[:], ALU.subtract).then_inc(s["r"], 1)
                    dve.tensor_tensor(H8(qs[:]), H8(k.ps[1][:, :]), bc(eG, HD), ALU.mult)
                    dve.wait_ge(s["vmm"], c + 1)
                    dve.tensor_tensor(H8(vn[:]), H8(k.ps[2][:, :]), bc(t["beta"][:, c, :], HD), ALU.mult).then_inc(s["vn"], 1)
                    dve.tensor_tensor(H8(S[:]), H8(S[:]), bc(eT, HD), ALU.mult)
                    if c >= 1:
                        finish(c - 1)
                    if c >= 2:
                        dve.wait_ge(s["tmm"], c - 1)
                    dve.wait_ge(s["omm"], c + 1)
                    dve.drain()
                    dve.tensor_tensor(out[:, c % 2, :], k.ps[3][:, :], qs[:], ALU.add)
                    dve.wait_ge(s["smm"], c + 1)
                    dve.tensor_tensor(g4(r[:]), g4(k.ps[4][:, :]), bm(k.c("block"), 4), ALU.mult)
                    dve.drain()
                    dve.tensor_tensor(S[:], S[:], r[:], ALU.add).then_inc(s["state"], 1)
                finish(NT - 1)

            @block.tensor
            def _(pe):
                def out_transposes(c):
                    pe.wait_ge(s["o"], c + 1)
                    if c >= 1:
                        pe.wait_ge(s["tsb"], c)
                    for m in range(4):
                        last = nc.tensor.transpose(k.ps[5][:, m * P:(m + 1) * P], out[:, c % 2, m * P:(m + 1) * P], k.c("ident"))
                    last.then_inc(s["tmm"], 1)

                for c in range(NT):
                    tok = slice(c * P, (c + 1) * P)
                    pe.wait_ge(s["state"], c + 1)
                    for m in range(4):
                        last = nc.tensor.matmul(k.ps[0][:, m * P:(m + 1) * P], t["qkv"][:, 4 + m, tok], S[:, m * P:(m + 1) * P], start=True, stop=True)
                        last = nc.tensor.matmul(k.ps[1][:, m * P:(m + 1) * P], t["qkv"][:, m, tok], S[:, m * P:(m + 1) * P], start=True, stop=True)
                    last.then_inc(s["ks"], 1)
                    pe.wait_ge(s["r"], c + 1)
                    for h in range(GH):
                        last = nc.tensor.matmul(k.ps[2][:, h * HD:(h + 1) * HD], t["S"][:, c * GH + h, :], r[:, h * HD:(h + 1) * HD], start=True, stop=True)
                    last.then_inc(s["vmm"], 1)
                    pe.wait_ge(s["vn"], c + 1)
                    for h in range(GH):
                        last = nc.tensor.matmul(k.ps[3][:, h * HD:(h + 1) * HD], t["att"][:, c * GH + h, :], vn[:, h * HD:(h + 1) * HD], start=True, stop=True)
                    last.then_inc(s["omm"], 1)
                    pe.wait_ge(s["kd"], c + 1)
                    for m in range(4):
                        last = nc.tensor.matmul(k.ps[4][:, m * P:(m + 1) * P], kd[:, m * P:(m + 1) * P], vn[:, m * P:(m + 1) * P], start=True, stop=True)
                    last.then_inc(s["smm"], 1)
                    if c >= 1:
                        out_transposes(c - 1)
                out_transposes(NT - 1)
    k.end()


def attention_phase(k, t):
    nc = k.nc
    units = [(n, hp) for n in range(NT) for hp in range(4)]
    with ExitStack() as mem:
        sb = lambda n, s: mem.enter_context(nc.sbuf_tensor(n, s, F32))
        NB = 4
        sc, pT = sb("a_sc", [P, NB, 2, 2 * WIN]), sb("a_pT", [P, 2, 4, P])
        mx, nmx, den, snk = (sb(f"a_{n}", [P, NB, 2]) for n in ("mx", "nmx", "den", "snk"))
        out = sb("a_out", [P, 2, GW])
        names = ("smm", "mx", "exp", "snk", "tmm", "tsb", "pv", "out", "omm", "osb")
        s = {n: k.sem(f"a_{n}") for n in names}
        with nc.Block() as block:
            @block.tensor
            def _(pe):
                def scores(u):
                    n, hp = units[u]
                    if u >= 2:
                        pe.wait_ge(s["mx"], u - 1)
                    for i in range(2):
                        g = (2 * hp + i) // 4
                        o = HD * i
                        last = nc.tensor.matmul(k.ps[2 * (u % 2) + i][:, 0:256], t["swq"][o:o + HD, hp, n * P:(n + 1) * P],
                                                t["swk"][o:o + HD, g, n * P:n * P + 256], start=True, stop=True)
                    last.then_inc(s["smm"], 1)

                def transposes(u):
                    pe.wait_ge(s["exp"], u + 1)
                    if u >= 2:
                        pe.wait_ge(s["tsb"], u - 1)
                    for i in range(2):
                        for b in range(2):
                            last = nc.tensor.transpose(k.ps[4 + u % 2][:, (2 * i + b) * P:(2 * i + b + 1) * P],
                                                       sc[:, u % NB, i, b * P:(b + 1) * P], k.c("ident"))
                    last.then_inc(s["tmm"], 1)

                def values(u):
                    n, hp = units[u]
                    pe.wait_ge(s["tsb"], u + 1)
                    if u >= 1:
                        pe.wait_ge(s["out"], u)
                    for i in range(2):
                        g = (2 * hp + i) // 4
                        for b in range(2):
                            last = nc.tensor.matmul(k.ps[6][:, i * HD:(i + 1) * HD], pT[:, u % 2, 2 * i + b, :],
                                                    t["swv"][:, n + b, g * HD:(g + 1) * HD], start=b == 0, stop=b == 1)
                    last.then_inc(s["pv"], 1)

                def out_transposes(n):
                    pe.wait_ge(s["out"], 4 * n + 4)
                    if n >= 1:
                        pe.wait_ge(s["osb"], n)
                    for m in range(4):
                        last = nc.tensor.transpose(k.ps[7][:, m * P:(m + 1) * P], out[:, n % 2, m * P:(m + 1) * P], k.c("ident"))
                    last.then_inc(s["omm"], 1)

                scores(0)
                scores(1)
                for u in range(len(units)):
                    transposes(u)
                    if u + 2 < len(units):
                        scores(u + 2)
                    if u >= 1:
                        values(u - 1)
                    if u >= 5 and u % 4 == 1:
                        out_transposes(u // 4 - 1)
                values(len(units) - 1)
                out_transposes(NT - 1)

            @block.vector
            def _(dve):
                def prepare(u):
                    n, hp = units[u]
                    m0 = 0 if n == 0 else 256
                    dve.wait_ge(s["smm"], u + 1)
                    if u >= NB:
                        dve.wait_ge(s["tmm"], u - NB + 1)
                    for i in range(2):
                        dve.scalar_tensor_tensor(sc[:, u % NB, i, :], k.ps[2 * (u % 2) + i][:, 0:256], HD ** -0.5, k.c("swa", m0, m0 + 256), ALU.mult, ALU.add)
                    dve.drain()
                    dve.tensor_reduce(mx[:, u % NB, :], sc[:, u % NB], AX.X, ALU.max)
                    dve.drain()
                    dve.tensor_tensor(mx[:, u % NB, :], mx[:, u % NB, :], k.r("sinks", 2 * hp, 2 * hp + 2), ALU.max)
                    dve.drain()
                    dve.tensor_tensor(snk[:, u % NB, :], k.r("sinks", 2 * hp, 2 * hp + 2), mx[:, u % NB, :], ALU.subtract)
                    dve.tensor_scalar(nmx[:, u % NB, :], mx[:, u % NB, :], -1.0, None, ALU.mult).then_inc(s["mx"], 1)

                def finish(u):
                    n, hp = units[u]
                    dve.wait_ge(s["snk"], u + 1)
                    dve.tensor_tensor(den[:, u % NB, :], den[:, u % NB, :], snk[:, u % NB, :], ALU.add)
                    dve.drain()
                    dve.reciprocal(den[:, u % NB, :], den[:, u % NB, :])
                    dve.drain()
                    dve.wait_ge(s["pv"], u + 1)
                    if hp == 0 and n >= 2:
                        dve.wait_ge(s["omm"], n - 1)
                    dve.tensor_tensor(out[:, n % 2, hp * P:(hp + 1) * P].rearrange("p (i e) -> p i e", i=2),
                                      k.ps[6][:, 0:P].rearrange("p (i e) -> p i e", i=2), bc(den[:, u % NB, :], HD), ALU.mult).then_inc(s["out"], 1)

                prepare(0)
                prepare(1)
                for u in range(len(units)):
                    dve.wait_ge(s["tmm"], u + 1)
                    dve.tensor_copy(pT[:, u % 2], g4(k.ps[4 + u % 2][:, :])).then_inc(s["tsb"], 1)
                    if u + 2 < len(units):
                        prepare(u + 2)
                    if u >= 1:
                        finish(u - 1)
                finish(len(units) - 1)

            @block.scalar
            def _(act):
                def mixed(n):
                    act.wait_ge(s["omm"], n + 1)
                    act.activation(t["mix"][:, 4:8, n * P:(n + 1) * P], g4(k.ps[7][:, :]), ACT.Copy).then_inc(s["osb"], 1)

                for u, (n, hp) in enumerate(units):
                    act.wait_ge(s["mx"], u + 1)
                    for i in range(2):
                        last = act.activation(sc[:, u % NB, i, :], sc[:, u % NB, i, :], ACT.Exp, bias=nmx[:, u % NB, i:i + 1],
                                              accum_out=den[:, u % NB, i:i + 1])
                    last.then_inc(s["exp"], 1)
                    act.activation(snk[:, u % NB, :], snk[:, u % NB, :], ACT.Exp).then_inc(s["snk"], 1)
                    if hp == 2 and n >= 1:
                        mixed(n - 1)
                mixed(NT - 1)
    k.end()


def output_phase(k, name, mix, first, halves, gate, keep):
    nc = k.nc
    s_mm, s_sb = k.sem(f"{name}_mm"), k.sem(f"{name}_sb")
    with nc.Block() as block:
        @block.sync
        def _(sp):
            k.send_pieces(sp, keep)

        @block.tensor
        def _(pe):
            for n in range(2):
                for h in range(halves):
                    w = k.piece(pe, first + n * halves + h)
                    for m in range(4):
                        u = 4 * n + m
                        if u >= 4 and h == 0:
                            pe.wait_ge(s_sb, u - 3)
                        for kk in range(KT):
                            last = nc.tensor.matmul(k.ps[m][:, :], w[:, kk, m * P:(m + 1) * P], mix[:, h * KT + kk, :],
                                                    start=h == 0 and kk == 0, stop=h == halves - 1 and kk == KT - 1)
                        if h == halves - 1:
                            last.then_inc(s_mm, 1)
                    k.piece_done()

        @block.vector
        def _(dve):
            for u in range(KT):
                dve.wait_ge(s_mm, u + 1)
                dve.scalar_tensor_tensor(k.xT[:, u, :], k.ps[u % 4][:, :], gate(u), k.xT[:, u, :], ALU.mult, ALU.add).then_inc(s_sb, 1)
    k.end()


def router_phase(k, name, t, w_src, n_logits, top, b_row, hier):
    nc = k.nc
    with ExitStack() as mem:
        sb = lambda n, s, d=F32: mem.enter_context(nc.sbuf_tensor(f"{name}_{n}", s, d))
        wr = sb("wr", [P, KT, n_logits])
        htok = sb("htok", [P, NT, D])
        lg, lm, eq, key = sb("lg", [P, NT, n_logits]), sb("lm", [P, NT, E]), sb("eq", [P, NT, E]), sb("key", [P, NT, E])
        oh = sb("oh", [P, top, NT, E])
        asg, pre = sb("asg", [P, NT, E]), sb("pre", [P, NT, E])
        m, mk = sb("m", [P, top, NT]), sb("mk", [P, NT])
        gl, gm, geq, gk, pg = sb("gl", [P, NT, 4]), sb("gm", [P, NT]), sb("geq", [P, NT, 4]), sb("gk", [P, NT]), sb("pg", [P, NT])
        cnt, blk, tot, beg = sb("cnt", [P, E]), sb("blk", [P, 4, E]), sb("tot", [P, E]), sb("beg", [P, E])
        pos, sl = sb("pos", [P, NT, E]), sb("sl", [P, top, NT])
        cmp_, tabf = sb("cmp", [P, 64, E]), sb("tabf", [P, 64])
        zero, lt = sb("zero", [P, E]), sb("lt", [n_logits, T])
        names = ("w", "ltmm", "lt", "lmm", "tmm", "tsb", "row", "gexp_in", "gexp", "exp_in", "exp", "asg", "rank", "slots", "sent")
        s = {n: k.sem(f"{name}_{n}") for n in names}
        with nc.Block() as block:
            @block.sync
            def _(sp):
                sp.dma_start(wr[:], w_src).then_inc(s["w"], 16)

            @block.tensor
            def _(pe):
                pe.wait_ge(s["w"], 16)
                for kk in range(KT):
                    last = nc.tensor.matmul(k.ps[5][0:n_logits, :], wr[:, kk, :], k.hT[:, kk, :], start=kk == 0, stop=kk == KT - 1)
                last.then_inc(s["ltmm"], 1)
                for n in range(2 * NT):
                    if n == 1:
                        pe.wait_ge(s["lt"], 1)
                        for i in range(NT):
                            last = nc.tensor.transpose(k.ps[0][:, i * 64:i * 64 + n_logits], lt[:, i * P:(i + 1) * P], k.c("ident", 0, n_logits)[0:n_logits, :])
                        last.then_inc(s["lmm"], 1)
                    i, half = divmod(n, 2)
                    if n >= 2:
                        pe.wait_ge(s["tsb"], n - 1)
                    for j in range(4):
                        last = nc.tensor.transpose(k.ps[2 + n % 2][:, j * P:(j + 1) * P], k.hT[:, 4 * half + j, i * P:(i + 1) * P], k.c("ident"))
                    last.then_inc(s["tmm"], 1)
                pe.wait_ge(s["asg"], 1)
                fl = lambda a: a[:].rearrange("p i e -> p (i e)")
                nc.tensor.matmul(k.ps[1][:, 0:NT * E], k.c("lt"), fl(asg), start=True, stop=False)
                nc.tensor.matmul(k.ps[1][:, 0:NT * E], k.c("ones"), fl(pre), start=False, stop=True)
                nc.tensor.matmul(k.ps[4][:, 0:E], k.c("ones"), pre[:, NT - 1, :], start=True, stop=False)
                nc.tensor.matmul(k.ps[4][:, 0:E], k.c("ones"), asg[:, NT - 1, :], start=False, stop=True).then_inc(s["rank"], 1)

            @block.scalar
            def _(act):
                act.wait_ge(s["ltmm"], 1)
                act.activation(lt[:], k.ps[5][0:n_logits, :], ACT.Copy).then_inc(s["lt"], 1)
                for n in range(2 * NT):
                    i, half = divmod(n, 2)
                    act.wait_ge(s["tmm"], n + 1)
                    act.activation(htok[:, i, half * 512:(half + 1) * 512], k.ps[2 + n % 2][:, :], ACT.Copy).then_inc(s["tsb"], 1)
                if hier:
                    act.wait_ge(s["gexp_in"], 1)
                    act.activation(gl[:], gl[:], ACT.Exp).then_inc(s["gexp"], 1)
                act.wait_ge(s["exp_in"], 1)
                act.activation(m[:], m[:], ACT.Exp).then_inc(s["exp"], 1)

            @block.vector
            def _(dve):
                def run(i):
                    dve.drain()
                    return i

                def first_max(x, rev, mx, eqt, kt, keyt, n):
                    dve.tensor_reduce(mx, x, AX.X, ALU.max)
                    dve.drain()
                    dve.tensor_tensor(eqt, x, bc(mx, n), ALU.is_equal)
                    dve.drain()
                    dve.tensor_tensor(keyt, eqt, bm(rev, NT), ALU.mult)
                    dve.drain()
                    dve.tensor_reduce(kt, keyt, AX.X, ALU.max)
                    dve.drain()

                dve.memset(zero[:], 0.0)
                dve.wait_ge(s["lmm"], 1)
                lgp = k.ps[0][:, 0:256].rearrange("p (i n) -> p i n", i=NT)[:, :, 0:n_logits]
                run(dve.tensor_tensor(lg[:], lgp, bm(b_row, NT), ALU.add))
                if hier:
                    first_max(lg[:, :, 0:4], k.c("rev4"), gm[:], geq[:], gk[:], gl[:], 4)
                    dve.tensor_tensor(geq[:], gl[:], bc(gk[:], 4), ALU.is_equal)
                    dve.drain()
                    run(dve.tensor_tensor(gl[:], lg[:, :, 0:4], bc(gm[:], 4), ALU.subtract).then_inc(s["gexp_in"], 1))
                    dve.wait_ge(s["gexp"], 1)
                    run(dve.tensor_reduce(pg[:], gl[:], AX.X, ALU.add))
                    run(dve.reciprocal(pg[:], pg[:]))
                    run(dve.tensor_scalar(geq[:], geq[:], BIG, -BIG, ALU.mult, ALU.add))
                    for gi in range(4):
                        dve.tensor_tensor(lm[:, :, 8 * gi:8 * gi + 8], lg[:, :, 4 + 8 * gi:12 + 8 * gi], bc(geq[:, :, gi], 8), ALU.add)
                else:
                    dve.tensor_copy(lm[:], lg[:])
                dve.drain()
                for n in range(top):
                    first_max(lm[:], k.c("rev"), m[:, n, :], eq[:], mk[:], key[:], E)
                    run(dve.tensor_tensor(oh[:, n], key[:], bc(mk[:], E), ALU.is_equal))
                    run(dve.scalar_tensor_tensor(lm[:], oh[:, n], -3.0 * BIG, lm[:], ALU.mult, ALU.add))
                run(dve.tensor_tensor(asg[:], oh[:, 0], oh[:, 1], ALU.add))
                for n in range(2, top):
                    run(dve.tensor_tensor(asg[:], asg[:], oh[:, n], ALU.add))
                dve.memset(pre[:, 0, :], 0.0)
                dve.drain()
                for i in range(1, NT):
                    last = dve.tensor_tensor(pre[:, i, :], pre[:, i - 1, :], asg[:, i - 1, :], ALU.add)
                    if i == NT - 1:
                        last.then_inc(s["asg"], 1)
                    dve.drain()
                for n in range(top - 1, -1, -1):
                    dve.tensor_tensor(m[:, n, :], m[:, n, :], m[:, 0, :], ALU.subtract) if n else dve.memset(m[:, 0, :], 0.0)
                    dve.drain()
                dve.tensor_copy(zero[:, 0:1], zero[:, 1:2]).then_inc(s["exp_in"], 1)
                dve.wait_ge(s["exp"], 1)
                run(dve.tensor_reduce(mk[:], m[:].rearrange("p n i -> p i n"), AX.X, ALU.add))
                run(dve.reciprocal(mk[:], mk[:]))
                if hier:
                    run(dve.tensor_tensor(mk[:], mk[:], pg[:], ALU.mult))
                dve.tensor_tensor(t["wts"][:, 0:top, :], m[:], bm(mk[:], top), ALU.mult)
                dve.wait_ge(s["rank"], 1)
                run(dve.tensor_copy(cnt[:], k.ps[4][:, 0:E]))
                run(dve.tensor_tensor(blk[:], bm(cnt[:], 4), bc(k.c("thresh"), E), ALU.is_gt))
                run(dve.tensor_reduce(cnt[:], blk[:].rearrange("p j e -> p e j"), AX.X, ALU.add))
                dve.tensor_tensor_scan(tot[:], cnt[:], zero[:], 0.0, ALU.add, ALU.add)
                dve.drain()
                run(dve.tensor_tensor(beg[:], tot[:], cnt[:], ALU.subtract))
                run(dve.scalar_tensor_tensor(pos[:], bm(beg[:], NT), float(P), k.ps[1][:, 0:NT * E].rearrange("p (i e) -> p i e", i=NT), ALU.mult, ALU.add))
                for n in range(top):
                    run(dve.tensor_tensor(key[:], oh[:, n], pos[:], ALU.mult))
                    run(dve.tensor_reduce(sl[:, n, :], key[:], AX.X, ALU.add))
                dve.tensor_copy(t["slots"][:, 0:top, :], sl[:]).then_inc(s["slots"], 1)
                run(dve.tensor_tensor(cmp_[:], bm(tot[:], 64), bc(k.c("slot"), E), ALU.is_le))
                run(dve.tensor_reduce(tabf[:], cmp_[:], AX.X, ALU.add))
                run(dve.tensor_scalar(tabf[:], tabf[:], float(E - 1), None, ALU.min))
                dve.tensor_copy(t["table"][:, 0:64], tabf[:])
                dve.tensor_scalar(cnt[:, 0:1], tot[:, E - 1:E], -1.0, None, ALU.add)
                dve.tensor_scalar(cnt[:, 2:3], tot[:, E - 1:E], -2.0, None, ALU.add)
                dve.tensor_scalar(cnt[:, 1:2], tot[:, E - 1:E], 0.5, -0.25, ALU.mult, ALU.add)
                dve.drain()
                run(dve.tensor_scalar(cnt[:, 1:2], cnt[:, 1:2], MAGIC, None, ALU.add))
                run(dve.tensor_scalar(cnt[:, 1:2], cnt[:, 1:2], -MAGIC, None, ALU.add))
                dve.tensor_copy(t["table"][:, 64:67], cnt[:, 0:3])

            @block.gpsimd
            def _(pool):
                pool.wait_ge(s["slots"], 1)
                pool.wait_ge(s["tsb"], 2 * NT)
                pool.wait_ge(k.cleared, 16)
                for n in range(top):
                    for i in range(NT):
                        pool.indirect_dma_start(out=k.a["xs"], out_offset=bass.IndirectOffsetOnAxis(ap=t["slots"][:, n, i:i + 1], axis=0),
                                                in_=htok[:, i, :], in_offset=None).then_inc(s["sent"], 16)
                pool.wait_ge(s["sent"], 16 * top * NT)
    k.end()


def expert_phase(k, name, t, up, down, bias, ff, sets, extra_slots):
    nc = k.nc
    NJ = up.shape[0] // E
    ND = down.shape[0] // E
    NW = NJ + ND
    FK = ff // P
    PER = FK // NJ
    with ExitStack() as mem:
        sb = lambda n, s, d=F32: mem.enter_context(nc.sbuf_tensor(f"{name}_{n}", s, d))
        extra = sb("extra", [P, extra_slots, PIECE]) if extra_slots else None
        slot = lambda n: k.ring[:, n, :] if n < RING else extra[:, n - RING, :]
        buf = lambda v, j: slot(v * NW + j)
        xg, xt = sb("xg", [P, sets, D]), sb("xt", [P, KT, P])
        hb, u1, sg = sb("hb", [P, 2, 512]), sb("u1", [P, 2, 256]), sb("sg", [P, 2, 256])
        av, at, y = sb("av", [P, ff]), sb("at", [P, FK, P]), sb("y", [P, D])
        bb = sb("bb", [P, 2 * ff + D]) if bias is not None else None
        sign = sb("sign", [P, 2])
        names = ("h_mm", "h_free", "g_min", "sig", "a_out", "xt_mm", "xt_sb", "at_mm", "at_sb", "y_mm", "y_sb", "y_out", "b1_in", "b2_in")
        s = {n: k.sem(f"{name}_{n}") for n in names}
        x_in = [k.sem(f"{name}_x{v}_in") for v in range(sets)]
        w_in = [[k.sem(f"{name}_w{v}_{j}_in") for j in range(NW)] for v in range(sets)]
        turns = lambda eng: eng.value_load(t["table"][0:1, 63 + sets:64 + sets], min_val=3, max_val=(MAXB - 1) // sets)
        expert = lambda eng, b: eng.value_load(t["table"][0:1, bass.ds(b, 1)], min_val=0, max_val=E - 1)
        ncp = (FK + 3) // 4
        with nc.Block() as block:
            @block.sync
            def _(sp):
                n = turns(sp)

                def load(e, v, j):
                    if j < NJ:
                        src = up[bass.ds(e * NJ + j, 1), :, :]
                    else:
                        src = down[bass.ds(e * ND + (j - NJ), 1), :, :]
                    w = src.shape[-1]
                    sp.dma_start(buf(v, j)[:, 0:w], src.rearrange("a p n -> p (a n)")).then_inc(w_in[v][j], 16)

                def load_bias(e, lo, hi, sem):
                    sp.dma_start(bb[:, lo:hi], bias[bass.ds(e, 1), lo:hi].to_broadcast([P, hi - lo])).then_inc(sem, 16)

                def load_up(b, v, wait=True):
                    e = expert(sp, b)
                    for j in range(NJ):
                        if wait:
                            sp.wait_ge(s["h_mm"], b * NJ + (j + 1 - sets * NJ))
                        load(e, v, j)
                    if bb is not None:
                        if wait:
                            sp.wait_ge(s["h_free"], b * NJ)
                        load_bias(e, 0, 2 * ff, s["b1_in"])

                def load_down(b, v, wait=True):
                    e = expert(sp, b)
                    for j in range(ND):
                        if wait:
                            sp.wait_ge(s["y_mm"], b * 2 + ((j + 1 if ND == 2 else 2) - 2 * sets))
                        load(e, v, NJ + j)
                    if bb is not None:
                        if wait:
                            sp.wait_ge(s["y_sb"], b + 1)
                        load_bias(e, 2 * ff, 2 * ff + D, s["b2_in"])

                for b in range(sets):
                    load_up(b, b, wait=False)
                    load_down(b, b, wait=False)
                if sets == 1:
                    load_up(1, 0)
                    short = sp.value_load(t["table"][0:1, 66:67], min_val=2, max_val=MAXB - 2)
                    with sp.Fori(0, short) as i:
                        load_up(i + 2, 0)
                        load_down(i + 1, 0)
                    load_down(short + 1, 0)
                else:
                    with sp.Fori(0, n) as i:
                        for v in range(sets):
                            load_up(i * sets + (v + sets), v)
                            load_down(i * sets + (v + sets), v)

            @block.gpsimd
            def _(pool):
                n = turns(pool)
                rows = lambda b: k.a["xs"][bass.ds(b * P, P), :]
                for b in range(sets):
                    pool.dma_start(xg[:, b, :], rows(b)).then_inc(x_in[b], 16)
                pool.dma_start(y[:], k.a["xs"][0:P, :]).then_inc(s["y_out"], 16)
                pool.wait_ge(s["xt_mm"], 2)
                pool.dma_start(xg[:, 0, :], rows(sets)).then_inc(x_in[0], 16)

                def store(b):
                    pool.wait_ge(s["y_sb"], b + 2)
                    pool.dma_start(rows(b), y[:]).then_inc(s["y_out"], 16)

                with pool.Fori(0, n) as i:
                    for v in range(sets):
                        b = i * sets + (v + 1)
                        pool.wait_ge(s["xt_mm"], b * 2 + 2)
                        pool.dma_start(xg[:, (v + 1) % sets, :], rows(b + sets)).then_inc(x_in[(v + 1) % sets], 16)
                        store(b - 1)
                store(n * sets)
                for v in range(sets):
                    for j in range(NW):
                        pool.wait_ge(w_in[v][j], n * 16 + 16)
                for v in range(sets):
                    pool.wait_ge(x_in[v], n * 16 + (32 if v == 0 else 16))
                pool.wait_ge(s["y_out"], n * (16 * sets) + 32)

            @block.tensor
            def _(pe):
                n = turns(pe)

                def transpose_x(v, use):
                    pe.wait_ge(x_in[v], use * 16 + 16)
                    for half in range(2):
                        for j in range(4):
                            kk = 4 * half + j
                            last = nc.tensor.transpose(k.ps[2 + half][:, j * P:(j + 1) * P], xg[:, v, kk * P:(kk + 1) * P], k.c("ident"))
                        last.then_inc(s["xt_mm"], 1)

                def up_products(b, v, use, first=False):
                    pe.wait_ge(s["xt_sb"], b * 2 + 2)
                    for j in range(NJ):
                        pe.wait_ge(w_in[v][j], use * 16 + 16)
                        if not first:
                            pe.wait_ge(s["h_free"], b * NJ + (j + 1 - NJ))
                        w = buf(v, j).rearrange("p (k n) -> p k n", k=KT)
                        for kk in range(KT):
                            last = nc.tensor.matmul(k.ps[j][:, :], xt[:, kk, :], w[:, kk, :], start=kk == 0, stop=kk == KT - 1)
                        last.then_inc(s["h_mm"], 1)

                def transpose_a(b):
                    for j in range(NJ):
                        pe.wait_ge(s["a_out"], b * NJ + (j + 1))
                        for i in range(PER):
                            f = j * PER + i
                            last = nc.tensor.transpose(k.ps[6 + f // 4][:, (f % 4) * P:(f % 4 + 1) * P], av[:, f * P:(f + 1) * P], k.c("ident"))
                            if f % 4 == 3 or f == FK - 1:
                                last.then_inc(s["at_mm"], 1)

                def down_product(b, v, use):
                    pe.wait_ge(s["at_sb"], b * ncp + ncp)
                    pe.wait_ge(s["y_sb"], b + 1)
                    for h in range(2):
                        if h < ND:
                            pe.wait_ge(w_in[v][NJ + h], use * 16 + 16)
                        w = buf(v, NJ + min(h, ND - 1))[:, 0:FK * (512 if ND == 2 else D)].rearrange("p (k n) -> p k n", k=FK)
                        for kk in range(FK):
                            rhs = w[:, kk, :] if ND == 2 else w[:, kk, h * 512:(h + 1) * 512]
                            last = nc.tensor.matmul(k.ps[4 + h][:, :], at[:, kk, :], rhs, start=kk == 0, stop=kk == FK - 1)
                        last.then_inc(s["y_mm"], 1)

                transpose_x(0, 0)
                up_products(0, 0, 0, first=True)
                pe.wait_ge(s["h_free"], NJ)
                transpose_x(1 % sets, 1 // sets)
                transpose_a(0)
                with pe.Fori(0, n) as i:
                    for v in range(sets):
                        b = i * sets + (v + 1)
                        up_products(b, (v + 1) % sets, i + (v + 1) // sets)
                        if NJ <= 2:
                            transpose_x((v + 2) % sets, i + (v + 2) // sets)
                        down_product(b - 1, v, i)
                        if NJ > 2:
                            pe.wait_ge(s["h_free"], b * NJ + NJ)
                            transpose_x((v + 2) % sets, i + (v + 2) // sets)
                        transpose_a(b)
                down_product(n * sets, 0, n)

            @block.scalar
            def _(act):
                n = turns(act)

                def copy_x(b):
                    act.wait_ge(s["xt_mm"], b * 2 + 2)
                    for half in range(2):
                        act.activation(xt[:, 4 * half:4 * half + 4, :], g4(k.ps[2 + half][:, :]), ACT.Copy).then_inc(s["xt_sb"], 1)

                def block_work(b):
                    for j in range(NJ):
                        act.wait_ge(s["g_min"], b * NJ + (j + 1))
                        if bb is None:
                            act.activation(sg[:, j % 2, :], k.ps[j][:, 0:256], ACT.Silu).then_inc(s["sig"], 1)
                        else:
                            act.activation(sg[:, j % 2, :], hb[:, j % 2, 0:256], ACT.Sigmoid, scale=ALPHA).then_inc(s["sig"], 1)
                    copy_x(b + 1)
                    for c in range(ncp):
                        act.wait_ge(s["at_mm"], b * ncp + (c + 1))
                        w = min(4, FK - 4 * c)
                        act.activation(at[:, 4 * c:4 * c + w, :], g4(k.ps[6 + c][:, 0:w * P], w), ACT.Copy).then_inc(s["at_sb"], 1)

                copy_x(0)
                block_work(0)
                with act.Fori(0, n) as i:
                    for v in range(sets):
                        block_work(i * sets + (v + 1))

            @block.vector
            def _(dve):
                n = turns(dve)

                def activate(b):
                    if bb is not None:
                        dve.wait_ge(s["b1_in"], b * 16 + 16)
                    for j in range(NJ):
                        h, u, g = hb[:, j % 2, :], u1[:, j % 2, :], sg[:, j % 2, :]
                        a = av[:, j * 256:(j + 1) * 256]
                        dve.wait_ge(s["h_mm"], b * NJ + (j + 1))
                        if bb is None:
                            dve.tensor_copy(u, k.ps[j][:, 256:512]).then_inc(s["g_min"], 1)
                            dve.wait_ge(s["sig"], b * NJ + (j + 1))
                            dve.tensor_tensor(a, g, u, ALU.mult).then_inc(s["a_out"], 1)
                            dve.memset(sign[:, 0:1], 0.0).then_inc(s["h_free"], 1)
                        else:
                            dve.tensor_tensor(h, k.ps[j][:, :], bb[:, j * 512:(j + 1) * 512], ALU.add).then_inc(s["h_free"], 1)
                            dve.drain()
                            dve.tensor_scalar(h[:, 0:256], h[:, 0:256], LIMIT, None, ALU.min).then_inc(s["g_min"], 1)
                            dve.tensor_scalar(u, h[:, 256:512], LIMIT, -LIMIT, ALU.min, ALU.max)
                            dve.drain()
                            dve.scalar_tensor_tensor(u, u, 1.0, h[:, 0:256], ALU.add, ALU.mult)
                            dve.drain()
                            dve.wait_ge(s["sig"], b * NJ + (j + 1))
                            dve.tensor_tensor(a, u, g, ALU.mult).then_inc(s["a_out"], 1)

                def rows_out(b):
                    if bb is not None:
                        dve.wait_ge(s["b2_in"], b * 16 + 16)
                    dve.wait_ge(s["y_out"], b * 16 + 16)
                    for h in range(2):
                        dve.wait_ge(s["y_mm"], b * 2 + (h + 1))
                        o = y[:, h * 512:(h + 1) * 512]
                        if bb is None:
                            last = dve.tensor_copy(o, k.ps[4 + h][:, :])
                        else:
                            last = dve.tensor_tensor(o, k.ps[4 + h][:, :], bb[:, 2 * ff + h * 512:2 * ff + (h + 1) * 512], ALU.add)
                    last.then_inc(s["y_sb"], 1)

                dve.memset(sign[:, 1:2], 0.0).then_inc(s["y_sb"], 1)
                activate(0)
                with dve.Fori(0, n) as i:
                    for v in range(sets):
                        activate(i * sets + (v + 1))
                        rows_out(i * sets + v)
                rows_out(n * sets)
    k.end()


def combine_phase(k, name, t, top, gate, keep):
    nc = k.nc
    units = [(i, n) for i in range(NT) for n in range(top)]
    with ExitStack() as mem:
        sb = lambda n, s, d=F32: mem.enter_context(nc.sbuf_tensor(f"{name}_{n}", s, d))
        yb, acc = sb("yb", [P, 4, D]), sb("acc", [P, 2, D])
        got = [k.sem(f"{name}_got{i}") for i in range(4)]
        s_used, s_acc, s_mm, s_sb = (k.sem(f"{name}_{n}") for n in ("used", "acc", "mm", "sb"))
        with nc.Block() as block:
            @block.sync
            def _(sp):
                if keep:
                    sp.wait_ge(s_used, len(units) - 4)
                    k.send_pieces(sp, keep)

            @block.gpsimd
            def _(pool):
                for u, (i, n) in enumerate(units):
                    if u >= 4:
                        pool.wait_ge(s_used, u - 3)
                    pool.indirect_dma_start(out=yb[:, u % 4, :], out_offset=None, in_=k.a["xs"],
                                            in_offset=bass.IndirectOffsetOnAxis(ap=t["slots"][:, n, i:i + 1], axis=0)).then_inc(got[u % 4], 16)

            @block.vector
            def _(dve):
                def add_x(i):
                    for half in range(2):
                        dve.wait_ge(s_mm, 2 * i + half + 1)
                        for j in range(4):
                            kk = 4 * half + j
                            x = k.xT[:, kk, i * P:(i + 1) * P]
                            last = dve.scalar_tensor_tensor(x, k.ps[2 * (i % 2) + half][:, j * P:(j + 1) * P], gate(kk), x, ALU.mult, ALU.add)
                        last.then_inc(s_sb, 1)

                for u, (i, n) in enumerate(units):
                    dve.wait_ge(got[u % 4], 16 * (u // 4 + 1))
                    w = t["wts"][:, n, i:i + 1]
                    if n == 0:
                        if i >= 2:
                            dve.wait_ge(s_mm, 2 * (i - 1))
                        dve.tensor_scalar(acc[:, i % 2, :], yb[:, u % 4, :], w, None, ALU.mult).then_inc(s_used, 1)
                    else:
                        dve.drain()
                        dve.scalar_tensor_tensor(acc[:, i % 2, :], yb[:, u % 4, :], w, acc[:, i % 2, :], ALU.mult, ALU.add).then_inc(s_used, 1)
                    if n == top - 1 and i >= 1:
                        add_x(i - 1)
                add_x(NT - 1)

            @block.tensor
            def _(pe):
                for i in range(NT):
                    pe.wait_ge(s_used, (i + 1) * top)
                    for half in range(2):
                        if i >= 2:
                            pe.wait_ge(s_sb, 2 * (i - 2) + half + 1)
                        for j in range(4):
                            kk = 4 * half + j
                            last = nc.tensor.transpose(k.ps[2 * (i % 2) + half][:, j * P:(j + 1) * P], acc[:, i % 2, kk * P:(kk + 1) * P], k.c("ident"))
                        last.then_inc(s_mm, 1)
    k.end()


def project2_phase(k, t, hc, first):
    nc = k.nc
    NX = 16
    with ExitStack() as mem:
        cv = mem.enter_context(nc.sbuf_tensor("p2_cv", [P, 2, T + CTX], F32))
        s_mm, s_cv, s_silu, s_dt = (k.sem(f"p2_{n}") for n in ("mm", "conv", "silu", "dt"))
        with nc.Block() as block:
            @block.sync
            def _(sp):
                k.send_pieces(sp, first + 6)

            @block.tensor
            def _(pe):
                for m in range(CONV_T):
                    if m >= 2:
                        pe.wait_ge(s_cv, m - 1)
                    w = k.piece(pe, first + m // 4)
                    c0 = (m % 4) * P
                    main, ctx_ = k.ps[2 * (m % 2)], k.ps[2 * (m % 2) + 1]
                    for kk in range(KT):
                        last = nc.tensor.matmul(main[:, :], w[:, kk, c0:c0 + P], k.hT[:, kk, :], start=kk == 0, stop=kk == KT - 1)
                    if m < NX:
                        for kk in range(KT):
                            last = nc.tensor.matmul(ctx_[:, 0:CTX], w[:, kk, c0:c0 + P], hc[:, kk, :], start=kk == 0, stop=kk == KT - 1)
                    last.then_inc(s_mm, 1)
                    if m % 4 == 3:
                        k.piece_done()
                w = k.piece(pe, first + 5)
                for i in range(NT + NC_):
                    h = k.hT[:, :, i * P:(i + 1) * P] if i < NT else hc[:, :, (i - NT) * P:(i - NT + 1) * P]
                    for kk in range(KT):
                        last = nc.tensor.matmul(k.ps[4][:, i * DT_C:(i + 1) * DT_C], h[:, kk, :], w[:, kk, :], start=kk == 0, stop=kk == KT - 1)
                last.then_inc(s_dt, 1)
                k.piece_done()

            @block.vector
            def _(dve):
                for m in range(CONV_T):
                    dve.wait_ge(s_mm, m + 1)
                    if m >= 2:
                        dve.wait_ge(s_silu, m - 1)
                    w = lambda j: k.v("conv2", 5 * m + j, 5 * m + j + 1)
                    parts = [(k.ps[2 * (m % 2)], 0, T)] + ([(k.ps[2 * (m % 2) + 1], T, CTX)] if m < NX else [])
                    for x, at, n in parts:
                        dve.tensor_scalar(cv[:, m % 2, at:at + n], x[:, 0:n], w(2), None, ALU.mult)
                    for j in (0, 1, 3, 4):
                        dve.drain()
                        d = j - 2
                        lo, hi = max(0, -d), max(0, d)
                        for x, at, n in parts:
                            y = cv[:, m % 2, at + lo:at + n - hi]
                            last = dve.scalar_tensor_tensor(y, x[:, lo + d:n - hi + d], w(j), y, ALU.mult, ALU.add)
                    last.then_inc(s_cv, 1)
                dve.wait_ge(s_dt, 1)
                dve.tensor_copy(t["dt"][:].rearrange("p i c -> p (i c)"), k.ps[4][:, 0:(NT + NC_) * DT_C])

            @block.scalar
            def _(act):
                for m in range(CONV_T):
                    act.wait_ge(s_cv, m + 1)
                    dst = t["mix"][:, m, :] if m < XT else t["bc"][:, m - XT, :]
                    b = k.v("convb2", m, m + 1)
                    last = act.activation(dst, cv[:, m % 2, 0:T], ACT.Silu, bias=b)
                    if m < NX:
                        last = act.activation(t["xc"][:, m, :], cv[:, m % 2, T:T + CTX], ACT.Silu, bias=b)
                    last.then_inc(s_silu, 1)
    k.end()


def ssd_prepare_phase(k, t):
    nc = k.nc
    NTT = NT + NC_
    W = NTT * DT_C
    with ExitStack() as mem:
        sb = lambda n, s, d=F32: mem.enter_context(nc.sbuf_tensor(f"q_{n}", s, d))
        tmp, tmp2, aexp = sb("tmp", [P, NTT, DT_C]), sb("tmp2", [P, NTT, DT_C]), sb("aexp", [P, DT_C])
        names = ("e_in", "e1", "e2", "a", "cum", "ecum", "coef", "tmm", "tsb", "xw", "smm", "ssb", "spill", "skip")
        s = {n: k.sem(f"q_{n}") for n in names}
        main = [("m", i, j) for i in range(NT) for j in range(4)]
        ctx_ = [("c", i, j) for i in range(NC_) for j in range(4)]
        jobs = ctx_ + main
        ring = k.ring[:].rearrange("p r n -> p (r n)")
        ctok = ring[:, 4096:8192].rearrange("p (i n) -> p i n", i=NC_)
        xw = ring[:, 8192:8192 + 4 * SSD_W].rearrange("p (n c) -> p n c", n=4)
        with nc.Block() as block:
            @block.sync
            def _(sp):
                sp.dma_start(k.a["spill_h"], k.hT[:]).then_inc(s["spill"], 16)
                sp.wait_ge(s["spill"], 16)

            @block.scalar
            def _(act):
                act.wait_ge(s["e_in"], 1)
                act.activation(tmp[:], tmp[:], ACT.Exp)
                act.activation(aexp[:], k.r("a_log2"), ACT.Exp).then_inc(s["e1"], 1)
                act.drain()
                act.activation(tmp[:], tmp[:], ACT.Ln, bias=k.c("one")).then_inc(s["e2"], 1)
                act.wait_ge(s["cum"], 1)
                for d, b in ((0, 0), (1, 1)):
                    src = k.ps[b][:, 0:W].rearrange("p (i d h) -> p i d h", i=NTT, d=2)[:, :, d, :]
                    act.activation(t["coef"][:, :, d, :], src, ACT.Exp)
                act.activation(t["etot"][:].rearrange("p i d h -> p (i d h)"), k.ps[2][:, 0:W], ACT.Exp).then_inc(s["ecum"], 1)
                for n, (kind, i, j) in enumerate(jobs):
                    act.wait_ge(s["tmm"], n + 1)
                    if kind == "c":
                        dst = ctok[:, i, j * 512:(j + 1) * 512]
                    elif j < 3:
                        dst = t["xtok"][:, i, j * 512:(j + 1) * 512]
                    else:
                        dst = t["btok"][:, i, :]
                    act.activation(dst, k.ps[3 + n % 2][:, :], ACT.Copy).then_inc(s["tsb"], 1)
                for n in range(2 * SSD_G):
                    d, g = divmod(n, SSD_G)
                    act.wait_ge(s["smm"], n + 1)
                    act.activation(t["state"][:, d, g * 384:(g + 1) * 384], k.ps[5 + n % 2][:, 0:384], ACT.Copy).then_inc(s["ssb"], 1)

            @block.vector
            def _(dve):
                dt, a = t["dt"], t["a"]
                dve.tensor_tensor(dt[:], dt[:], bm(k.r("dt_bias2"), NTT), ALU.add)
                dve.drain()
                dve.tensor_scalar(tmp2[:], dt[:], -1.0, None, ALU.mult)
                dve.drain()
                dve.tensor_tensor(tmp[:], dt[:], tmp2[:], ALU.min).then_inc(s["e_in"], 1)
                dve.wait_ge(s["e2"], 1)
                dve.scalar_tensor_tensor(dt[:], dt[:], 0.0, tmp[:], ALU.max, ALU.add)
                dve.tensor_scalar(aexp[:], aexp[:], -1.0, None, ALU.mult)
                dve.drain()
                dve.tensor_tensor(a[:], dt[:], bm(aexp[:], NTT), ALU.mult).then_inc(s["a"], 1)
                dve.wait_ge(s["ecum"], 1)
                dve.tensor_tensor(t["coef"][:].rearrange("p i d h -> p i (d h)"), t["coef"][:].rearrange("p i d h -> p i (d h)"), dt[:], ALU.mult).then_inc(s["coef"], 1)
                dve.drain()
                for n in range(2 * NC_):
                    d, i = divmod(n, NC_)
                    dve.wait_ge(s["tsb"], 4 * NC_)
                    dve.tensor_tensor(xw[:, n, :].rearrange("p (h e) -> p h e", h=SSD_H), ctok[:, i, 0:SSD_W].rearrange("p (h e) -> p h e", h=SSD_H),
                                      bc(t["coef"][:, NT + i, d, :], HD), ALU.mult).then_inc(s["xw"], 1)
                dve.wait_ge(s["tmm"], len(jobs))
                for m in range(XT):
                    dve.tensor_scalar(t["mix"][:, m, :], t["mix"][:, m, :], k.v("skip", m, m + 1), None, ALU.mult)

            @block.tensor
            def _(pe):
                pe.wait_ge(s["a"], 1)
                fl = t["a"][:].rearrange("p i c -> p (i c)")
                c0, c1 = NT * DT_C, (NT + 1) * DT_C
                nc.tensor.matmul(k.ps[0][:, 0:W], k.c("gt"), fl, start=True, stop=False)
                nc.tensor.matmul(k.ps[0][:, c0:c1], k.c("ones"), t["a"][:, NT + 1, :], start=False, stop=True)
                nc.tensor.matmul(k.ps[1][:, 0:W], k.c("lt"), fl, start=True, stop=False)
                nc.tensor.matmul(k.ps[1][:, c1:W], k.c("ones"), t["a"][:, NT, :], start=False, stop=True)
                nc.tensor.matmul(k.ps[2][:, 0:W], k.c("ones"), fl, start=True, stop=True).then_inc(s["cum"], 1)
                for n, (kind, i, j) in enumerate(jobs):
                    if n >= 2:
                        pe.wait_ge(s["tsb"], n - 1)
                    for q in range(4):
                        m = 4 * j + q
                        if kind == "c":
                            src = t["xc"][:, m, i * P:(i + 1) * P]
                        else:
                            src = (t["mix"][:, m, :] if m < XT else t["bc"][:, m - XT, :])[:, i * P:(i + 1) * P]
                        last = nc.tensor.transpose(k.ps[3 + n % 2][:, q * P:(q + 1) * P], src, k.c("ident"))
                    last.then_inc(s["tmm"], 1)
                for n in range(2 * SSD_G):
                    d, g = divmod(n, SSD_G)
                    if n >= 2:
                        pe.wait_ge(s["ssb"], n - 1)
                    pe.wait_ge(s["xw"], NC_ * (d + 1))
                    for i in range(NC_):
                        last = nc.tensor.matmul(k.ps[5 + n % 2][:, 0:384], ctok[:, i, (XT + g) * P:(XT + g + 1) * P], xw[:, d * NC_ + i, g * 384:(g + 1) * 384],
                                                start=i == 0, stop=i == NC_ - 1)
                    last.then_inc(s["smm"], 1)
    k.end()


def ssd_scan_phase(k, t, first):
    nc = k.nc
    TF = k.hT[:].rearrange("p k n -> p (k n)")
    TX = k.xT[:].rearrange("p k n -> p (k n)")
    R6 = lambda ap: ap.rearrange("p (h n) -> p h n", h=HPG)
    R3 = lambda ap: ap.rearrange("p (m n) -> p m n", m=3)
    TR = k.ring[:, 1, :]
    gf, gb = (R6(TF[:, 0:768]), R6(TR[:, 0:768])), (R6(TF[:, 768:1536]), R6(TR[:, 768:1536]))
    ew, dl = (R6(TF[:, 1536:2304]), R6(TX[:, 2048:2816])), (R6(TF[:, 2304:3072]), R6(TX[:, 2816:3584]))
    eg = (R3(TF[:, 3072:3456]), R3(TX[:, 3584:3968]))
    xw = TX[:, 0:SSD_W]
    cb = (TX[:, 1536:1664], TX[:, 3968:4096])
    tmp = R3(TX[:, 1664:2048])
    fwd = [("f", c, g) for c in range(NT) for g in range(SSD_G)]
    bwd = [("b", c, g) for c in reversed(range(NT)) for g in range(SSD_G)]
    units = fwd + bwd
    NF = len(fwd)
    off_banks = lambda u: (k.ps[0], k.ps[1]) if u >= NF and u % 2 else (k.ps[4], k.ps[5])
    names = ("gf", "gb", "pmm", "e", "cb", "w", "ymm", "omm", "eg", "y", "off", "xw", "smm", "ssb", "dl")
    s = {n: k.sem(f"r_{n}") for n in names}
    assert first % RING == 2
    with nc.Block() as block:
        @block.sync
        def _(sp):
            k.send_pieces(sp, first + 2)

        @block.gpsimd
        def _(pool):
            for u, (kind, c, g) in enumerate(units):
                d = 0 if kind == "f" else 1
                if kind == "f":
                    if u >= 2:
                        pool.wait_ge(s["pmm"], u - 1)
                    for h in range(HPG):
                        hh = SSD_H + g * HPG + h
                        last = pool.tensor_scalar(gb[u % 2][:, h, :], k.c("ge"), t["a"][:, c, hh:hh + 1], None, ALU.mult)
                    last.then_inc(s["gb"], 1)
                if u >= SSD_G:
                    pool.wait_ge(s["smm"], u - SSD_G + 1)
                hs = slice(g * HPG, (g + 1) * HPG)
                pool.tensor_tensor(xw.rearrange("p (h e) -> p h e", h=SSD_H)[:, hs], t["xtok"][:, c, :].rearrange("p (h e) -> p h e", h=SSD_H)[:, hs],
                                   bc(t["coef"][:, c, d, hs], HD), ALU.mult).then_inc(s["xw"], 1)

        @block.tensor
        def _(pe):
            def decay_sums(u):
                _, c, g = units[u]
                tok = slice(c * P, (c + 1) * P)
                pe.wait_ge(s["gf"], u + 1)
                pe.wait_ge(s["gb"], u + 1)
                if u >= 1:
                    pe.wait_ge(s["e"], u)
                for half in range(2):
                    hs = slice(3 * half, 3 * half + 3)
                    nc.tensor.matmul(k.ps[half][:, 0:384], k.c("gt"), gf[u % 2][:, hs, :].rearrange("p h n -> p (h n)"), start=True, stop=False)
                    nc.tensor.matmul(k.ps[half][:, 0:384], k.c("lt"), gb[u % 2][:, hs, :].rearrange("p h n -> p (h n)"), start=False, stop=True)
                if u >= 1:
                    pe.wait_ge(s["cb"], u)
                nc.tensor.matmul(k.ps[2][:, 0:P], t["bc"][:, g, tok], t["bc"][:, SSD_G + g, tok], start=True, stop=True).then_inc(s["pmm"], 1)

            def state_part(u):
                kind, c, g = units[u]
                d = 0 if kind == "f" else 1
                C = t["bc"][:, SSD_G + g, c * P:(c + 1) * P]
                sums, part = off_banks(u)
                if u == NF + 1:
                    pe.wait_ge(s["e"], NF)
                elif u >= 1:
                    back = u if u <= NF else u - 1
                    pe.wait_ge(s["eg"], back)
                    pe.wait_ge(s["off"], back)
                if u >= SSD_G:
                    pe.wait_ge(s["ssb"], u - SSD_G + 1)
                for m in range(3):
                    h0 = g * HPG + 2 * m
                    for half in range(2):
                        lhs = t["a"][:, c, d * SSD_H + h0 + half:d * SSD_H + h0 + half + 1].to_broadcast([P, HD])
                        nc.tensor.matmul(sums[half * HD:(half + 1) * HD, m * P:(m + 1) * P], lhs, k.c("le" if d == 0 else "ge"), start=True, stop=True)
                    last = nc.tensor.matmul(part[:, m * P:(m + 1) * P], t["state"][:, d, g * 384 + m * P:g * 384 + (m + 1) * P], C, start=True, stop=True)
                last.then_inc(s["omm"], 1)

            decay_sums(0)
            state_part(0)
            for u, (kind, c, g) in enumerate(units):
                if u + 1 < NF:
                    decay_sums(u + 1)
                if kind == "b" and u + 1 < len(units):
                    state_part(u + 1)
                if kind == "f":
                    pe.wait_ge(s["w"], u + 1)
                    if u >= 1:
                        pe.wait_ge(s["y"], u)
                    for m in range(3):
                        for half in range(2):
                            h = 2 * m + half
                            last = nc.tensor.matmul(k.ps[3][half * HD:(half + 1) * HD, m * P:(m + 1) * P], t["xtok"][:, c, (g * HPG + h) * HD:(g * HPG + h + 1) * HD],
                                                    ew[u % 2][:, h, :], start=True, stop=True)
                    last.then_inc(s["ymm"], 1)
                pe.wait_ge(s["xw"], u + 1)
                if u >= 2:
                    pe.wait_ge(s["ssb"], u - 1)
                nc.tensor.matmul(k.ps[6 + u % 2][:, 0:384], t["btok"][:, c, g * P:(g + 1) * P], xw[:, g * 384:(g + 1) * 384], start=True, stop=True).then_inc(s["smm"], 1)
                if kind == "f":
                    state_part(u + 1)

        @block.scalar
        def _(act):
            def masks(u):
                _, c, g = units[u]
                if u >= 2:
                    act.wait_ge(s["pmm"], u - 1)
                for h in range(HPG):
                    hh = g * HPG + h
                    last = act.activation(gf[u % 2][:, h, :], k.c("le"), ACT.Copy, scale=t["a"][:, c, hh:hh + 1])
                last.then_inc(s["gf"], 1)
                if u >= 2:
                    act.wait_ge(s["w"], u - 1)
                for h in range(HPG):
                    hh = g * HPG + h
                    last = act.activation(dl[u % 2][:, h, :], k.c("ge"), ACT.Copy, scale=t["dt"][:, c, SSD_H + hh:SSD_H + hh + 1])
                last.then_inc(s["dl"], 1)

            masks(0)
            for u, (kind, c, g) in enumerate(units):
                if kind == "f":
                    act.wait_ge(s["pmm"], u + 1)
                    if u >= 2:
                        act.wait_ge(s["ymm"], u - 1)
                    for half in range(2):
                        last = act.activation(ew[u % 2][:, 3 * half:3 * half + 3, :], k.ps[half][:, 0:384].rearrange("p (h n) -> p h n", h=3), ACT.Exp)
                    last.then_inc(s["e"], 1)
                    act.activation(cb[u % 2], k.ps[2][:, 0:P], ACT.Copy).then_inc(s["cb"], 1)
                    if u + 1 < NF:
                        masks(u + 1)
                act.wait_ge(s["omm"], u + 1)
                if u >= 2:
                    act.wait_ge(s["off"], u - 1)
                act.activation(eg[u % 2], R3(off_banks(u)[0][:, 0:384]), ACT.Exp).then_inc(s["eg"], 1)

        @block.vector
        def _(dve):
            def inside(u):
                _, c, g = units[u]
                y = t["mix"][:, 3 * g:3 * g + 3, c * P:(c + 1) * P]
                dve.wait_ge(s["ymm"], u + 1)
                dve.tensor_tensor(y, y, R3(k.ps[3][:, 0:384]), ALU.add).then_inc(s["y"], 1)

            for u, (kind, c, g) in enumerate(units):
                d = 0 if kind == "f" else 1
                tok = slice(c * P, (c + 1) * P)
                y = t["mix"][:, 3 * g:3 * g + 3, tok]
                S = t["state"][:, d, g * 384:(g + 1) * 384]
                S6 = S.rearrange("p (h e) -> p h e", h=HPG)
                w, weights = dl[u % 2], ew[u % 2]
                if kind == "f":
                    dve.wait_ge(s["dl"], u + 1)
                    for h in range(HPG):
                        hh = g * HPG + h
                        dve.scalar_tensor_tensor(w[:, h, :], k.c("le"), t["dt"][:, c, hh:hh + 1], w[:, h, :], ALU.mult, ALU.add)
                    if u >= 1:
                        inside(u - 1)
                    dve.wait_ge(s["cb"], u + 1)
                    dve.drain()
                    dve.tensor_tensor(w, w, bm(cb[u % 2], HPG), ALU.mult)
                    dve.drain()
                    dve.tensor_tensor(weights, weights, w, ALU.mult).then_inc(s["w"], 1)
                if u == NF:
                    inside(u - 1)
                    dve.drain()
                dve.wait_ge(s["eg"], u + 1)
                dve.tensor_tensor(tmp, R3(off_banks(u)[1][:, 0:384]), eg[u % 2], ALU.mult).then_inc(s["off"], 1)
                dve.tensor_tensor(S6, S6, bc(t["etot"][:, c, d, g * HPG:(g + 1) * HPG], HD), ALU.mult)
                dve.drain()
                dve.tensor_tensor(y, y, tmp, ALU.add)
                dve.wait_ge(s["smm"], u + 1)
                dve.tensor_tensor(S, S, k.ps[6 + u % 2][:, 0:384], ALU.add).then_inc(s["ssb"], 1)
                dve.drain()
    k.end()


def gate2_phase(k, t, first):
    nc = k.nc
    with ExitStack() as mem:
        sb = lambda n, s, d=F32: mem.enter_context(nc.sbuf_tensor(f"z_{n}", s, d))
        zs, sq, r = sb("zs", [P, 2, T]), sb("sq", [P, 2, T]), sb("r", [P, T])
        ut, pw = sb("ut", [P, NT, T]), sb("pw", [P, POOL_G, P])
        pl = sb("pl", [P, 2, T])
        names = ("h", "x", "pw", "mm", "silu", "y", "sq", "ss", "rt", "umm", "usb", "pmm", "psb", "omm", "osb")
        s = {n: k.sem(f"z_{n}") for n in names}
        with nc.Block() as block:
            @block.sync
            def _(sp):
                sp.dma_start(k.hT[:], k.a["spill_h"]).then_inc(s["h"], 16)
                k.send_pieces(sp, first + 3)
                sp.dma_start(k.xT[:], k.a["spill_x"]).then_inc(s["x"], 16)
                sp.dma_start(pw[:], k.a["pool_w"]).then_inc(s["pw"], 16)
                k.send_pieces(sp, first + 4 + RING)
                sp.wait_ge(s["x"], 16)

            @block.tensor
            def _(pe):
                pe.wait_ge(s["h"], 16)
                for m in range(XT):
                    w = k.piece(pe, first + m // 4)
                    if m >= 2:
                        pe.wait_ge(s["silu"], m - 1)
                    for kk in range(KT):
                        last = nc.tensor.matmul(k.ps[m % 2][:, :], w[:, kk, (m % 4) * P:(m % 4 + 1) * P], k.hT[:, kk, :], start=kk == 0, stop=kk == KT - 1)
                    last.then_inc(s["mm"], 1)
                    if m % 4 == 3:
                        k.piece_done()
                    if m >= 1:
                        pe.wait_ge(s["sq"], m)
                        nc.tensor.matmul(k.ps[2][:, :], k.c("ones"), sq[:, (m - 1) % 2, :], start=m == 1, stop=False).then_inc(s["ss"], 1)
                w = k.piece(pe, first + 3)
                for i in range(NT):
                    if i >= 2:
                        pe.wait_ge(s["usb"], i - 1)
                    for kk in range(KT):
                        last = nc.tensor.matmul(k.ps[3 + i % 2][:, :], k.hT[:, kk, i * P:(i + 1) * P], w[:, kk, :], start=kk == 0, stop=kk == KT - 1)
                    last.then_inc(s["umm"], 1)
                    if i == 0:
                        pe.wait_ge(s["sq"], XT)
                        nc.tensor.matmul(k.ps[2][:, :], k.c("ones"), sq[:, (XT - 1) % 2, :], start=False, stop=True).then_inc(s["ss"], 1)
                k.piece_done()
                pe.wait_ge(s["pw"], 16)
                for g in range(POOL_G):
                    pe.wait_ge(s["usb"], NT)
                    if g >= 2:
                        pe.wait_ge(s["psb"], g - 1)
                    for i in range(NT):
                        last = nc.tensor.matmul(k.ps[5 + g % 2][:, i * P:(i + 1) * P], ut[:, i, g * P:(g + 1) * P], k.c("pool", g * P, (g + 1) * P), start=True, stop=True)
                    last.then_inc(s["pmm"], 1)
                    pe.wait_ge(s["psb"], g + 1)
                    if g >= 2:
                        pe.wait_ge(s["osb"], g - 1)
                    nc.tensor.matmul(k.ps[g % 2][:, :], pw[:, g, :], pl[:, g % 2, :], start=True, stop=True).then_inc(s["omm"], 1)

            @block.scalar
            def _(act):
                for m in range(XT):
                    act.wait_ge(s["mm"], m + 1)
                    if m >= 2:
                        act.wait_ge(s["y"], m - 1)
                    act.activation(zs[:, m % 2, :], k.ps[m % 2][:, :], ACT.Silu).then_inc(s["silu"], 1)
                    if m >= 1:
                        act.wait_ge(s["y"], m)
                        if m >= 3:
                            act.wait_ge(s["ss"], m - 2)
                        act.activation(sq[:, (m - 1) % 2, :], t["mix"][:, m - 1, :], ACT.Square).then_inc(s["sq"], 1)
                act.wait_ge(s["y"], XT)
                act.wait_ge(s["ss"], XT - 2)
                act.activation(sq[:, (XT - 1) % 2, :], t["mix"][:, XT - 1, :], ACT.Square).then_inc(s["sq"], 1)
                act.wait_ge(s["ss"], XT)
                act.activation(r[:], k.ps[2][:, :], ACT.Sqrt, scale=1.0 / SSD_W, bias=k.c("eps")).then_inc(s["rt"], 1)
                for g in range(POOL_G):
                    act.wait_ge(s["pmm"], g + 1)
                    if g >= 2:
                        act.wait_ge(s["omm"], g - 1)
                    act.activation(pl[:, g % 2, :], k.ps[5 + g % 2][:, :], ACT.Copy).then_inc(s["psb"], 1)

            @block.vector
            def _(dve):
                for m in range(XT):
                    dve.wait_ge(s["silu"], m + 1)
                    dve.tensor_tensor(t["mix"][:, m, :], t["mix"][:, m, :], zs[:, m % 2, :], ALU.mult).then_inc(s["y"], 1)
                for i in range(NT):
                    dve.wait_ge(s["umm"], i + 1)
                    dve.tensor_copy(ut[:, i, :], k.ps[3 + i % 2][:, :]).then_inc(s["usb"], 1)
                dve.wait_ge(s["rt"], 1)
                dve.reciprocal(r[:], r[:])
                dve.drain()
                for m in range(XT):
                    dve.scalar_tensor_tensor(t["mix"][:, m, :], t["mix"][:, m, :], k.v("g_ssd", m, m + 1), r[:], ALU.mult, ALU.mult)
                for g in range(POOL_G):
                    dve.wait_ge(s["omm"], g + 1)
                    dve.tensor_scalar(t["mix"][:, XT + g, :], k.ps[g % 2][:, :], k.v("pscale", g, g + 1), None, ALU.mult).then_inc(s["osb"], 1)
    k.end()


def two_blocks(nc, a, stop=None):
    ctx = ExitStack()
    with ctx:
        k = Core(nc, ctx, a)
        win, win2 = a["w_in"], a["w_in_2"]
        ada = [a["w_ada"][i] for i in range(MOD_P)]
        cols = lambda w, c0, c1, r0=0: w[r0 * P:(r0 + KT) * P, c0:c1].rearrange("(k p) n -> p k n", p=P)
        in1 = [cols(win, 512 * i, 512 * (i + 1)) for i in range(4)] + [cols(win, 2064, 2576)] + [a["w_tail"]]
        in1 = [x for i, w in enumerate(in1) for x in (w, a["w_mod"][MOD_ORDER[2 * i]], a["w_mod"][MOD_ORDER[2 * i + 1]])]
        out1 = [cols(a["w_out"], 512 * i, 512 * (i + 1)) for i in range(2)]
        z0 = CONV_T * P + DT_C
        in2 = [cols(win2, 512 * i, 512 * (i + 1)) for i in range(5)] + [cols(win2, CONV_T * P, z0)] + \
              [cols(win2, z0 + 512 * i, z0 + 512 * (i + 1)) for i in range(4)]
        out2 = [cols(a["w_out_2"], 512 * n, 512 * (n + 1), KT * h) for n in range(2) for h in range(2)]
        k.pieces = ada + in1 + out1 + in2 + out2
        p_in1, p_out1 = MOD_P, 30
        p_in2, p_z, p_out2 = 32, 38, 42
        table = k.sb("table", [P, 68], I32)
        slots = k.sb("slots", [P, TOP2, NT], I32)
        wts = k.sb("wts", [P, TOP2, NT])
        t = {"table": table, "slots": slots, "wts": wts}
        modulation_phase(k)
        if stop == "mod":
            return k
        g = lambda n: (lambda kk: k.gain[:, n, kk:kk + 1])
        norm_phase(k, "n1", k.xT, k.hT, T, g(0), lambda kk: k.mod1[:, kk:kk + 1])
        with ExitStack() as mem:
            def sb(n, s, d=F32):
                t[n] = mem.enter_context(nc.sbuf_tensor(f"t_{n}", s, d))
            sb("qkv", [P, 12, T])
            sb("z", [P, NT, T])
            sb("swq", [P, 4, T])
            sb("swk", [P, SKV, WIN + T])
            sb("swv", [P, NT + 1, P])
            sb("ab", [P, NT, 16])
            for n in ("g", "beta"):
                sb(n, [P, NT, GH])
            sb("aexp", [P, GH])
            sb("dec", [P, 3, NT, GH])
            project1_phase(k, t, p_in1)
            if stop == "proj1":
                return k
            head_norm_phase(k, t)
            if stop == "head":
                return k
            t["att"] = k.hT[:].rearrange("p k (a b) -> p (k a) b", b=P)
            sb("mix", [P, KT, T])
            attention_phase(k, t)
            if stop == "attn":
                return k
            with ExitStack() as mem2:
                t["kvt"] = k.ring[:, 0, :].rearrange("p (a c n) -> p a c n", a=2, c=NT)
                t["S"] = k.ring[:, 1, :].rearrange("p (g n) -> p g n", n=P)
                gdn_prepare_phase(k, t)
                if stop == "gprep":
                    return k
                gdn_scan_phase(k, t)
            if stop == "gdn":
                return k
            output_phase(k, "o1", t["mix"], p_out1, 1, lambda m: k.mod1[:, 16 + m:17 + m], p_in2)
        if stop == "out1":
            return k
        norm_phase(k, "n2", k.xT, k.hT, T, g(1), lambda kk: k.mod1[:, 24 + kk:25 + kk])
        router_phase(k, "rt1", t, a["w_rt"], 4 + E, TOP1, k.r("b_rt"), True)
        if stop == "router1":
            return k
        expert_phase(k, "ex1", t, a["up1"], a["down1"], None, FF1, 2, 0)
        combine_phase(k, "cb1", t, TOP1, lambda kk: k.mod1[:, 40 + kk:41 + kk], p_in2 + 1)
        if stop == "block1":
            return k
        norm_phase(k, "n3", k.xT, k.hT, T, g(2), lambda kk: k.mod2[:, kk, 0:1], spill=a["spill_x"], pieces=p_in2 + 2)
        with ExitStack() as mem:
            def sb(n, s, d=F32):
                t[n] = mem.enter_context(nc.sbuf_tensor(f"u_{n}", s, d))
            sb("mix", [P, MIXT, T])
            with ExitStack() as mem1:
                for n, shape in (("bc", [P, 8, T]), ("dt", [P, NT + NC_, DT_C]), ("a", [P, NT + NC_, DT_C]),
                                 ("coef", [P, NT + NC_, 2, SSD_H]), ("etot", [P, NT + NC_, 2, SSD_H])):
                    t[n] = mem1.enter_context(nc.sbuf_tensor(f"u_{n}", shape, F32))
                xt_b = mem1.enter_context(nc.sbuf_tensor("u_xb", [P, 8192], F32))
                t["xtok"] = xt_b[:, 0:NT * SSD_W].rearrange("p (i c) -> p i c", i=NT)
                t["btok"] = xt_b[:, NT * SSD_W:8192].rearrange("p (i c) -> p i c", i=NT)
                hc = xt_b[:, 0:KT * CTX].rearrange("p (k n) -> p k n", k=KT)
                xflat = k.xT[:].rearrange("p k n -> p (k n)")
                cx = xflat[:, 0:KT * CTX].rearrange("p (k n) -> p k n", k=KT)
                norm_phase(k, "n4", cx, hc, CTX, g(4), lambda kk: k.mod2[:, kk, 1:2], load=a["ctxT"], pieces=p_in2 + RING)
                t["xc"] = xflat.rearrange("p (m n) -> p m n", n=CTX)
                project2_phase(k, t, hc, p_in2)
                if stop == "proj2":
                    return k
                t["state"] = k.ring[:, 0, 0:2 * SSD_W].rearrange("p (d c) -> p d c", d=2)
                ssd_prepare_phase(k, t)
                if stop == "sprep":
                    return k
                ssd_scan_phase(k, t, p_z)
                if stop == "sscan":
                    return k
            gate2_phase(k, t, p_z)
            if stop == "gate2":
                return k
            output_phase(k, "o2", t["mix"], p_out2, 2, lambda m: k.mod2[:, 16 + m, 0:1], p_out2 + 4)
        if stop == "out2":
            return k
        norm_phase(k, "n5", k.xT, k.hT, T, g(3), lambda kk: k.mod2[:, 24 + kk, 0:1])
        router_phase(k, "rt2", t, a["w_rt2"], E, TOP2, k.r("b_rt2"), False)
        if stop == "router2":
            return k
        expert_phase(k, "ex2", t, a["up2"], a["down2"], a["bias2"], FF2, 1, 2)
        combine_phase(k, "cb2", t, TOP2, lambda kk: k.mod2[:, 40 + kk, 0:1], 0)
        norm_phase(k, "n6", k.xT, k.hT, T, lambda kk: k.v("g_fin", kk, kk + 1), None, store=a["out"])
    return k


def head_constants():
    tiles = 8 + 4 + SKV
    pick = np.zeros((P, 4 * tiles), np.float32)
    pick[np.arange(P), 2 * tiles + np.arange(P) // HD] = 1.0
    spread = np.zeros((2 * tiles, tiles * P + 1), np.float32)
    for m in range(tiles):
        for h in range(2):
            spread[2 * m + h, m * P + h * HD:m * P + (h + 1) * HD] = 1.0
    spread[:, tiles * P] = np.where(np.arange(2 * tiles) < 16, 1.0, 1.0 / HD)
    return pick, spread


def lay_out(x):
    f = np.ascontiguousarray
    col = lambda v: f(np.asarray(v).reshape(-1, P).T)
    i = x
    halves = lambda v: np.concatenate([np.asarray(v).reshape(-1, 1)] * 2, 0)
    conv = np.asarray(i["conv_w"])[0].reshape(4, 12, P).transpose(2, 1, 0).reshape(P, -1)
    conv2 = np.asarray(i["conv_w_2"])[0].reshape(5, CONV_T, P).transpose(2, 1, 0).reshape(P, -1)
    skip = np.repeat(np.asarray(i["d_skip_2"])[0], HD)
    vec = dict(c=col(i["c"]), c2=col(i["c_2"]), cc2=col(i["c_ctx_2"]), b_ada=col(i["b_ada"]), b_mod=col(i["b_mod_2"]),
               g_mix=col(i["norm_mix"]), g_ffn=col(i["norm_ffn"]), g1_2=col(i["norm1_w_2"]), g2_2=col(i["norm2_w_2"]),
               g_fin=col(i["final_norm_w_2"]), conv=conv, conv2=conv2, convb2=col(i["conv_b_2"]), qn=halves(i["q_norm"]),
               kn=halves(i["k_norm"]), skip=col(skip), pscale=col(i["pool_scale_2"]), g_ssd=col(i["ssd_norm_w_2"]))
    row = dict(a_log=i["a_log"], dt_bias=i["dt_bias"], g_out=i["gdn_out_norm"], sinks=i["sinks"],
               b_rt=np.concatenate([np.asarray(i["b_group"]).ravel(), np.asarray(i["b_router"]).ravel()]),
               a_log2=i["a_log_2"], dt_bias2=i["dt_bias_2"], b_rt2=i["router_b_2"])
    ktile = lambda w: f(np.asarray(w).reshape(KT, P, -1).transpose(1, 0, 2))
    pieces = lambda w: f(np.asarray(w)[0].reshape(KT, P, 12, 512).transpose(2, 1, 0, 3))
    w_in = np.asarray(i["w_in"])[0]
    tail = np.concatenate([w_in[:, c:c + HD] for c in (2576, 2576, 2576 + HD, 2576 + HD)] + [w_in[:, 2576 + P:2832], w_in[:, 2048:2064]], 1)
    gate, up = np.asarray(i["w_gate"])[0], np.asarray(i["w_up"])[0]
    up1 = np.concatenate([gate, up], 2).reshape(E, KT, P, 512).transpose(0, 2, 1, 3)
    down1 = np.asarray(i["w_down"])[0].reshape(E, 2, P, D).transpose(0, 2, 1, 3)
    w1 = np.asarray(i["w1_2"])[0].reshape(E, KT, P, 4, 256, 2).transpose(0, 3, 2, 1, 5, 4)
    w2 = np.asarray(i["w2_2"])[0].reshape(E, KT, P, 2, 512).transpose(0, 3, 2, 1, 4)
    b1 = np.asarray(i["b1_2"])[0].reshape(E, 4, 256, 2).transpose(0, 1, 3, 2).reshape(E, -1)
    return {
        "xT": f(np.asarray(i["x"])[0].T.reshape(KT, P, T).transpose(1, 0, 2)),
        "ctxT": f(np.asarray(i["ctx_2"])[0].T.reshape(KT, P, CTX).transpose(1, 0, 2)),
        "head_pick": head_constants()[0], "head_spread": head_constants()[1],
        "pos": f(np.asarray(i["positions"]).reshape(1, T)),
        "cst": shape_constants(),
        "vec": f(np.concatenate([vec[n] for n in VEC], 1)),
        "row": f(np.concatenate([np.asarray(row[n]).ravel() for n in ROW]).reshape(1, -1)),
        "w_ada": pieces(i["w_ada"]), "w_mod": pieces(i["w_mod_2"]),
        "w_in": f(w_in), "w_tail": ktile(tail), "w_out": f(np.asarray(i["w_out"])[0]),
        "w_rt": ktile(np.concatenate([np.asarray(i["w_group"])[0], np.asarray(i["w_router"])[0]], 1)),
        "up1": f(up1).reshape(E, P, -1), "down1": f(down1).reshape(E, P, -1),
        "w_in_2": f(np.asarray(i["w_in_2"])[0]), "w_out_2": f(np.asarray(i["w_out_2"])[0]),
        "pool_w": f(np.asarray(i["pool_w_2"])[0].transpose(1, 0, 2)),
        "w_rt2": ktile(np.asarray(i["router_w_2"])[0]),
        "up2": f(w1).reshape(4 * E, P, -1), "down2": f(w2).reshape(2 * E, P, -1),
        "bias2": f(np.concatenate([b1, np.asarray(i["b2_2"])[0]], 1)),
    }


def declare(nc, arrays):
    a = {}
    for name, x in arrays.items():
        a[name] = nc.dram_tensor(f"in_{name}", x.shape, mybir.dt.from_np(x.dtype), kind="ExternalInput").ap()
    for name, shape in (("xs", ((MAXB + 2) * P, D)), ("spill_h", (P, KT, T)), ("spill_x", (P, KT, T))):
        a[name] = nc.dram_tensor(name, shape, F32).ap()
    a["out"] = nc.dram_tensor("out_T", (D, T), F32, kind="ExternalOutput").ap()
    return a


def kernel(**inputs):
    import concourse.bacc as bacc
    from concourse.bass_utils import run_bass_kernel_spmd

    arrays = lay_out(inputs)
    nc = bacc.Bacc("TRN2", target_bir_lowering=False, num_devices=1)
    two_blocks(nc, declare(nc, arrays))
    r = run_bass_kernel_spmd(nc, [{f"in_{n}": x for n, x in arrays.items()}], core_ids=[0])
    return np.ascontiguousarray(np.asarray(r.results[0]["out_T"]).T).reshape(1, T, D)
```
